# Optimizing a Trainium2 kernel written in Bass

```python
import math
import jax, jax.numpy as jnp
from jax import lax
import numpy as np

D_MODEL = 1024
BATCH = 1
SEQ = 128
DEPTH = 2
DEC_BATCH = 1
DEC_SEQ = 512
PAST_LEN = 128

GRID_W = 64
N_MIXERS = 2
N_A_LAYERS = (DEPTH + 1) // 2
N_B_LAYERS = DEPTH // 2
EXPAND = 2
D_INNER = EXPAND * D_MODEL
HYENA_ORDER = 2
FILTER_EMB = 33
FILTER_BANDS = (FILTER_EMB - 1) // 2
FILTER_HIDDEN = 64
DECAY_TARGET = 1e-2
FAST_DECAY_PCT = 0.3
SLOW_DECAY_PCT = 1.5
MIN_DECAY = math.log(DECAY_TARGET) / SLOW_DECAY_PCT
MAX_DECAY = math.log(DECAY_TARGET) / FAST_DECAY_PCT
HEAD_SIZE = 64
N_HEADS = D_INNER // HEAD_SIZE
DECAY_LORA = 64
ICLR_LORA = 64
N_SHIFT_MIX = 6
NORM_EPS = 1e-6
GN_EPS = 64e-5

kernel_name = "hyena_rwkv7_prefix_diffusion_step"

def _rms_norm(x, g):
    xf = x.astype(jnp.float32)
    y = xf * lax.rsqrt(jnp.mean(xf * xf, axis=-1, keepdims=True) + NORM_EPS)
    return (y * g.astype(jnp.float32)).astype(x.dtype)

def _adaln(cond, w, b):
    m = jax.nn.silu(cond) @ w + b
    shift, scale, gate = jnp.split(m, 3, axis=-1)
    return shift[:, None, :], scale[:, None, :], gate[:, None, :]

def _short_conv(u, w, b):
    up = jnp.pad(u, ((0, 0), (1, 1), (0, 0)))
    return up[:, :-2] * w[0] + up[:, 1:-1] * w[1] + up[:, 2:] * w[2] + b

def _hyena_filter_spectrum(L, w1, b1, w2, b2, w3, b3, freq, w4):
    f32 = jnp.float32
    t = jnp.linspace(0.0, 1.0, L, dtype=f32)[:, None]
    pos = jnp.arange(L, dtype=f32)[:, None]
    bands = jnp.linspace(1e-4, FILTER_BANDS - 1, FILTER_BANDS, dtype=f32)[None, :]
    ang = (2.0 * math.pi / L) * pos * bands
    feats = jnp.concatenate([t, jnp.cos(ang), -jnp.sin(ang)], axis=-1)
    fr = freq.astype(f32)
    hid = jnp.sin(fr * (feats @ w1.astype(f32) + b1.astype(f32)))
    hid = jnp.sin(fr * (hid @ w2.astype(f32) + b2.astype(f32)))
    hid = jnp.sin(fr * (hid @ w3.astype(f32) + b3.astype(f32)))
    h = (hid @ w4.astype(f32)).reshape(L, 2, HYENA_ORDER, D_INNER)
    deltas = jnp.abs(jnp.linspace(MIN_DECAY, MAX_DECAY, D_INNER, dtype=f32))
    h = h * jnp.exp(-t[:, :, None, None] * deltas)
    h_f, h_b = h[:, 0], h[:, 1]
    taps = jnp.concatenate([h_f, jnp.zeros_like(h_f[:1]), h_b[:0:-1]], axis=0)
    return jnp.fft.rfft(taps, axis=0)

def _long_conv(u, spec, bias):
    L = u.shape[1]
    n = 2 * L
    U = jnp.fft.rfft(u, n=n, axis=1)
    y = jnp.fft.irfft(U * spec[None], n=n, axis=1)[:, :L]
    return y + u * bias

def _hyena_mixer(h, P, j):
    f32 = jnp.float32
    L = h.shape[1]
    E = D_INNER
    proj = h @ P["hy_w_in"][j] + P["hy_b_in"][j]
    vx, zg = proj[..., : 3 * E], proj[..., 3 * E:]
    vx = _short_conv(vx, P["hy_conv_w"][j], P["hy_conv_b"][j])
    v, x1, x2 = jnp.split(vx, 3, axis=-1)
    spec = _hyena_filter_spectrum(L, P["hy_f_w1"][j], P["hy_f_b1"][j], P["hy_f_w2"][j], P["hy_f_b2"][j],
                                  P["hy_f_w3"][j], P["hy_f_b3"][j], P["hy_f_freq"][j], P["hy_f_w4"][j])
    fft_bias = P["hy_fft_bias"][j].astype(f32)
    y = v.astype(f32)
    for o, gate in enumerate((x1, x2)):
        y = gate.astype(f32) * _long_conv(y, spec[:, o], fft_bias[o])
    y = y.astype(h.dtype) * jax.nn.silu(zg)
    return y @ P["hy_w_out"][j] + P["hy_b_out"][j]

def _shift_context(x):
    half = x.shape[-1] // 2
    prev = jnp.pad(x[:, :-1, :half], ((0, 0), (1, 0), (0, 0)))
    nxt = jnp.pad(x[:, 1:, half:], ((0, 0), (0, 1), (0, 0)))
    return jnp.concatenate([prev, nxt], axis=-1)

def _shift_grid(x):
    B, L, D = x.shape
    rows = L // GRID_W
    q = D // 4
    g = x.reshape(B, rows, GRID_W, D)
    left = jnp.pad(g[:, :, :-1, :q], ((0, 0), (0, 0), (1, 0), (0, 0)))
    right = jnp.pad(g[:, :, 1:, q:2 * q], ((0, 0), (0, 0), (0, 1), (0, 0)))
    up = jnp.pad(g[:, :-1, :, 2 * q:3 * q], ((0, 0), (1, 0), (0, 0), (0, 0)))
    down = jnp.pad(g[:, 1:, :, 3 * q:], ((0, 0), (0, 1), (0, 0), (0, 0)))
    return jnp.concatenate([left, right, up, down], axis=-1).reshape(B, L, D)

def _wkv7_scan(r, w, k, v, a, b, s0, reverse):
    def step(S, inp):
        r_t, w_t, k_t, v_t, a_t, b_t = inp
        sa = jnp.einsum("bhvk,bhk->bhv", S, a_t)
        S = S * w_t[:, :, None, :] + sa[..., :, None] * b_t[..., None, :] + v_t[..., :, None] * k_t[..., None, :]
        return S, jnp.einsum("bhvk,bhk->bhv", S, r_t)
    xs = tuple(jnp.moveaxis(t, 1, 0) for t in (r, w, k, v, a, b))
    s_fin, ys = lax.scan(step, s0.astype(jnp.float32), xs, reverse=reverse)
    return jnp.moveaxis(ys, 0, 1), s_fin

def _rwkv_mixer(h, h_shift, s0_f, s0_b, P, j):
    f32 = jnp.float32
    B, L, _ = h.shape
    xx = h_shift - h
    mu = P["rw_mu"][j]
    xr, xw, xk, xv, xa, xg = (h + xx * mu[m] for m in range(N_SHIFT_MIX))
    r = (xr @ P["rw_w_r"][j]).astype(f32)
    k = (xk @ P["rw_w_k"][j]).astype(f32)
    v = (xv @ P["rw_w_v"][j]).astype(f32)
    zg = xg @ P["rw_w_z"][j]
    w_lo = jnp.tanh(jnp.einsum("bld,zdr->zblr", xw, P["rw_w1"][j]))
    w_raw = (P["rw_w0"][j][:, None, None, :] + jnp.einsum("zblr,zre->zble", w_lo, P["rw_w2"][j])).astype(f32)
    decay = jnp.exp(-jnp.exp(-jax.nn.softplus(-w_raw) - 0.5))
    a_lo = jnp.einsum("bld,zdr->zblr", xa, P["rw_a1"][j])
    iclr = jax.nn.sigmoid((P["rw_a0"][j][:, None, None, :]
                           + jnp.einsum("zblr,zre->zble", a_lo, P["rw_a2"][j])).astype(f32))
    k_k = P["rw_k_k"][j].astype(f32)
    k_a = P["rw_k_a"][j].astype(f32)
    heads = lambda t: t.reshape(t.shape[:-1] + (N_HEADS, HEAD_SIZE))
    kk = heads(k * k_k)
    kk = kk / jnp.maximum(jnp.sqrt(jnp.sum(kk * kk, axis=-1, keepdims=True)), 1e-12)
    k_dir = heads(k[None] * (1.0 + (iclr - 1.0) * k_a))
    r_h, v_h = heads(r), heads(v)
    decay_h, iclr_h = heads(decay), heads(iclr)
    o_f, s_f = _wkv7_scan(r_h, decay_h[0], k_dir[0], v_h, -kk, kk * iclr_h[0], s0_f, False)
    o_b, s_b = _wkv7_scan(r_h, decay_h[1], k_dir[1], v_h, -kk, kk * iclr_h[1], s0_b, True)
    o = o_f + o_b
    mean = jnp.mean(o, axis=-1, keepdims=True)
    var = jnp.mean(jnp.square(o - mean), axis=-1, keepdims=True)
    o = (o - mean) * lax.rsqrt(var + GN_EPS)
    bonus = jnp.einsum("blhn,zblhn,zhn->blh", r_h, k_dir, P["rw_r_k"][j].astype(f32))[..., None] * v_h
    o = (o.reshape(B, L, D_INNER) * P["rw_gn_w"][j].astype(f32) + P["rw_gn_b"][j].astype(f32)
         + bonus.reshape(B, L, D_INNER))
    out = (o.astype(h.dtype) * jax.nn.silu(zg)) @ P["rw_w_o"][j]
    return out, s_f, s_b

def _trunk(x, cond, shift_fn, init_fwd, init_bwd, P):
    B = x.shape[0]
    fin_f, fin_b = [], []
    for i in range(DEPTH):
        shift, scale, gate = _adaln(cond, P["ada_w"][i], P["ada_b"][i])
        h = _rms_norm(x, P["norm_pre"][i]) * (1.0 + scale) + shift
        j = i // N_MIXERS
        if i % N_MIXERS == 0:
            out = _hyena_mixer(h, P, j)
        else:
            if init_fwd is None:
                s0_f = jnp.zeros((B, N_HEADS, HEAD_SIZE, HEAD_SIZE), jnp.float32)
                s0_b = jnp.zeros((B, N_HEADS, HEAD_SIZE, HEAD_SIZE), jnp.float32)
            else:
                s0_f, s0_b = init_fwd[:, j], init_bwd[:, j]
            out, s_f, s_b = _rwkv_mixer(h, shift_fn(h), s0_f, s0_b, P, j)
            fin_f.append(s_f)
            fin_b.append(s_b)
        x = x + gate * _rms_norm(out, P["norm_post"][i])
    return x, fin_f, fin_b

def setup_inputs(seed: int = 0) -> dict:
    key = jax.random.key(seed)
    ks = iter(jax.random.split(key, 64))
    f32 = jnp.float32
    nrm = lambda shape, s: jax.random.normal(next(ks), shape, f32) * s
    uni = lambda shape, lo, hi: jax.random.uniform(next(ks), shape, f32, lo, hi)
    D, E, H, N = D_MODEL, D_INNER, N_HEADS, HEAD_SIZE
    NA, NB, FH = N_A_LAYERS, N_B_LAYERS, FILTER_HIDDEN
    inp = {}
    inp["x_prompt"] = nrm((BATCH, SEQ, D), 1.0)
    inp["x_sample"] = nrm((DEC_BATCH, DEC_SEQ, D), 1.0)
    inp["state_rwkv_fwd"] = nrm((DEC_BATCH, NB, H, N, N), 0.3)
    inp["state_rwkv_bwd"] = nrm((DEC_BATCH, NB, H, N, N), 0.3)
    inp["c"] = nrm((DEC_BATCH, D), 1.0)
    inp["c_ctx"] = nrm((D,), 1.0)
    inp["ada_w"] = nrm((DEPTH, D, 3 * D), D ** -0.5)
    inp["ada_b"] = nrm((DEPTH, 3 * D), 0.02)
    inp["norm_pre"] = 1.0 + nrm((DEPTH, D), 0.05)
    inp["norm_post"] = 1.0 + nrm((DEPTH, D), 0.05)
    inp["hy_w_in"] = nrm((NA, D, 4 * E), D ** -0.5)
    inp["hy_b_in"] = nrm((NA, 4 * E), 0.02)
    inp["hy_conv_w"] = nrm((NA, 3, 3 * E), 3 ** -0.5)
    inp["hy_conv_b"] = nrm((NA, 3 * E), 0.02)
    inp["hy_f_w1"] = nrm((NA, FILTER_EMB, FH), FILTER_EMB ** -0.5)
    inp["hy_f_b1"] = nrm((NA, FH), 0.1)
    inp["hy_f_w2"] = nrm((NA, FH, FH), FH ** -0.5)
    inp["hy_f_b2"] = nrm((NA, FH), 0.1)
    inp["hy_f_w3"] = nrm((NA, FH, FH), FH ** -0.5)
    inp["hy_f_b3"] = nrm((NA, FH), 0.1)
    inp["hy_f_freq"] = 1.0 + nrm((NA, FH), 0.1)
    inp["hy_f_w4"] = nrm((NA, FH, 2 * HYENA_ORDER * E), FH ** -0.5)
    inp["hy_fft_bias"] = nrm((NA, HYENA_ORDER, E), 0.5)
    inp["hy_w_out"] = nrm((NA, E, D), E ** -0.5)
    inp["hy_b_out"] = nrm((NA, D), 0.02)
    inp["rw_mu"] = uni((NB, N_SHIFT_MIX, D), 0.0, 1.0)
    inp["rw_w_r"] = nrm((NB, D, E), D ** -0.5)
    inp["rw_w_k"] = nrm((NB, D, E), D ** -0.5)
    inp["rw_w_v"] = nrm((NB, D, E), D ** -0.5)
    inp["rw_w_z"] = nrm((NB, D, E), D ** -0.5)
    inp["rw_w0"] = uni((NB, 2, E), -4.0, 0.0)
    inp["rw_w1"] = nrm((NB, 2, D, DECAY_LORA), D ** -0.5)
    inp["rw_w2"] = nrm((NB, 2, DECAY_LORA, E), 0.1 * DECAY_LORA ** -0.5)
    inp["rw_a0"] = nrm((NB, 2, E), 0.5)
    inp["rw_a1"] = nrm((NB, 2, D, ICLR_LORA), D ** -0.5)
    inp["rw_a2"] = nrm((NB, 2, ICLR_LORA, E), 0.5 * ICLR_LORA ** -0.5)
    inp["rw_k_k"] = 0.85 + nrm((NB, E), 0.05)
    inp["rw_k_a"] = 1.0 + nrm((NB, E), 0.05)
    inp["rw_r_k"] = nrm((NB, 2, H, N), 0.1)
    inp["rw_gn_w"] = 1.0 + nrm((NB, E), 0.05)
    inp["rw_gn_b"] = nrm((NB, E), 0.02)
    inp["rw_w_o"] = nrm((NB, E, D), E ** -0.5)
    return inp

def reference(x_prompt, x_sample, state_rwkv_fwd, state_rwkv_bwd, c, c_ctx, ada_w, ada_b, norm_pre, norm_post,
              hy_w_in, hy_b_in, hy_conv_w, hy_conv_b, hy_f_w1, hy_f_b1, hy_f_w2, hy_f_b2, hy_f_w3, hy_f_b3,
              hy_f_freq, hy_f_w4, hy_fft_bias, hy_w_out, hy_b_out, rw_mu, rw_w_r, rw_w_k, rw_w_v, rw_w_z,
              rw_w0, rw_w1, rw_w2, rw_a0, rw_a1, rw_a2, rw_k_k, rw_k_a, rw_r_k, rw_gn_w, rw_gn_b, rw_w_o):
    P = dict(ada_w=ada_w, ada_b=ada_b, norm_pre=norm_pre, norm_post=norm_post,
             hy_w_in=hy_w_in, hy_b_in=hy_b_in, hy_conv_w=hy_conv_w, hy_conv_b=hy_conv_b,
             hy_f_w1=hy_f_w1, hy_f_b1=hy_f_b1, hy_f_w2=hy_f_w2, hy_f_b2=hy_f_b2, hy_f_w3=hy_f_w3, hy_f_b3=hy_f_b3,
             hy_f_freq=hy_f_freq, hy_f_w4=hy_f_w4, hy_fft_bias=hy_fft_bias, hy_w_out=hy_w_out, hy_b_out=hy_b_out,
             rw_mu=rw_mu, rw_w_r=rw_w_r, rw_w_k=rw_w_k, rw_w_v=rw_w_v, rw_w_z=rw_w_z,
             rw_w0=rw_w0, rw_w1=rw_w1, rw_w2=rw_w2, rw_a0=rw_a0, rw_a1=rw_a1, rw_a2=rw_a2,
             rw_k_k=rw_k_k, rw_k_a=rw_k_a, rw_r_k=rw_r_k, rw_gn_w=rw_gn_w, rw_gn_b=rw_gn_b, rw_w_o=rw_w_o)
    y_prompt, fin_f, fin_b = _trunk(x_prompt, c_ctx[None, :], _shift_context, None, None, P)
    new_state_fwd = jnp.stack(fin_f, axis=1)
    new_state_bwd = jnp.stack(fin_b, axis=1)
    y_sample, _, _ = _trunk(x_sample, c, _shift_grid, state_rwkv_fwd, state_rwkv_bwd, P)
    return (y_prompt, y_sample, new_state_fwd, new_state_bwd)


_drawn_inputs = setup_inputs


def setup_inputs(seed=0):
    import zlib

    import numpy as np

    out = dict(_drawn_inputs(seed))
    spreads = {}
    factors = {'state_rwkv_fwd': 7.039,
     'state_rwkv_bwd': 7.774,
     'hy_b_out': 24.547,
     'rw_w1': 2.896,
     'rw_w2': 3.219,
     'rw_gn_w': 3.01,
     'rw_gn_b': 7.614}
    for name, (base, spread) in spreads.items():
        noise = np.random.default_rng([zlib.crc32(name.encode()), seed]).standard_normal(out[name].shape)
        drawn = base * np.exp(spread * noise) if base else spread * noise
        out[name] = __import__('jax').numpy.asarray(drawn.astype(out[name].dtype))
    for name, factor in factors.items():
        out[name] = (out[name] * factor).astype(out[name].dtype)
    return out
```

```python
import concourse.bass as bass
from concourse import mybir
from contextlib import ExitStack
import numpy as np

F32 = mybir.dt.float32
ALU = mybir.AluOpType
ACT = mybir.ActivationFunctionType
MUL, ADD, SUB = ALU.mult, ALU.add, ALU.subtract

P = 128
D = 1024
E = 2048
LS, LP = 512, 128
T = LS + LP
NT = T // P
KD = D // P
KE = E // P
GRID = 64
ROWS = LS // GRID
HID = 64
EMB = 33
C = 64
NC = T // C
CS = LS // C
LEVELS = 6
CB = 512
NB = E // CB
EPS = 1e-6
GN_EPS = 64e-5
DECAY_MAX = float(np.exp(-0.5))

TAB = {}
_at = 0
for _name, _n in (("ident", P), ("heads", P), ("mask_f", 2 * P), ("mask_b", 2 * P), ("amask_f", P), ("amask_b", P),
                  ("level", LEVELS * P), ("chunk", T), ("feats", T), ("selc", 2 * P)):
    TAB[_name] = (_at, _at + _n)
    _at += _n
TAB_N = _at
DFT = {}
_at = 0
for _name, _n in (("fwd", 4 * 2 * 256), ("inv", 4 * 2 * 256), ("fwdp", 2 * P), ("invp", 2 * P)):
    DFT[_name] = (_at, _at + _n)
    _at += _n
DFT_N = _at


class Steps:

    def __init__(self, nc, stack, name, marks, by=1):
        self.sem = stack.enter_context(nc.semaphore(name))
        self.name, self.marks, self.n, self.by = name, marks, 0, by

    def note(self, label):
        if not self.marks.get("counted"):
            self.marks[self.name, label] = self.n

    def per(self):
        return self.marks.get((self.name, None), 0)

    def did(self, ins, label=None):
        ins.then_inc(self.sem, self.by)
        self.n += self.by
        if not self.marks.get("counted"):
            self.marks[self.name, label] = self.marks[self.name, None] = self.n
        return ins

    def mark(self, label):
        return self.marks.get((self.name, label), 0)

    def now(self, label, i=None):
        return self.mark(label) if i is None else i * self.per() + (self.per() + self.mark(label))

    def before(self, label, i):
        return i * self.per() + self.mark(label)

    def here(self, i=None):
        return self.n if i is None else i * self.per() + (self.per() + self.n)

    def start(self, eng):
        if self.per():
            eng.sem_inc(self.sem, self.per())


def make_ops(nc):
    def mm(out, lhsT, rhs, first=True, last=True):
        return nc.tensor.matmul(out, lhsT, rhs, start=first, stop=last)

    def stt(out, in0, scalar, in1, op0, op1):
        return nc.vector.scalar_tensor_tensor(out=out, in0=in0, scalar=scalar, in1=in1, op0=op0, op1=op1)

    def ts(out, in0, s1, s2, op0, op1=None):
        if op1 is None:
            return nc.vector.tensor_scalar(out, in0, s1, None, op0)
        return nc.vector.tensor_scalar(out, in0, s1, s2, op0, op1)

    def tt(out, a, b, op):
        return nc.vector.tensor_tensor(out, a, b, op)

    def act(out, in_, f, **kw):
        return nc.scalar.activation(out, in_, f, **kw)

    return mm, stt, ts, tt, act


def modulation(nc, A, G, M):
    mm, stt, ts, tt, act = make_ops(nc)
    ps, tab, col = G["ps"], G["tab"], G["col"]
    with ExitStack() as st:
        sb = lambda n, s: st.enter_context(nc.sbuf_tensor(n, s, F32))
        crow, csig, condT = sb("crow", [16, P]), sb("csig", [16, P]), sb("condT", [P, 16])
        rows = sb("vrows", [P, 4, P])
        frow = sb("frow", [4, HID])
        RING = 3
        aw = sb("aw", [P, RING, 3 * D])
        mrow = sb("mrow", [2, 2, 3 * D])
        abrow = sb("abrow", [2, 2, 3 * D])
        prow = sb("prow", [2, 2, D])
        s_small = st.enter_context(nc.semaphore("mod_vectors_loaded"))
        s_tab = st.enter_context(nc.semaphore("mod_tables_loaded"))
        s_aw = [st.enter_context(nc.semaphore(f"mod_weights_{k}")) for k in range(RING)]
        s_out = st.enter_context(nc.semaphore("mod_gate_stored"))
        pe_, ac_, dv_ = (Steps(nc, st, f"mod_{n}", M) for n in ("pe", "act", "dve"))
        nload = [0]

        with nc.Block() as block:
            @block.sync
            def _(sp):
                def small(dst, src):
                    sp.dma_start(dst, src).then_inc(s_small, 16)
                    nload[0] += 16
                nload[0] = 0
                sp.dma_start(tab[:, :], A["tab"]).then_inc(s_tab, 16)
                small(crow[0:8, :], A["c"].rearrange("a (k p) -> (a k) p", p=P))
                small(crow[8:16, :], A["c_ctx"].rearrange("(k p) -> k p", p=P))
                at = 0
                for a, n in ((A["norm_pre"].rearrange("l (k p) -> (l k) p", p=P), 16),
                             (A["hy_b_in"].rearrange("l (k p) -> (l k) p", p=P), 64),
                             (A["rw_mu"].rearrange("l m (k p) -> (l m k) p", p=P), 48),
                             (A["hy_conv_w"].rearrange("l j (k p) -> (l j k) p", p=P)[0:96, :], 96),
                             (None, 32),
                             (A["hy_conv_w"].rearrange("l j (k p) -> (l j k) p", p=P)[96:144, :], 48),
                             (A["hy_conv_b"].rearrange("l (k p) -> (l k) p", p=P), 48),
                             (A["rw_w0"].rearrange("l z (k p) -> (l z k) p", p=P), 32),
                             (A["rw_a0"].rearrange("l z (k p) -> (l z k) p", p=P), 32),
                             (A["rw_k_k"].rearrange("l (k p) -> (l k) p", p=P), 16),
                             (A["rw_k_a"].rearrange("l (k p) -> (l k) p", p=P), 16),
                             (A["rw_r_k"].rearrange("l z (k h) n -> (l z k) (h n)", h=2), 32),
                             (A["rw_gn_w"].rearrange("l (k p) -> (l k) p", p=P), 16),
                             (A["rw_gn_b"].rearrange("l (k p) -> (l k) p", p=P), 16)):
                    g, r = at // P, at % P
                    if a is not None:
                        small(rows[r:r + n, g, :], a)
                    else:
                        small(rows[r:r + n, g, :], A["hy_conv_b"].rearrange("l (k p) -> (l k) p", p=P)[0:n, :])
                    at += n
                for k, n in enumerate(("hy_f_b1", "hy_f_b2", "hy_f_b3", "hy_f_freq")):
                    small(frow[k:k + 1, :], A[n])
                for l in range(2):
                    for c in range(2):
                        small(abrow[c:c + 1, l, :], A["ada_b"][l:l + 1, :])
                        small(prow[c:c + 1, l, :], A["norm_post"][l:l + 1, :])
                for n in range(2 * KD):
                    l, k = n // KD, n % KD
                    if n >= RING:
                        sp.wait_ge(pe_.sem, pe_.now(("ada", n - RING)))
                    sp.dma_start(aw[:, n % RING, :], A["ada_w"][l, k * P:(k + 1) * P, :]).then_inc(s_aw[n % RING], 16)
                for l in range(2):
                    sp.wait_ge(dv_.sem, dv_.now(("gate", l)))
                    sp.dma_start(A["gate_d"][l], mrow[:, l, 2 * D:3 * D]).then_inc(s_out, 16)
                sp.wait_ge(s_out, 32)

            @block.scalar
            def _(a):
                a.wait_ge(s_small, nload[0])
                ac_.did(act(csig[:, :], crow[:, :], ACT.Sigmoid), "csig")

            @block.tensor
            def _(pe):
                pe.wait_ge(s_tab, 16)
                pe.wait_ge(s_small, nload[0])
                ident = tab[:, TAB["ident"][0]:TAB["ident"][1]]
                for g in range(4):
                    last = nc.tensor.transpose(ps[:, 6, g * P:(g + 1) * P], rows[:, g, :], ident)
                pe_.did(last, "cols")
                last = nc.tensor.transpose(ps[0:HID, 7, 0:4], frow[:, :], ident[0:4, 0:4])
                pe_.did(last, "fcols")
                pe.wait_ge(dv_.sem, dv_.now("fcols"))
                pe_.did(nc.tensor.transpose(ps[:, 7, 16:32], crow[:, :], ident[0:16, 0:16]), "condT")
                pe.wait_ge(dv_.sem, dv_.now("condT"))
                for l in range(2):
                    if l:
                        pe.wait_ge(dv_.sem, dv_.now(("row", l - 1)))
                    for k in range(KD):
                        n = l * KD + k
                        pe.wait_ge(s_aw[n % RING], 16 * (n // RING + 1))
                        for b in range(6):
                            last = mm(ps[0:2, b, :], condT[:, k:16:KD], aw[:, n % RING, b * 512:(b + 1) * 512], k == 0, k == KD - 1)
                        pe_.did(last, ("ada", n))
                    pe.wait_ge(dv_.sem, dv_.now(("row", l)))
                    if l:
                        pe.wait_ge(dv_.sem, dv_.now(("mcols", l - 1)))
                    for j in range(16):
                        last = nc.tensor.transpose(ps[:, 7, 64 + 2 * j:66 + 2 * j], mrow[:, l, j * P:(j + 1) * P], ident[0:2, 0:2])
                    pe_.did(last, ("mcols", l))

            @block.vector
            def _(v):
                def link(ins, label=None):
                    dv_.did(ins, label)
                    v.wait_ge(dv_.sem, dv_.here())
                v.wait_ge(ac_.sem, ac_.now("csig"))
                dv_.did(tt(crow[:, :], crow[:, :], csig[:, :], MUL), "silu")
                v.wait_ge(pe_.sem, pe_.now("cols"))
                dv_.did(nc.vector.tensor_copy(col[:, :, :], ps[:, 6, :].rearrange("p (g n) -> p g n", g=4)), "cols")
                v.wait_ge(pe_.sem, pe_.now("fcols"))
                dv_.did(nc.vector.tensor_copy(G["fcol"][:, :], ps[0:HID, 7, 0:4]), "fcols")
                v.wait_ge(pe_.sem, pe_.now("condT"))
                link(nc.vector.tensor_copy(condT[:, :], ps[:, 7, 16:32]), "condT")
                npre = col[:, 0, 0:16].rearrange("p (l k) -> p l k", l=2)
                for l in range(2):
                    v.wait_ge(pe_.sem, pe_.now(("ada", l * KD + KD - 1)))
                    link(tt(mrow[:, l, :], ps[0:2, 0:6, :].rearrange("p b n -> p (b n)"), abrow[:, l, :], ADD), ("row", l))
                    dv_.did(tt(mrow[:, l, 2 * D:3 * D], mrow[:, l, 2 * D:3 * D], prow[:, l, :], MUL), ("gate", l))
                    v.wait_ge(pe_.sem, pe_.now(("mcols", l)))
                    mc = ps[:, 7, 64:96].rearrange("p (j c) -> p j c", c=2)
                    dv_.did(nc.vector.tensor_copy(G["shf"][:, l, :, :], mc[:, 0:8, :]))
                    for c in range(2):
                        last = dv_.did(stt(G["scl"][:, l, :, c], mc[:, 8:16, c], 1.0, npre[:, l, :], ADD, MUL), ("mcols", l))


def load_norm(nc, A, G, M, l, hT):
    mm, stt, ts, tt, act = make_ops(nc)
    ps, tab = G["ps"], G["tab"]
    with ExitStack() as st:
        sb = lambda n, s: st.enter_context(nc.sbuf_tensor(f"{n}{l}", s, F32))
        x, sq, ss, rs = sb("nx", [P, NT, D]), sb("nsq", [P, D]), sb("nss", [P, NT]), sb("nrs", [P, NT])
        sx = [st.enter_context(nc.semaphore(f"norm{l}_x{j}")) for j in range(NT)]
        pe_, ac_, dv_ = (Steps(nc, st, f"norm{l}_{n}", M) for n in ("pe", "act", "dve"))
        with nc.Block() as block:
            @block.sync
            def _(sp):
                for j in range(NT):
                    src = A["x1_d"][j * P:(j + 1) * P, :] if l else (A["x_sample"][0, j * P:(j + 1) * P, :] if j < 4 else A["x_prompt"][0, :, :])
                    sp.dma_start(x[:, j, :], src).then_inc(sx[j], 16)

            @block.scalar
            def _(a):
                for j in range(NT):
                    a.wait_ge(sx[j], 16)
                    if j:
                        a.wait_ge(ac_.sem, ac_.here())
                    ac_.did(act(sq[:, :], x[:, j, :], ACT.Square, accum_out=ss[:, j:j + 1]), ("ss", j))
                a.wait_ge(dv_.sem, dv_.now("var"))
                ac_.did(act(rs[:, :], ss[:, :], ACT.Sqrt), "std")
                for k in range(KD):
                    a.wait_ge(pe_.sem, pe_.now(("tr", k)))
                    kw = lambda c: dict(scale=G["scl"][:, l, k, c:c + 1], bias=G["shf"][:, l, k, c:c + 1])
                    act(hT[:, k, 0:LS], ps[:, 2 * (k % 2), :], ACT.Identity, **kw(0))
                    ac_.did(act(hT[:, k, LS:T], ps[:, 2 * (k % 2) + 1, 0:LP], ACT.Identity, **kw(1)), ("h", k))

            @block.vector
            def _(v):
                def link(ins, label=None):
                    dv_.did(ins, label)
                    v.wait_ge(dv_.sem, dv_.here())
                v.wait_ge(ac_.sem, ac_.now(("ss", NT - 1)))
                dv_.did(ts(ss[:, :], ss[:, :], 1.0 / D, EPS, MUL, ADD), "var")
                v.wait_ge(ac_.sem, ac_.now("std"))
                link(nc.vector.reciprocal(rs[:, :], rs[:, :]))
                for j in range(NT):
                    dv_.did(ts(x[:, j, :], x[:, j, :], rs[:, j:j + 1], None, MUL), ("xn", j))

            @block.tensor
            def _(pe):
                ident = tab[:, TAB["ident"][0]:TAB["ident"][1]]
                pe.wait_ge(dv_.sem, dv_.now(("xn", NT - 1)))
                for k in range(KD):
                    if k >= 2:
                        pe.wait_ge(ac_.sem, ac_.now(("h", k - 2)))
                    for j in range(NT):
                        last = nc.tensor.transpose(ps[:, 2 * (k % 2) + j // 4, (j % 4) * P:(j % 4 + 1) * P], x[:, j, k * P:(k + 1) * P], ident)
                    pe_.did(last, ("tr", k))


def filter_hidden(nc, A, G, M):
    mm, stt, ts, tt, act = make_ops(nc)
    ps, tab, fcol, hid = G["ps"], G["tab"], G["fcol"], G["hid"]
    ROUND = 1.5 * 2 ** 23
    HI = 6.28125
    LO = 2 * np.pi - HI
    with ExitStack() as st:
        sb = lambda n, s: st.enter_context(nc.sbuf_tensor(n, s, F32))
        w = [sb("fw1", [EMB, HID]), sb("fw2", [HID, HID]), sb("fw3", [HID, HID])]
        arg, turn = sb("farg", [HID, T]), sb("fturn", [HID, T])
        s_w = st.enter_context(nc.semaphore("filter_weights_loaded"))
        pe_, ac_, dv_ = (Steps(nc, st, f"filter_{n}", M) for n in ("pe", "act", "dve"))
        psv = ps[0:HID, 0:2, :].rearrange("p b n -> p (b n)")
        with nc.Block() as block:
            @block.sync
            def _(sp):
                for k in range(3):
                    sp.dma_start(w[k][:, :], A[f"hy_f_w{k + 1}"][0]).then_inc(s_w, 16)

            @block.tensor
            def _(pe):
                pe.wait_ge(s_w, 48)
                for k in range(3):
                    src = tab[0:EMB, TAB["feats"][0]:TAB["feats"][1]] if k == 0 else hid[:, :]
                    if k:
                        pe.wait_ge(ac_.sem, ac_.now(("sin", k - 1)))
                    mm(psv[:, 0:LS], w[k][:, :], src[:, 0:LS])
                    pe_.did(mm(psv[:, LS:T], w[k][:, :], src[:, LS:T]), ("mm", k))

            @block.vector
            def _(v):
                def link(ins, label=None):
                    dv_.did(ins, label)
                    v.wait_ge(dv_.sem, dv_.here())
                for k in range(3):
                    v.wait_ge(pe_.sem, pe_.now(("mm", k)))
                    if k:
                        v.wait_ge(ac_.sem, ac_.now(("sin", k - 1)))
                    link(ts(arg[:, :], psv[:, 0:T], fcol[:, k:k + 1], fcol[:, 3:4], ADD, MUL))
                    link(ts(turn[:, :], arg[:, :], 1 / (2 * np.pi), ROUND, MUL, ADD))
                    link(ts(turn[:, :], turn[:, :], ROUND, None, SUB))
                    link(stt(arg[:, :], turn[:, :], -HI, arg[:, :], MUL, ADD))
                    link(stt(arg[:, :], turn[:, :], -LO, arg[:, :], MUL, ADD))
                    link(ts(arg[:, :], arg[:, :], 3.1415925, -3.1415925, ALU.min, ALU.max), ("arg", k))

            @block.scalar
            def _(a):
                for k in range(3):
                    a.wait_ge(dv_.sem, dv_.now(("arg", k)))
                    ac_.did(act(hid[:, :], arg[:, :], ACT.Sin), ("sin", k))


def hyena_in(nc, A, G, M, hT):
    mm, stt, ts, tt, act = make_ops(nc)
    ps, tab, col = G["ps"], G["tab"], G["col"]
    w_v = A["hy_w_in"][0].rearrange("(k p) n -> p k n", p=P)
    pair = [ps[:, 2 * q:2 * q + 2, :].rearrange("p b n -> p (b n)") for q in range(4)]
    with ExitStack() as st:
        sb = lambda n, s: st.enter_context(nc.sbuf_tensor(n, s, F32))
        w = [sb(f"hw{s}", [P, KD, P]) for s in range(4)]
        PADN = LS + LP + 3
        pad = [sb(f"hpad{s}", [P, PADN]) for s in range(3)]
        cv = [sb(f"hcv{s}", [P, T + 1]) for s in range(3)]
        out_t = [sb(f"hot{s}", [P, NT, P]) for s in range(2)]
        zsig, z, g = sb("hzs", [P, T]), sb("hz", [P, T]), sb("hg", [P, T])
        pc = sb("hpc", [P, 16])
        s_w = [st.enter_context(nc.semaphore(f"hy_weights_{s}")) for s in range(4)]
        s_o = [st.enter_context(nc.semaphore(f"hy_stored_{s}")) for s in range(3)]
        s_f = [st.enter_context(nc.semaphore(f"hy_store_buffer_free_{s}")) for s in range(3)]
        s_z = st.enter_context(nc.semaphore("hy_pad_cleared"))
        pe_, ac_, dv_ = (Steps(nc, st, f"hyin_{n}", M) for n in ("pe", "act", "dve"))
        with nc.Block() as block:
            @block.sync
            def _(sp):
                with sp.Fori(0, KE) as i:
                    for s in range(4):
                        sp.wait_ge(pe_.sem, pe_.before(("proj", s), i))
                        sp.dma_start(w[s][:, :, :], w_v[:, :, bass.ds(i * P + s * E, P)]).then_inc(s_w[s], 16)

            @block.gpsimd
            def _(po):
                for s in range(3):
                    nc.gpsimd.memset(pad[s][:, :], 0.0).then_inc(s_z, 1)
                    po.sem_inc(s_f[s], 1)
                with po.Fori(0, KE) as i:
                    for s in range(2):
                        po.wait_ge(ac_.sem, ac_.now(("vt", s), i))
                        po.dma_start(A["vx_d"][s].rearrange("(j p) n -> p j n", p=P)[:, :, bass.ds(i * P, P)], out_t[s][:, :, :]).then_inc(s_o[s], 16)
                    po.wait_ge(dv_.sem, dv_.now("g", i))
                    po.dma_start(A["g_d"][bass.ds(i * P, P), :], g[:, :]).then_inc(s_o[2], 16)
                    for s in range(3):
                        po.wait_ge(s_o[s], i * 16 + 16)
                        po.sem_inc(s_f[s], 1)
                for s in range(3):
                    po.wait_ge(s_o[s], 16 * KE)

            @block.tensor
            def _(pe):
                ident = tab[:, TAB["ident"][0]:TAB["ident"][1]]
                pe_.start(pe)

                def transpose(s, i):
                    pe.wait_ge(dv_.sem, dv_.now(("conv", s), i))
                    pe.wait_ge(ac_.sem, ac_.before(("vt", s), i))
                    for j in range(NT):
                        src = cv[s][:, j // 2 + 2 * P * (j % 2):min(j // 2 + 2 * P * (j % 2) + 2 * P, LS):2] if j < 4 else cv[s][:, LS + 1:T + 1]
                        last = nc.tensor.transpose(pair[2 + s][:, j * P:(j + 1) * P], src, ident)
                    pe_.did(last, ("tr", s))

                with pe.Fori(0, KE) as i:
                    for s in range(4):
                        pe.wait_ge(s_w[s], i * 16 + 16)
                        if s >= 2:
                            pe.wait_ge(ac_.sem, ac_.now(("pad", s - 2), i))
                        elif s == 0:
                            pe.wait_ge(ac_.sem, ac_.before(("pad", 2), i))
                        else:
                            pe.wait_ge(dv_.sem, dv_.before("z", i))
                        for k in range(KD):
                            mm(pair[s % 2][:, 0:LS], w[s][:, k, :], hT[:, k, 0:LS], k == 0, k == KD - 1)
                            last = mm(pair[s % 2][:, LS:T], w[s][:, k, :], hT[:, k, LS:T], k == 0, k == KD - 1)
                        pe_.did(last, ("proj", s))
                        if s in (1, 2):
                            transpose(s - 1, i)

            @block.scalar
            def _(a):
                ac_.start(a)
                a.wait_ge(s_z, 3)
                with a.Fori(0, KE) as i:
                    def to_pad(s):
                        a.wait_ge(pe_.sem, pe_.now(("proj", s), i))
                        a.wait_ge(dv_.sem, dv_.before(("conv", s), i))
                        act(pad[s][:, 1:LS + 1], pair[s % 2][:, 0:LS], ACT.Identity, bias=pc[:, s:s + 1])
                        ac_.did(act(pad[s][:, LS + 2:T + 2], pair[s % 2][:, LS:T], ACT.Identity, bias=pc[:, s:s + 1]), ("pad", s))

                    def turned(s):
                        a.wait_ge(pe_.sem, pe_.now(("tr", s), i))
                        a.wait_ge(s_f[s], i + 1)
                        ac_.did(act(out_t[s][:, :, :].rearrange("p j n -> p (j n)"), pair[2 + s][:, 0:T], ACT.Copy), ("vt", s))

                    a.wait_ge(dv_.sem, dv_.now("pc", i))
                    to_pad(0)
                    to_pad(1)
                    turned(0)
                    to_pad(2)
                    turned(1)
                    a.wait_ge(pe_.sem, pe_.now(("proj", 3), i))
                    a.wait_ge(dv_.sem, dv_.before("z", i))
                    ac_.did(act(zsig[:, :], pair[1][:, 0:T], ACT.Sigmoid, bias=pc[:, 3:4]), "zs")

            @block.vector
            def _(v):
                dv_.start(v)
                bin_c = col[:, 0, 16:80].rearrange("p (s k) -> p s k", s=4)
                cw01 = col[:, 1, 0:96].rearrange("p (j k) -> p j k", k=KE)
                cwb = col[:, 2, 0:96].rearrange("p (j k) -> p j k", k=KE)
                with v.Fori(0, KE) as i:
                    def link(ins, label=None):
                        dv_.did(ins, label)
                        v.wait_ge(dv_.sem, dv_.here(i))
                    v.wait_ge(ac_.sem, ac_.before("zs", i))
                    nc.vector.tensor_copy(pc[:, 0:4], bin_c[:, :, bass.ds(i, 1)].rearrange("p s o -> p (s o)"))
                    nc.vector.tensor_copy(pc[:, 4:10], cw01[:, :, bass.ds(i, 1)].rearrange("p s o -> p (s o)"))
                    link(nc.vector.tensor_copy(pc[:, 10:16], cwb[:, :, bass.ds(i, 1)].rearrange("p s o -> p (s o)")), "pc")
                    for s in range(3):
                        v.wait_ge(ac_.sem, ac_.now(("pad", s), i))
                        if s < 2:
                            v.wait_ge(pe_.sem, pe_.before(("tr", s), i))
                        link(ts(cv[s][:, :], pad[s][:, 1:T + 2], pc[:, 7 + s:8 + s], pc[:, 13 + s:14 + s], MUL, ADD))
                        link(stt(cv[s][:, :], pad[s][:, 0:T + 1], pc[:, 4 + s:5 + s], cv[s][:, :], MUL, ADD))
                        link(stt(cv[s][:, :], pad[s][:, 2:T + 3], pc[:, 10 + s:11 + s], cv[s][:, :], MUL, ADD), ("conv", s))
                    v.wait_ge(ac_.sem, ac_.now("zs", i))
                    link(stt(z[:, :], pair[1][:, 0:T], pc[:, 3:4], zsig[:, :], ADD, MUL), "z")
                    v.wait_ge(s_f[2], i + 1)
                    dv_.did(tt(g[:, 0:LS], z[:, 0:LS], cv[2][:, 0:LS], MUL))
                    dv_.did(tt(g[:, LS:T], z[:, LS:T], cv[2][:, LS + 1:T + 1], MUL), "g")


def hyena_conv(nc, A, G, M):
    mm, stt, ts, tt, act = make_ops(nc)
    ps, hid = G["ps"], G["hid"]
    pair = [ps[:, 2 * q:2 * q + 2, :] for q in range(4)]
    w4_v = A["hy_f_w4"][0].rearrange("k (g n) -> k g n", g=4)
    JOBS = [("filt", 0, j) for j in range(NT)] + [("fix", 0)] + [("H", 0, q) for q in range(5)] + [("X", 0, q) for q in range(5)] \
        + [("filt", 1, j) for j in range(NT)] + [("fix", 1)] + [("inv", 0, q) for q in range(3)] \
        + [("H", 1, q) for q in range(5)] + [("X", 1, q) for q in range(5)] + [("inv", 1, q) for q in range(4)]
    slot = {job: n % 4 for n, job in enumerate(JOBS)}
    with ExitStack() as st:
        sb = lambda n, s: st.enter_context(nc.sbuf_tensor(n, s, F32))
        dft = sb("dft", [P, DFT_N])
        vx = [sb("cv_v", [P, NT, CB]), sb("cv_x1", [P, NT, CB])]
        w4 = sb("w4", [HID, 4, CB])
        wsd = sb("wsd", [HID, 2, CB])
        dec = sb("dec", [P, NT, CB])
        bias = sb("fbias", [1, 2, CB])
        g = sb("cg", [P, 4, T])
        hsd = sb("hsd", [P, 2, NT, CB])
        H = sb("H", [P, 2, NT, CB])
        X = sb("X", [P, 2, NT, CB])
        Y = sb("Y", [P, 2, NT, CB])
        tmp = sb("ctmp", [P, NT, CB])
        osave = sb("osave", [P, 2, CB])
        yout = sb("yout", [P, 4, T])
        fwd = dft[:, DFT["fwd"][0]:DFT["fwd"][1]].rearrange("p (m t k) -> p m t k", m=4, t=2)
        inv = dft[:, DFT["inv"][0]:DFT["inv"][1]].rearrange("p (m k t) -> p m k t", m=4, k=2)
        fwdp = dft[:, DFT["fwdp"][0]:DFT["fwdp"][1]].rearrange("p (m k) -> p m k", m=2)
        invp = dft[:, DFT["invp"][0]:DFT["invp"][1]].rearrange("p (m t) -> p m t", m=2)
        loads = ("v", "x1", "w4", "dec", "bias", "g")
        s_l = {n: st.enter_context(nc.semaphore(f"conv_loaded_{n}")) for n in loads}
        s_dft = st.enter_context(nc.semaphore("conv_dft_loaded"))
        s_y = st.enter_context(nc.semaphore("conv_stored"))
        s_f = st.enter_context(nc.semaphore("conv_store_buffer_free"))
        pe_, ac_, dv_ = (Steps(nc, st, f"conv_{n}", M) for n in ("pe", "act", "dve"))

        with nc.Block() as block:
            @block.sync
            def _(sp):
                sp.dma_start(dft[:, :], A["dft"]).then_inc(s_dft, 16)
                with sp.Fori(0, NB) as i:
                    cs = bass.ds(i * CB, CB)
                    sp.wait_ge(pe_.sem, pe_.before(("fix", 1), i))
                    sp.wait_ge(dv_.sem, dv_.before(("w", 1), i))
                    sp.dma_start(w4[:, :, :], w4_v[:, :, cs]).then_inc(s_l["w4"], 16)
                    sp.wait_ge(dv_.sem, dv_.before(("ev", ("filt", 1, NT - 1)), i))
                    sp.dma_start(dec[:, :, :], A["decay"].rearrange("(j p) n -> p j n", p=P)[:, :, cs]).then_inc(s_l["dec"], 16)
                    sp.wait_ge(dv_.sem, dv_.before(("ev", ("fix", 1)), i))
                    sp.dma_start(bias[:, :, :], A["hy_fft_bias"][:, :, cs]).then_inc(s_l["bias"], 16)
                    sp.wait_ge(pe_.sem, pe_.before(("X", 1, 4), i))
                    for s, n in ((0, "v"), (1, "x1")):
                        sp.dma_start(vx[s][:, :, :], A["vx_d"][s].rearrange("(j p) n -> p j n", p=P)[:, :, cs]).then_inc(s_l[n], 16)
                    sp.wait_ge(dv_.sem, dv_.before(("ev", ("inv", 1, 3)), i))
                    sp.dma_start(g[:, :, :], A["g_d"][cs, :].rearrange("(c p) t -> p c t", p=P)).then_inc(s_l["g"], 16)

            @block.gpsimd
            def _(po):
                po.sem_inc(s_f, 1)
                with po.Fori(0, NB) as i:
                    po.wait_ge(dv_.sem, dv_.now(("ev", ("inv", 1, 3)), i))
                    po.dma_start(A["y_d"][bass.ds(i * CB, CB), :].rearrange("(c p) t -> p c t", p=P), yout[:, :, :]).then_inc(s_y, 16)
                    po.wait_ge(s_y, i * 16 + 16)
                    po.sem_inc(s_f, 1)
                po.wait_ge(s_y, 16 * NB)

            @block.tensor
            def _(pe):
                pe_.start(pe)
                pe.wait_ge(s_dft, 16)
                with pe.Fori(0, NB) as i:
                    for n, job in enumerate(JOBS):
                        if n >= 4:
                            pe.wait_ge(dv_.sem, dv_.now(("ev", JOBS[n - 4]), i))
                        else:
                            last_user = max(m for m in range(len(JOBS)) if m % 4 == n)
                            pe.wait_ge(dv_.sem, dv_.before(("ev", JOBS[last_user]), i))
                        q = pair[slot[job]]
                        kind, o = job[0], job[1]
                        if kind == "filt":
                            j = job[2]
                            if j == 0:
                                pe.wait_ge(dv_.sem, dv_.now(("w", o), i))
                            mm(q[:, 0, :], hid[:, j * P:(j + 1) * P], wsd[:, 0, :])
                            last = mm(q[:, 1, :], hid[:, j * P:(j + 1) * P], wsd[:, 1, :])
                        elif kind == "fix":
                            last = mm(q[:, 0, :], hid[:, 0:P], w4[:, 2 + o, :])
                        elif kind in ("H", "X"):
                            m = job[2]
                            if kind == "H":
                                src = [hsd[:, 0, :, :], hsd[:, 1, :, :]]
                                pe.wait_ge(dv_.sem, dv_.now(("row0", o), i))
                            elif o == 0:
                                src = [vx[0][:, :, :]] * 2
                                if m == 0:
                                    pe.wait_ge(s_l["v"], i * 16 + 16)
                            else:
                                src = [vx[0][:, :, :]] * 2
                                pe.wait_ge(dv_.sem, dv_.now(("ev", ("inv", 0, 2)), i))
                            if m < 4:
                                cs, kt = m // 2, m % 2
                                for par in range(2):
                                    for t in range(2):
                                        last = mm(q[:, par, :], fwd[:, 2 * cs + par, t, kt * P:(kt + 1) * P], src[cs][:, 2 * par + t, :], t == 0, t == 1)
                            else:
                                for cs in range(2):
                                    last = mm(q[:, cs, :], fwdp[:, cs, :], src[cs][:, 4, :])
                        elif o == 0:
                            m = job[2]
                            pe.wait_ge(dv_.sem, dv_.now(("comb", 0), i))
                            if m < 2:
                                for h in range(2):
                                    for kt in range(2):
                                        for cs in range(2):
                                            last = mm(q[:, h, :], inv[:, 2 * cs + m, kt, h * P:(h + 1) * P], X[:, cs, 2 * m + kt, :], kt + cs == 0, kt + cs == 2)
                            else:
                                for cs in range(2):
                                    last = mm(q[:, 0, :], invp[:, cs, :], Y[:, cs, 4, :], cs == 0, cs == 1)
                        else:
                            c4 = job[2]
                            ch = slice(c4 * P, (c4 + 1) * P)
                            pe.wait_ge(dv_.sem, dv_.now(("comb", 1), i))
                            for par in range(2):
                                for kt in range(2):
                                    for cs in range(2):
                                        mm(q[:, 0, par * 256:(par + 1) * 256], X[:, cs, 2 * par + kt, ch], inv[:, 2 * cs + par, kt, :], kt + cs == 0, kt + cs == 2)
                            for cs in range(2):
                                last = mm(q[:, 1, 0:P], Y[:, cs, 4, ch], invp[:, cs, :], cs == 0, cs == 1)
                        pe_.did(last, job)

            @block.scalar
            def _(a):
                ac_.start(a)
                with a.Fori(0, NB) as i:
                    todo = [j for j in JOBS if j[0] in ("H", "X") and j[2] < 4]
                    for n, job in enumerate(todo):
                        a.wait_ge(pe_.sem, pe_.now(job, i))
                        if n >= 2:
                            a.wait_ge(dv_.sem, dv_.now(("ev", todo[n - 2]), i))
                        else:
                            a.wait_ge(dv_.sem, dv_.before(("ev", todo[len(todo) - 2 + n]), i))
                        ac_.did(act(osave[:, n % 2, :], pair[slot[job]][:, 1, :], ACT.Copy), job)

            @block.vector
            def _(v):
                dv_.start(v)
                with v.Fori(0, NB) as i:
                    cnt = [0]

                    def link(ins, label=None):
                        dv_.did(ins, label)
                        v.wait_ge(dv_.sem, dv_.here(i))

                    def weights(o):
                        if o == 0:
                            v.wait_ge(s_l["w4"], i * 16 + 16)
                            v.wait_ge(pe_.sem, pe_.before(("filt", 1, NT - 1), i))
                        else:
                            v.wait_ge(pe_.sem, pe_.now(("filt", 0, NT - 1), i))
                        dv_.did(tt(wsd[:, 0, :], w4[:, o, :], w4[:, 2 + o, :], ADD))
                        dv_.did(tt(wsd[:, 1, :], w4[:, o, :], w4[:, 2 + o, :], SUB), ("w", o))

                    def filt(o):
                        if o == 0:
                            v.wait_ge(s_l["dec"], i * 16 + 16)
                            v.wait_ge(pe_.sem, pe_.before(("H", 1, 4), i))
                        else:
                            v.wait_ge(pe_.sem, pe_.now(("H", 0, 4), i))
                        for j in range(NT):
                            v.wait_ge(pe_.sem, pe_.now(("filt", o, j), i))
                            dj = dec[:, j:j + 1, :].to_broadcast([P, 2, CB])
                            link(tt(hsd[:, :, j, :], pair[slot["filt", o, j]][:, :, :], dj, MUL), ("ev", ("filt", o, j)))
                        v.wait_ge(pe_.sem, pe_.now(("fix", o), i))
                        if o == 0:
                            v.wait_ge(s_l["bias"], i * 16 + 16)
                        link(tt(tmp[0:1, 0, :], bias[:, o, :], pair[slot["fix", o]][0:1, 0, :], SUB), ("ev", ("fix", o)))
                        dv_.did(tt(hsd[0:1, 0, 0, :], hsd[0:1, 0, 0, :], tmp[0:1, 0, :], ADD))
                        link(tt(hsd[0:1, 0, 4, :], hsd[0:1, 0, 4, :], tmp[0:1, 0, :], ADD), ("row0", o))

                    def spectrum(kind, o, dst):
                        if kind == "X" and o == 0:
                            v.wait_ge(pe_.sem, pe_.before(("inv", 1, 3), i))
                        for m in range(5):
                            job = (kind, o, m)
                            q = pair[slot[job]]
                            if m < 4:
                                cs, kt = m // 2, m % 2
                                v.wait_ge(ac_.sem, ac_.now(job, i))
                                osv = osave[:, cnt[0] % 2, :]
                                cnt[0] += 1
                                dv_.did(tt(dst[:, cs, kt, :], q[:, 0, :], osv, ADD))
                                if cs == 0:
                                    link(tt(dst[:, cs, 2 + kt, :], q[:, 0, :], osv, SUB), ("ev", job))
                                else:
                                    link(tt(dst[:, cs, 2 + kt, :], osv, q[:, 0, :], SUB), ("ev", job))
                            else:
                                v.wait_ge(pe_.sem, pe_.now(job, i))
                                link(nc.vector.tensor_copy(dst[:, :, 4, :], q[:, :, :]), ("ev", job))

                    def product(o):
                        if o == 0:
                            v.wait_ge(pe_.sem, pe_.before(("inv", 1, 3), i))
                        else:
                            v.wait_ge(pe_.sem, pe_.now(("inv", 0, 2), i))
                        f = lambda a: a.rearrange("p j n -> p (j n)")
                        Xr, Xs, Hr, Hs = f(X[:, 0]), f(X[:, 1]), f(H[:, 0]), f(H[:, 1])
                        Yr, Ys, t_ = f(Y[:, 0]), f(Y[:, 1]), f(tmp[:, :, :])
                        dv_.did(tt(Yr, Xr, Hr, MUL))
                        link(tt(t_, Xs, Hs, MUL))
                        link(tt(Yr, Yr, t_, SUB))
                        dv_.did(tt(Ys, Xr, Hs, MUL))
                        link(tt(t_, Xs, Hr, MUL))
                        link(tt(Ys, Ys, t_, ADD))
                        dv_.did(tt(X[:, 0, 0:2, :], Y[:, 0, 0:2, :], Y[:, 0, 2:4, :], ADD))
                        dv_.did(tt(X[:, 0, 2:4, :], Y[:, 0, 0:2, :], Y[:, 0, 2:4, :], SUB))
                        dv_.did(tt(X[:, 1, 0:2, :], Y[:, 1, 0:2, :], Y[:, 1, 2:4, :], SUB))
                        link(tt(X[:, 1, 2:4, :], Y[:, 1, 0:2, :], Y[:, 1, 2:4, :], ADD), ("comb", o))

                    weights(0)
                    filt(0)
                    spectrum("H", 0, H)
                    spectrum("X", 0, X)
                    weights(1)
                    product(0)
                    filt(1)
                    for m in range(3):
                        job = ("inv", 0, m)
                        v.wait_ge(pe_.sem, pe_.now(job, i))
                        if m == 0:
                            v.wait_ge(s_l["x1"], i * 16 + 16)
                            v.wait_ge(pe_.sem, pe_.now(("X", 0, 4), i))
                        q = pair[slot[job]]
                        js = slice(2 * m, min(2 * m + 2, NT))
                        w_ = 2 if m < 2 else 1
                        link(tt(vx[0][:, js, :], q[:, 0:w_, :], vx[1][:, js, :], MUL), ("ev", job))
                    spectrum("H", 1, H)
                    spectrum("X", 1, X)
                    product(1)
                    v.wait_ge(s_l["g"], i * 16 + 16)
                    v.wait_ge(s_f, i + 1)
                    for c4 in range(4):
                        job = ("inv", 1, c4)
                        v.wait_ge(pe_.sem, pe_.now(job, i))
                        q = pair[slot[job]]
                        dst = yout[:, c4, 0:LS].rearrange("p (t r) -> p r t", r=2)
                        gg = g[:, c4, 0:LS].rearrange("p (t r) -> p r t", r=2)
                        dv_.did(tt(dst, q[:, 0, :].rearrange("p (r t) -> p r t", r=2), gg, MUL))
                        dv_.did(tt(yout[:, c4, LS:T], q[:, 1, 0:LP], g[:, c4, LS:T], MUL), ("ev", job))


def out_proj(nc, A, G, M, l, w_dram):
    mm, stt, ts, tt, act = make_ops(nc)
    ps = G["ps"]
    HALF = D // 2
    RING = 6
    with ExitStack() as st:
        sb = lambda n, s: st.enter_context(nc.sbuf_tensor(f"{n}{l}", s, F32))
        y = sb("oy", [P, KE, T])
        w = sb("ow", [P, RING, HALF])
        o = sb("oo", [P, NT, D])
        x = sb("ox", [P, NT, D])
        gate = sb("ogate", [P, 2, D])
        bo = sb("obias", [P, D]) if l == 0 else None
        sq, ss, rs = sb("osq", [P, D]), sb("oss", [P, NT]), sb("ors", [P, NT])
        s_y = [st.enter_context(nc.semaphore(f"out{l}_y{k}")) for k in range(4)]
        s_w = [st.enter_context(nc.semaphore(f"out{l}_w{k}")) for k in range(RING)]
        s_x = st.enter_context(nc.semaphore(f"out{l}_x_loaded"))
        s_o = st.enter_context(nc.semaphore(f"out{l}_stored"))
        pe_, ac_, dv_ = (Steps(nc, st, f"out{l}_{n}", M) for n in ("pe", "act", "dve"))
        n_x = [0]
        with nc.Block() as block:
            @block.sync
            def _(sp):
                for k4 in range(4):
                    sp.dma_start(y[:, 4 * k4:4 * k4 + 4, :], A["y_d"][k4 * CB:(k4 + 1) * CB, :].rearrange("(k p) t -> p k t", p=P)).then_inc(s_y[k4], 16)
                n_x[0] = 0
                def xl(dst, src):
                    sp.dma_start(dst, src).then_inc(s_x, 16)
                    n_x[0] += 16
                if l == 0:
                    xl(x[:, 0:4, :], A["x_sample"][0].rearrange("(j p) n -> p j n", p=P))
                    xl(x[:, 4, :], A["x_prompt"][0])
                    xl(bo[:, :], A["hy_b_out"][0:1, :].partition_broadcast(P))
                else:
                    xl(x[:, :, :], A["x1_d"].rearrange("(j p) n -> p j n", p=P))
                for c in range(2):
                    xl(gate[:, c, :], A["gate_d"][l, c:c + 1, :].partition_broadcast(P))
                for n in range(2 * KE):
                    h, k = n // KE, n % KE
                    if n >= RING:
                        sp.wait_ge(pe_.sem, pe_.now(("k", n - RING)))
                    sp.dma_start(w[:, n % RING, :], w_dram[0, k * P:(k + 1) * P, h * HALF:(h + 1) * HALF]).then_inc(s_w[n % RING], 16)
                for j in range(NT):
                    sp.wait_ge(dv_.sem, dv_.now(("x", j)))
                    dst = A["x1_d"][j * P:(j + 1) * P, :] if l == 0 else (A["y_sample"][0, j * P:(j + 1) * P, :] if j < 4 else A["y_prompt"][0])
                    sp.dma_start(dst, x[:, j, :]).then_inc(s_o, 16)
                sp.wait_ge(s_o, 16 * NT)

            @block.tensor
            def _(pe):
                for n in range(2 * KE):
                    h, k = n // KE, n % KE
                    if h == 0 and k % 4 == 0:
                        pe.wait_ge(s_y[k // 4], 16)
                    pe.wait_ge(s_w[n % RING], 16 * (n // RING + 1))
                    if h == 1 and k == 0:
                        pe.wait_ge(dv_.sem, dv_.now(("oj", 0, NT - 1)))
                    for j in range(NT):
                        last = mm(ps[:, j, :], y[:, k, j * P:(j + 1) * P], w[:, n % RING, :], k == 0, k == KE - 1)
                    pe_.did(last, ("k", n))

            @block.vector
            def _(v):
                def link(ins, label=None):
                    dv_.did(ins, label)
                    v.wait_ge(dv_.sem, dv_.here())
                v.wait_ge(s_x, n_x[0])
                for h in range(2):
                    v.wait_ge(pe_.sem, pe_.now(("k", (h + 1) * KE - 1)))
                    hs = slice(h * HALF, (h + 1) * HALF)
                    for j in range(NT):
                        if l == 0:
                            ins = tt(o[:, j, hs], ps[:, j, :], bo[:, hs], ADD)
                        else:
                            ins = nc.vector.tensor_copy(o[:, j, hs], ps[:, j, :])
                        dv_.did(ins, ("oj", h, j))
                v.wait_ge(ac_.sem, ac_.now("ss"))
                dv_.did(ts(ss[:, :], ss[:, :], 1.0 / D, EPS, MUL, ADD), "var")
                v.wait_ge(ac_.sem, ac_.now("std"))
                link(nc.vector.reciprocal(rs[:, :], rs[:, :]))
                for j in range(NT):
                    link(stt(o[:, j, :], o[:, j, :], rs[:, j:j + 1], gate[:, j // 4, :], MUL, MUL))
                    dv_.did(tt(x[:, j, :], x[:, j, :], o[:, j, :], ADD), ("x", j))

            @block.scalar
            def _(a):
                for j in range(NT):
                    a.wait_ge(dv_.sem, dv_.now(("oj", 1, j)))
                    if j:
                        a.wait_ge(ac_.sem, ac_.here())
                    ac_.did(act(sq[:, :], o[:, j, :], ACT.Square, accum_out=ss[:, j:j + 1]), "ss")
                a.wait_ge(dv_.sem, dv_.now("var"))
                ac_.did(act(rs[:, :], ss[:, :], ACT.Sqrt), "std")
def rwkv_in(nc, A, G, M, hT):
    mm, stt, ts, tt, act = make_ops(nc)
    ps, col = G["ps"], G["col"]
    pair = [ps[:, 2 * q:2 * q + 2, :].rearrange("p b n -> p (b n)") for q in range(4)]
    MIX = {"r": 0, "w": 1, "k": 2, "v": 3, "a": 4, "z": 5}
    BIG = ("r", "k", "v", "z")
    SEQ = ("w", "a") + BIG
    U = 4
    with ExitStack() as st:
        sb = lambda n, s: st.enter_context(nc.sbuf_tensor(n, s, F32))
        xx = sb("xx", [P, KD, T])
        mix = [sb(f"mix{b}", [P, KD, T]) for b in range(2)]
        lw = [sb(f"lora_w{b}", [P, KD, 2, HID]) for b in range(2)]
        w = [sb(f"rw{u}", [P, KD, P]) for u in range(U)]
        out = [sb(f"rout{u}", [P, T]) for u in range(U)]
        sig = sb("rsig", [P, T])
        s_lw = st.enter_context(nc.semaphore("rw_lora_loaded"))
        s_w = [st.enter_context(nc.semaphore(f"rw_weights_{u}")) for u in range(U)]
        s_o = [st.enter_context(nc.semaphore(f"rw_stored_{u}")) for u in range(U)]
        s_f = [st.enter_context(nc.semaphore(f"rw_store_buffer_free_{u}")) for u in range(U)]
        mx = Steps(nc, st, "rw_mixes", M)
        lo_pe, lo_ac = Steps(nc, st, "rw_lora_pe", M), Steps(nc, st, "rw_lora_act", M)
        pe_ = {b: Steps(nc, st, f"rw_pe_{b}", M) for b in BIG}
        ac_ = {b: Steps(nc, st, f"rw_act_{b}", M) for b in BIG}
        dv_ = Steps(nc, st, "rw_dve_z", M)
        ROUNDS = KE // U
        mu = col[:, 0, 80:128].rearrange("p (m k) -> p m k", m=6)

        with nc.Block() as block:
            @block.sync
            def _(sp):
                for b, n in enumerate(("rw_w1", "rw_a1")):
                    for z in range(2):
                        sp.dma_start(lw[b][:, :, z, :], A[n][0, z].rearrange("(k p) r -> p k r", p=P)).then_inc(s_lw, 16)
                for bi, b in enumerate(BIG):
                    w_v = A[f"rw_w_{b}"][0].rearrange("(k p) n -> p k n", p=P)
                    if bi:
                        sp.wait_ge(pe_[BIG[bi - 1]].sem, (ROUNDS + 1) * pe_[BIG[bi - 1]].per())
                    with sp.Fori(0, ROUNDS) as i:
                        for u in range(U):
                            sp.wait_ge(pe_[b].sem, pe_[b].before(("proj", u), i))
                            sp.dma_start(w[u][:, :, :], w_v[:, :, bass.ds(i * U * P + u * P, P)]).then_inc(s_w[u], 16)

            @block.vector
            def _(v):
                dv_.start(v)

                def link(ins, label=None):
                    mx.did(ins, label)
                    v.wait_ge(mx.sem, mx.here())
                link(ts(xx[:, :, :], hT[:, :, :], -1.0, None, MUL))
                grid = lambda a, k0: a[:, k0:k0 + 2, 0:LS].rearrange("p k (r c) -> p k r c", c=GRID)
                for k in range(2):
                    for k0, dst, src in ((0, (slice(None), slice(1, GRID)), (slice(None), slice(0, GRID - 1))),
                                         (2, (slice(None), slice(0, GRID - 1)), (slice(None), slice(1, GRID)))):
                        g = lambda a, sl: a[:, k0 + k, 0:LS].rearrange("p (r c) -> p r c", c=GRID)[:, sl[0], sl[1]]
                        mx.did(tt(g(xx, dst), g(xx, dst), g(hT, src), ADD))
                mx.did(tt(xx[:, 4:6, GRID:LS], xx[:, 4:6, GRID:LS], hT[:, 4:6, 0:LS - GRID], ADD))
                mx.did(tt(xx[:, 6:8, 0:LS - GRID], xx[:, 6:8, 0:LS - GRID], hT[:, 6:8, GRID:LS], ADD))
                mx.did(tt(xx[:, 0:4, LS + 1:T], xx[:, 0:4, LS + 1:T], hT[:, 0:4, LS:T - 1], ADD))
                link(tt(xx[:, 4:8, LS:T - 1], xx[:, 4:8, LS:T - 1], hT[:, 4:8, LS + 1:T], ADD))

                def make(n):
                    b = SEQ[n]
                    if n >= 2:
                        p_ = SEQ[n - 2]
                        if p_ in BIG:
                            v.wait_ge(pe_[p_].sem, (ROUNDS + 1) * pe_[p_].per())
                        else:
                            v.wait_ge(lo_pe.sem, lo_pe.now(p_))
                    for k in range(KD):
                        mx.did(stt(mix[n % 2][:, k, :], xx[:, k, :], mu[:, MIX[b], k:k + 1], hT[:, k, :], MUL, ADD), ("mix", b))
                for n in range(len(SEQ)):
                    make(n)
                with v.Fori(0, ROUNDS) as i:
                    for u in range(U):
                        v.wait_ge(ac_["z"].sem, ac_["z"].now(("sig", u), i))
                        v.wait_ge(s_f[u], 3 * ROUNDS + i + 1)
                        dv_.did(tt(out[u][:, :], pair[u][:, 0:T], sig[:, :], MUL), ("z", u))

            @block.tensor
            def _(pe):
                pe.wait_ge(s_lw, 64)
                for n, b in enumerate(SEQ):
                    pe.wait_ge(mx.sem, mx.now(("mix", b)))
                    m = mix[n % 2]
                    if b in ("w", "a"):
                        for k in range(KD):
                            lhsT = lw[n][:, k, :, :].rearrange("p z r -> p (z r)")
                            mm(pair[n][:, 0:LS], lhsT, m[:, k, 0:LS], k == 0, k == KD - 1)
                            last = mm(pair[n][:, LS:T], lhsT, m[:, k, LS:T], k == 0, k == KD - 1)
                        lo_pe.did(last, b)
                        continue
                    bi = BIG.index(b)
                    if bi == 0:
                        pe.wait_ge(lo_ac.sem, lo_ac.now("a"))
                    else:
                        pe.wait_ge(ac_[BIG[bi - 1]].sem, (ROUNDS + 1) * ac_[BIG[bi - 1]].per())
                    pe_[b].start(pe)
                    with pe.Fori(0, ROUNDS) as i:
                        for u in range(U):
                            pe.wait_ge(s_w[u], (bi * ROUNDS + i) * 16 + 16)
                            if b == "z":
                                pe.wait_ge(dv_.sem, dv_.before(("z", u), i))
                            else:
                                pe.wait_ge(ac_[b].sem, ac_[b].before(("out", u), i))
                            for k in range(KD):
                                mm(pair[u][:, 0:LS], w[u][:, k, :], m[:, k, 0:LS], k == 0, k == KD - 1)
                                last = mm(pair[u][:, LS:T], w[u][:, k, :], m[:, k, LS:T], k == 0, k == KD - 1)
                            pe_[b].did(last, ("proj", u))

            @block.scalar
            def _(a):
                for n, (b, f, dst) in enumerate((("w", ACT.Tanh, G["wlo"]), ("a", ACT.Copy, G["alo"]))):
                    a.wait_ge(lo_pe.sem, lo_pe.now(b))
                    lo_ac.did(act(dst[:, :], pair[n][:, 0:T], f), b)
                for bi, b in enumerate(BIG):
                    ac_[b].start(a)
                    with a.Fori(0, ROUNDS) as i:
                        for u in range(U):
                            a.wait_ge(pe_[b].sem, pe_[b].now(("proj", u), i))
                            if b == "z":
                                if u:
                                    a.wait_ge(dv_.sem, dv_.now(("z", u - 1), i))
                                else:
                                    a.wait_ge(dv_.sem, dv_.before(("z", U - 1), i))
                                ac_[b].did(act(sig[:, :], pair[u][:, 0:T], ACT.Sigmoid), ("sig", u))
                            else:
                                a.wait_ge(s_f[u], bi * ROUNDS + i + 1)
                                ac_[b].did(act(out[u][:, :], pair[u][:, 0:T], ACT.Copy), ("out", u))

            @block.gpsimd
            def _(po):
                for u in range(U):
                    po.sem_inc(s_f[u], 1)
                for bi, b in enumerate(BIG):
                    with po.Fori(0, ROUNDS) as i:
                        for u in range(U):
                            if b == "z":
                                po.wait_ge(dv_.sem, dv_.now(("z", u), i))
                            else:
                                po.wait_ge(ac_[b].sem, ac_[b].now(("out", u), i))
                            po.dma_start(A["rkvz_d"][bi, bass.ds(i * U * P + u * P, P), :], out[u][:, :]).then_inc(s_o[u], 16)
                        for u in range(U):
                            po.wait_ge(s_o[u], (bi * ROUNDS + i) * 16 + 16)
                            po.sem_inc(s_f[u], 1)
                for u in range(U):
                    po.wait_ge(s_o[u], 16 * ROUNDS * 4)


def rwkv_scan(nc, A, G, M):
    mm, stt, ts, tt, act = make_ops(nc)
    ps, tab, col = G["ps"], G["tab"], G["col"]
    T_ = lambda n: tab[:, TAB[n][0]:TAB[n][1]]
    ident, heads, chunk = T_("ident"), T_("heads"), T_("chunk")
    level = T_("level").rearrange("p (l n) -> p l n", l=LEVELS)
    HALVES = (slice(0, 64), slice(64, 128))
    G4 = [(0, 4), (4, 4), (8, 2)]
    G2 = [(2 * g, 2) for g in range(5)]
    SEQS = (("s", 0, CS), ("p", CS, NC))
    with ExitStack() as st:
        sb = lambda n, s: st.enter_context(nc.sbuf_tensor(n, s, F32))
        r, k, v, z = (sb(f"e_{n}", [P, T]) for n in "rkvz")
        pcl = sb("e_pc", [P, 10])
        omka = sb("e_omka", [P, 1])
        lw2, la2 = sb("e_w2", [P, P]), sb("e_a2", [P, P])
        ld = [sb(f"e_ld{d}", [P, T]) for d in range(2)]
        ic = [sb(f"e_ic{d}", [P, T]) for d in range(2)]
        cum, tmp, e1, e2, e3 = (sb(f"e_{n}", [P, T]) for n in ("cum", "tmp", "e1", "e2", "e3"))
        kk, kd, bb = (sb(f"e_{n}", [P, T]) for n in ("kk", "kd", "bb"))
        kr = sb("e_kr", [P, T])
        BDar = sb("BDar", [P, NC, 2, P])
        BDb, BDk, BDv = (sb(f"BD{n}", [P, NC, P]) for n in "bkv")
        At, Bt, Kt, V = (sb(f"e_{n}t", [P, NC, P]) for n in "abkv")
        Mb, Mk = sb("Mb", [P, NC, 2, P]), sb("Mk", [P, NC, 2, P])
        Am = sb("Am", [P, NC, P])
        Q, Y, Tm, TX, TA = (sb(f"e_{n}", [P, NC, P]) for n in ("Q", "Y", "T", "TX", "TA"))
        U = [sb(f"U{q}", [P, P]) for q in range(2)]
        S = {s: [sb(f"S{s}{q}", [P, P]) for q in range(2)] for s in "sp"}
        Sd, S_back = sb("Sd", [P, P]), sb("S_back", [P, P])
        st0 = sb("st0", [P, 2, P])
        stn = sb("stn", [P, 2, P])
        o, o2, bon, stat = (sb(f"e_{n}", [P, T]) for n in ("o", "o2", "bon", "stat"))
        yo = sb("e_yo", [P, T])
        names = ("r", "k", "v", "z", "w2", "a2", "s0", "s1", "s2", "s3")
        s_l = {n: st.enter_context(nc.semaphore(f"scan_loaded_{n}")) for n in names}
        s_y = st.enter_context(nc.semaphore("scan_y_stored"))
        s_n = st.enter_context(nc.semaphore("scan_state_stored"))
        s_f = st.enter_context(nc.semaphore("scan_store_buffers_free"))
        s_z = st.enter_context(nc.semaphore("scan_cleared"))
        pe_, ac_, dv_, po_ = (Steps(nc, st, f"scan_{n}", M) for n in ("pe", "act", "dve", "pool"))
        flat = lambda q: ps[:, 2 * q:2 * q + 2, :].rearrange("p b n -> p (b n)")
        half = lambda a, h: a[HALVES[h], :].rearrange("p (c t) -> p c t", t=C)

        with nc.Block() as block:
            @block.sync
            def _(sp):
                sp.wait_ge(s_z, 5)
                with sp.Fori(0, KE) as i:
                    ch = bass.ds(i * P, P)
                    for bi, (n, dst) in enumerate((("r", r), ("k", k), ("v", v), ("z", z))):
                        sp.wait_ge(dv_.sem, dv_.before("y", i))
                        sp.dma_start(dst[:, :], A["rkvz_d"][bi, ch, :]).then_inc(s_l[n], 16)
                    for n, src, dst in (("w2", "rw_w2", lw2), ("a2", "rw_a2", la2)):
                        sp.dma_start(dst[:, :], A[src][0].rearrange("z r e -> (z r) e")[:, ch]).then_inc(s_l[n], 16)
                    sp.wait_ge(pe_.sem, pe_.before(("S0", 1), i))
                    for d, src in enumerate(("state_rwkv_fwd", "state_rwkv_bwd")):
                        rows = A[src][0, 0].rearrange("h v k -> (h v) k")
                        for h in range(2):
                            sp.dma_start(st0[HALVES[h], d, HALVES[h]], rows[bass.ds(i * P + 64 * h, 64), :]).then_inc(s_l[f"s{2 * d + h}"], 16)

            @block.gpsimd
            def _(po):
                for t_ in (BDar, BDb, BDk, BDv, st0):
                    a = t_[:, :, :, :].rearrange("p c q n -> p (c q n)") if t_ is BDar else t_[:, :, :].rearrange("p c n -> p (c n)")
                    nc.gpsimd.memset(a, 0.0).then_inc(s_z, 1)
                po_.start(po)
                po.sem_inc(s_f, 1)
                with po.Fori(0, KE) as i:
                    for d in range(2):
                        po.wait_ge(dv_.sem, dv_.now(("Z", d, 0, 2), i))
                        po_.did(nc.gpsimd.tensor_tensor(Q[:, :, :], Q[:, :, :], ident.rearrange("p (o n) -> p o n", o=1).to_broadcast([P, NC, P]), ADD), ("Q", d, 0))
                    po.wait_ge(dv_.sem, dv_.now("y", i))
                    po.dma_start(A["y_d"][bass.ds(i * P, P), :], yo[:, :]).then_inc(s_y, 16)
                    po.wait_ge(ac_.sem, ac_.now("stn", i))
                    for d, n in enumerate(("new_state_fwd", "new_state_bwd")):
                        rows = A[n][0, 0].rearrange("h v k -> (h v) k")
                        for h in range(2):
                            po.dma_start(rows[bass.ds(i * P + 64 * h, 64), :], stn[HALVES[h], d, HALVES[h]]).then_inc(s_n, 16)
                    po.wait_ge(s_y, i * 16 + 16)
                    po.wait_ge(s_n, i * 64 + 64)
                    po.sem_inc(s_f, 1)
                po.wait_ge(s_y, 16 * KE)
                po.wait_ge(s_n, 64 * KE)

            @block.tensor
            def _(pe):
                pe_.start(pe)
                with pe.Fori(0, KE) as i:
                    D_ = lambda label: pe.wait_ge(dv_.sem, dv_.now(label, i))
                    A_ = lambda label: pe.wait_ge(ac_.sem, ac_.now(label, i))
                    pe.wait_ge(s_l["w2"], i * 16 + 16)
                    pe.wait_ge(s_l["a2"], i * 16 + 16)
                    pe.wait_ge(dv_.sem, dv_.before("y", i))
                    pe.wait_ge(ac_.sem, ac_.before("stn", i))
                    for q, (w_, lo) in enumerate(((lw2, "wlo"), (la2, "alo"))):
                        for d in range(2):
                            f = flat(2 * q + d)
                            mm(f[:, 0:LS], w_[HALVES[d], :], G[lo][HALVES[d], 0:LS])
                            last = mm(f[:, LS:T], w_[HALVES[d], :], G[lo][HALVES[d], LS:T])
                            pe_.did(last, ("lora", q, d) if (q, d) != (1, 1) else "lora")
                    D_("kk2")
                    A_(("sg", 0, 0))
                    mm(flat(0)[:, 0:LS], heads, tmp[:, 0:LS])
                    pe_.did(mm(flat(0)[:, LS:T], heads, tmp[:, LS:T]), "ss")
                    D_("BDv")
                    A_("ic1")
                    for g, (c0, n) in enumerate(G4):
                        for c in range(n):
                            last = nc.tensor.transpose(ps[:, 5 + g, c * P:(c + 1) * P], BDv[:, c0 + c, :], ident)
                        pe_.did(last, ("V", g))
                    A_(("sg", 0, 1))
                    for n in ("s0", "s1", "s2", "s3"):
                        pe.wait_ge(s_l[n], i * 16 + 16)
                    for d in range(2):
                        pe_.did(nc.tensor.transpose(ps[:, 2, d * P:(d + 1) * P], st0[:, d, :], ident), ("S0", d))

                    for d in range(2):
                        D_(("BD", d))
                        if d == 0:
                            A_("V")
                        else:
                            D_(("o", 0))
                            A_(("stn", 0))
                        for g, (c0, n) in enumerate(G4):
                            if g:
                                A_(("tr", d, g - 1))
                            for q, src in enumerate((BDar[:, :, 0, :], BDb[:, :, :], BDk[:, :, :])):
                                for c in range(n):
                                    last = nc.tensor.transpose(ps[:, 3 + q, c * P:(c + 1) * P], src[:, c0 + c, :], ident)
                            pe_.did(last, ("tr", d, g))
                        for g, (c0, n) in enumerate(G2):
                            if g >= 2:
                                D_(("M", d, g - 2))
                            for q, src in enumerate((BDb, BDk)):
                                for c in range(n):
                                    last = mm(ps[:, (6, 0)[g % 2] + q, c * 256:(c + 1) * 256], src[:, c0 + c, :], BDar[:, c0 + c, :, :].rearrange("p q n -> p (q n)"))
                            pe_.did(last, ("M", d, g))
                        A_(("tr", d, 2))
                        for g, (c0, n) in enumerate(G4):
                            for c in range(n):
                                last = mm(ps[:, 3 + g, c * P:(c + 1) * P], BDar[:, c0 + c, 0, :], BDb[:, c0 + c, :])
                            pe_.did(last, ("A", d, g))
                        D_(("M", d, 4))
                        if d == 0:
                            D_("S0")
                        for g, (c0, n) in enumerate(G4):
                            for c in range(n):
                                last = mm(ps[:, g, c * P:(c + 1) * P], Mk[:, c0 + c, 0, :], V[:, c0 + c, :])
                            pe_.did(last, ("XV", d, g))
                        pe.wait_ge(po_.sem, po_.now(("Q", d, 0), i))
                        D_(("A", d, 2))
                        for lv in range(LEVELS):
                            if lv:
                                for g, (c0, n) in enumerate(G4):
                                    if g == 0:
                                        A_(("T", d, lv - 1, 2))
                                    if lv > 1:
                                        D_(("Qn", d, lv - 1, g))
                                    for c in range(n):
                                        last = mm(ps[:, 3 + g, c * P:(c + 1) * P], Am[:, c0 + c, :], Q[:, c0 + c, :])
                                    pe_.did(last, ("Y", d, lv, g))
                                for g, (c0, n) in enumerate(G4):
                                    A_(("Y", d, lv, g))
                                    A_(("T", d, lv - 1, g))
                                    for c in range(n):
                                        last = mm(ps[:, (6, 7, 0)[g], c * P:(c + 1) * P], Tm[:, c0 + c, :], Y[:, c0 + c, :])
                                    pe_.did(last, ("Z", d, lv, g))
                            else:
                                A_(("XV", d, 0)), A_(("XV", d, 2))
                            if lv < LEVELS - 1:
                                for g, (c0, n) in enumerate(G4):
                                    if lv:
                                        D_(("Qn", d, lv, g))
                                    for c in range(n):
                                        last = nc.tensor.transpose(ps[:, (1, 2, 3)[g], c * P:(c + 1) * P], Q[:, c0 + c, :], ident)
                                    pe_.did(last, ("T", d, lv, g))
                        for g, (c0, n) in enumerate(G4):
                            D_(("Qn", d, LEVELS - 1, g))
                            A_(("XV", d, 2))
                            for c in range(n):
                                last = mm(ps[:, 3 + g, c * P:(c + 1) * P], Q[:, c0 + c, :], TX[:, c0 + c, :])
                            pe_.did(last, ("TX", d, g))
                            for c in range(n):
                                last = mm(ps[:, (6, 7, 0)[g], c * P:(c + 1) * P], At[:, c0 + c, :], Q[:, c0 + c, :])
                            pe_.did(last, ("TA", d, g))
                        A_(("TX", d, 2))
                        D_(("TA", d, 2))
                        D_(("Sinit", d))
                        for s, c0, c1 in SEQS:
                            order = range(c0, c1) if d == 0 else range(c1 - 1, c0 - 1, -1)
                            for n, c in enumerate(order):
                                cur = S[s][n % 2]
                                if n:
                                    D_(("S", d, s, n - 1))
                                elif s == "p":
                                    D_(("S", d, "s", CS - 1))
                                pe_.did(mm(ps[:, 1, 0:P], TA[:, c, :], cur[:, :]), ("U", d, s, n))
                                mm(ps[:, 2, 0:P], Kt[:, c, :], V[:, c, :], True, False)
                                if n >= 2:
                                    D_(("O", d, s, n - 2))
                                elif s == "p":
                                    D_(("O", d, "s", CS - 1))
                                ob = ps[:, 3 + n % 2, 0:P]
                                mm(ob, cur[:, :], BDar[:, c, 1, :], True, False)
                                mm(ob, V[:, c, :], Mk[:, c, 1, :], False, False)
                                D_(("U", d, s, n))
                                pe_.did(mm(ps[:, 2, 0:P], Bt[:, c, :], U[n % 2][:, :], False, True), ("S", d, s, n))
                                pe_.did(mm(ob, U[n % 2][:, :], Mb[:, c, 1, :], False, True), ("O", d, s, n))
                        D_(("S", d, "p", 1))
                        pe_.did(nc.tensor.transpose(ps[:, 5, d * P:(d + 1) * P], S["p"][0][:, :], ident), ("stn", d))
                    D_(("o", 1))
                    mm(flat(0)[:, 0:LS], heads, o[:, 0:LS])
                    pe_.did(mm(flat(0)[:, LS:T], heads, o[:, LS:T]), "mean")
                    D_("bonus_in")
                    mm(flat(3)[:, 0:LS], heads, bon[:, 0:LS])
                    pe_.did(mm(flat(3)[:, LS:T], heads, bon[:, LS:T]), "bonus")
                    A_("sq")
                    mm(flat(1)[:, 0:LS], heads, o2[:, 0:LS])
                    pe_.did(mm(flat(1)[:, LS:T], heads, o2[:, LS:T]), "var")

            @block.scalar
            def _(a):
                ac_.start(a)
                with a.Fori(0, KE) as i:
                    P_ = lambda label: a.wait_ge(pe_.sem, pe_.now(label, i))
                    D_ = lambda label: a.wait_ge(dv_.sem, dv_.now(label, i))
                    D_("pcl")
                    for q, dst in enumerate((ld, ic)):
                        for d in range(2):
                            P_(("lora", q, d) if (q, d) != (1, 1) else "lora")
                            a.wait_ge(dv_.sem, dv_.before("y", i))
                            ac_.did(act(dst[d][:, :], flat(2 * q + d)[:, 0:T], ACT.Sigmoid, bias=pcl[:, 2 * q + d:2 * q + d + 1]),
                                    ("sg", 0, d) if q == 0 else f"ic{d}")
                    P_("ss")
                    ac_.did(act(stat[:, :], flat(0)[:, 0:T], ACT.Sqrt), "norm")
                    for g, (c0, n) in enumerate(G4):
                        P_(("V", g))
                        last = act(V[:, c0:c0 + n, :].rearrange("p c n -> p (c n)"), ps[:, 5 + g, 0:n * P], ACT.Copy)
                    ac_.did(last, "V")
                    for d in range(2):
                        D_(("cum", d))
                        act(e1[:, :], cum[:, :], ACT.Exp)
                        act(e2[:, :], cum[:, :], ACT.Exp, scale=-1.0)
                        ac_.did(act(e3[:, :], tmp[:, :], ACT.Exp), ("exp", d))
                        for g, (c0, n) in enumerate(G4):
                            P_(("tr", d, g))
                            for q, dst in enumerate((At, Bt, Kt)):
                                last = act(dst[:, c0:c0 + n, :].rearrange("p c n -> p (c n)"), ps[:, 3 + q, 0:n * P], ACT.Copy)
                            ac_.did(last, ("tr", d, g))
                        for g, (c0, n) in enumerate(G4):
                            P_(("XV", d, g))
                            last = ac_.did(act(TX[:, c0:c0 + n, :].rearrange("p c n -> p (c n)"), ps[:, g, 0:n * P], ACT.Copy), ("XV", d, g))
                        for lv in range(LEVELS):
                            if lv:
                                for g, (c0, n) in enumerate(G4):
                                    P_(("Y", d, lv, g))
                                    ac_.did(act(Y[:, c0:c0 + n, :].rearrange("p c n -> p (c n)"), ps[:, 3 + g, 0:n * P], ACT.Copy), ("Y", d, lv, g))
                            if lv < LEVELS - 1:
                                for g, (c0, n) in enumerate(G4):
                                    P_(("T", d, lv, g))
                                    ac_.did(act(Tm[:, c0:c0 + n, :].rearrange("p c n -> p (c n)"), ps[:, (1, 2, 3)[g], 0:n * P], ACT.Copy), ("T", d, lv, g))
                        for g, (c0, n) in enumerate(G4):
                            P_(("TX", d, g))
                            if g == 0:
                                P_(("TX", d, 2))
                            ac_.did(act(TX[:, c0:c0 + n, :].rearrange("p c n -> p (c n)"), ps[:, 3 + g, 0:n * P], ACT.Copy), ("TX", d, g))
                        P_(("stn", d))
                        if d == 0:
                            a.wait_ge(s_f, i + 1)
                        ac_.did(act(stn[:, d, :], ps[:, 5, d * P:(d + 1) * P], ACT.Copy), ("stn", d))
                    D_("oc")
                    ac_.did(act(o2[:, :], o[:, :], ACT.Square), "sq")
                    D_("varv")
                    ac_.did(act(stat[:, :], stat[:, :], ACT.Sqrt), "gstd")
                    ac_.note("stn")

            @block.vector
            def _(v_):
                dv_.start(v_)
                w0a0 = col[:, 2, 96:128].rearrange("p (q k) -> p q k", k=KE)
                rest = col[:, 3, :].rearrange("p (q k) -> p q k", k=KE)
                v_.wait_ge(s_z, 5)
                with v_.Fori(0, KE) as i:
                    def link(ins, label=None):
                        dv_.did(ins, label)
                        v_.wait_ge(dv_.sem, dv_.here(i))
                    P_ = lambda label: v_.wait_ge(pe_.sem, pe_.now(label, i))
                    A_ = lambda label: v_.wait_ge(ac_.sem, ac_.now(label, i))
                    v_.wait_ge(ac_.sem, ac_.before("stn", i))
                    dv_.did(nc.vector.tensor_copy(pcl[:, 0:2], w0a0[:, :, bass.ds(i, 1)].rearrange("p s o -> p (s o)")))
                    link(nc.vector.tensor_copy(pcl[:, 2:10], rest[:, :, bass.ds(i, 1)].rearrange("p s o -> p (s o)")), "pcl")
                    dv_.did(ts(omka[:, :], pcl[:, 5:6], -1.0, 1.0, MUL, ADD))
                    v_.wait_ge(s_l["k"], i * 16 + 16)
                    link(ts(kk[:, :], k[:, :], pcl[:, 4:5], None, MUL))
                    link(tt(tmp[:, :], kk[:, :], kk[:, :], MUL), "kk2")
                    v_.wait_ge(s_l["v"], i * 16 + 16)
                    for h in range(2):
                        dv_.did(nc.vector.tensor_copy(BDv[HALVES[h], :, HALVES[h]], half(v, h)), "BDv")
                    A_("norm")
                    link(ts(stat[:, :], stat[:, :], 1e-12, None, ALU.max))
                    link(nc.vector.reciprocal(stat[:, :], stat[:, :]))
                    link(tt(kk[:, :], kk[:, :], stat[:, :], MUL), "kk")
                    v_.wait_ge(s_l["r"], i * 16 + 16)
                    for d in range(2):
                        A_(("sg", 0, d))
                        link(ts(ld[d][:, :], ld[d][:, :], -DECAY_MAX, None, MUL))
                        link(nc.vector.tensor_tensor_scan(cum[:, :], chunk, ld[d][:, :], 0.0, MUL, ADD))
                        if d == 0:
                            P_("ss")
                            link(tt(tmp[:, :], cum[:, :], ld[d][:, :], SUB), ("cum", d))
                        else:
                            c3 = cum[:, :].rearrange("p (c t) -> p c t", t=C)
                            tot = c3[:, :, C - 1:C].to_broadcast([P, NC, C])
                            link(tt(tmp[:, :].rearrange("p (c t) -> p c t", t=C), tot, c3, SUB))
                            link(tt(cum[:, :], tmp[:, :], ld[d][:, :], ADD), ("cum", d))
                        A_(f"ic{d}")
                        link(ts(kd[:, :], ic[d][:, :], pcl[:, 5:6], omka[:, :], MUL, ADD))
                        link(tt(kd[:, :], kd[:, :], k[:, :], MUL))
                        if d == 0:
                            dv_.did(ts(kr[:, :], kd[:, :], pcl[:, 6:7], None, MUL))
                        else:
                            link(stt(kr[:, :], kd[:, :], pcl[:, 7:8], kr[:, :], MUL, ADD))
                        link(tt(bb[:, :], kk[:, :], ic[d][:, :], MUL))
                        A_(("exp", d))
                        for h in range(2):
                            hh = HALVES[h]
                            dv_.did(stt(BDar[hh, :, 0, hh], half(kk, h), -1.0, half(e3, h), MUL, MUL))
                            dv_.did(tt(BDar[hh, :, 1, hh], half(r, h), half(e1, h), MUL))
                            dv_.did(tt(BDb[hh, :, hh], half(bb, h), half(e2, h), MUL))
                            dv_.did(tt(BDk[hh, :, hh], half(kd, h), half(e2, h), MUL), ("BD", d))
                        if d == 0:
                            P_(("S0", 1))
                            dv_.did(nc.vector.tensor_copy(S["s"][0][:, :], ps[:, 2, 0:P]))
                            dv_.did(nc.vector.tensor_copy(S_back[:, :], ps[:, 2, P:2 * P]), "S0")
                        mask = T_("mask_f" if d == 0 else "mask_b").rearrange("p (o n) -> p o n", o=1).to_broadcast([P, 2, 256])
                        for g, (c0, n) in enumerate(G2):
                            P_(("M", d, g))
                            for q, dst in enumerate((Mb, Mk)):
                                last = tt(dst[:, c0:c0 + 2, :, :].rearrange("p c q n -> p c (q n)"),
                                          ps[:, (6, 0)[g % 2] + q, :].rearrange("p (c n) -> p c n", c=2), mask, MUL)
                                dv_.did(last, ("M", d, g))
                        v_.wait_ge(dv_.sem, dv_.here(i))
                        lm = lambda l_, n: level[:, l_:l_ + 1, :].to_broadcast([P, n, P])
                        for g, (c0, n) in enumerate(G4):
                            dv_.did(tt(Q[:, c0:c0 + n, :], Mb[:, c0:c0 + n, 0, :], lm(0, n), MUL), ("Z", d, 0, g))
                        am = T_("amask_f" if d == 0 else "amask_b").rearrange("p (o n) -> p o n", o=1)
                        for g, (c0, n) in enumerate(G4):
                            P_(("A", d, g))
                            dv_.did(tt(Am[:, c0:c0 + n, :], ps[:, 3 + g, 0:n * P].rearrange("p (c n) -> p c n", c=n), am.to_broadcast([P, n, P]), MUL), ("A", d, g))
                        if d == 1:
                            dv_.did(nc.vector.tensor_copy(S["s"][0][:, :], S_back[:, :]))
                        v_.wait_ge(po_.sem, po_.now(("Q", d, 0), i))
                        for lv in range(1, LEVELS):
                            for g, (c0, n) in enumerate(G4):
                                P_(("Z", d, lv, g))
                                zz = ps[:, (6, 7, 0)[g], 0:n * P].rearrange("p (c n) -> p c n", c=n)
                                link(tt(TA[:, c0:c0 + n, :], zz, lm(lv, n), MUL))
                                dv_.did(tt(Q[:, c0:c0 + n, :], Q[:, c0:c0 + n, :], TA[:, c0:c0 + n, :], ADD), ("Qn", d, lv, g))
                        for g, (c0, n) in enumerate(G4):
                            P_(("TA", d, g))
                            dv_.did(nc.vector.tensor_copy(TA[:, c0:c0 + n, :].rearrange("p c n -> p (c n)"), ps[:, (6, 7, 0)[g], 0:n * P]), ("TA", d, g))
                        if d == 1:
                            P_(("stn", 0))
                        dv_.did(nc.vector.memset(S["p"][0][:, :], 0.0), ("Sinit", d))
                        A_(("TX", d, 2))
                        v_.wait_ge(dv_.sem, dv_.here(i))
                        for s, c0, c1 in SEQS:
                            order = range(c0, c1) if d == 0 else range(c1 - 1, c0 - 1, -1)
                            for n, c in enumerate(order):
                                cur, nxt = S[s][n % 2], S[s][(n + 1) % 2]
                                end = c * C + (C - 1 if d == 0 else 0)
                                pc = e1[:, end:end + 1]
                                link(ts(Sd[:, :], cur[:, :], pc, None, MUL))
                                P_(("U", d, s, n))
                                link(tt(U[n % 2][:, :], ps[:, 1, 0:P], TX[:, c, :], ADD), ("U", d, s, n))
                                P_(("S", d, s, n))
                                link(stt(nxt[:, :], ps[:, 2, 0:P], pc, Sd[:, :], MUL, ADD), ("S", d, s, n))
                                P_(("O", d, s, n))
                                for h in range(2):
                                    dst = o[HALVES[h], c * C:(c + 1) * C]
                                    src = ps[HALVES[h], 3 + n % 2, HALVES[h]]
                                    if d == 0:
                                        dv_.did(nc.vector.tensor_copy(dst, src), ("O", d, s, n))
                                    else:
                                        dv_.did(tt(dst, src, dst, ADD), ("O", d, s, n))
                        dv_.note(("o", d))
                        v_.wait_ge(dv_.sem, dv_.here(i))
                    dv_.did(tt(bon[:, :], kr[:, :], r[:, :], MUL), "bonus_in")
                    P_("mean")
                    link(stt(o[:, :], flat(0)[:, 0:T], -1.0 / 64, o[:, :], MUL, ADD), "oc")
                    P_("bonus")
                    link(tt(bon[:, :], flat(3)[:, 0:T], v[:, :], MUL))
                    P_("var")
                    link(ts(stat[:, :], flat(1)[:, 0:T], 1.0 / 64, GN_EPS, MUL, ADD), "varv")
                    A_("gstd")
                    link(nc.vector.reciprocal(stat[:, :], stat[:, :]))
                    link(tt(o[:, :], o[:, :], stat[:, :], MUL))
                    link(ts(o[:, :], o[:, :], pcl[:, 8:9], pcl[:, 9:10], MUL, ADD))
                    link(tt(o[:, :], o[:, :], bon[:, :], ADD))
                    v_.wait_ge(s_l["z"], i * 16 + 16)
                    v_.wait_ge(s_f, i + 1)
                    dv_.did(tt(yo[:, :], o[:, :], z[:, :], MUL), "y")


def rwkv(nc, A, G, M):
    with ExitStack() as st:
        for n in ("wlo", "alo"):
            G[n] = st.enter_context(nc.sbuf_tensor(n, [P, T], F32))
        with nc.sbuf_tensor("hT1", [P, KD, T], F32) as hT:
            load_norm(nc, A, G, M, 1, hT)
            rwkv_in(nc, A, G, M, hT)
        rwkv_scan(nc, A, G, M)


def program(nc, A, M):
    with ExitStack() as st:
        G = {}
        G["ps"] = st.enter_context(nc.psum_tensor("ps", [P, 8, 512], F32))
        for n, s in (("tab", [P, TAB_N]), ("col", [P, 4, P]), ("fcol", [HID, 4]),
                     ("scl", [P, 2, KD, 2]), ("shf", [P, 2, KD, 2])):
            G[n] = st.enter_context(nc.sbuf_tensor(n, s, F32))
        modulation(nc, A, G, M)
        with ExitStack() as s1:
            G["hid"] = s1.enter_context(nc.sbuf_tensor("hid", [HID, T], F32))
            filter_hidden(nc, A, G, M)
            with nc.sbuf_tensor("hT0", [P, KD, T], F32) as hT:
                load_norm(nc, A, G, M, 0, hT)
                hyena_in(nc, A, G, M, hT)
            hyena_conv(nc, A, G, M)
        out_proj(nc, A, G, M, 0, A["hy_w_out"])
        if STAGE == 1:
            return
        rwkv(nc, A, G, M)
        out_proj(nc, A, G, M, 1, A["rw_w_o"])


def constants():
    f = np.float32
    tab = np.zeros((P, TAB_N), np.float64)
    put = lambda n, a: tab.__setitem__((slice(0, a.shape[0]), slice(*TAB[n])), a)
    r = np.arange(P)
    row, c = r[:, None], r[None, :]
    same = row // 64 == c // 64
    put("ident", np.eye(P))
    put("heads", same.astype(f))
    put("mask_f", np.concatenate([same & (row < c), same & (row <= c)], 1).astype(f))
    put("mask_b", np.concatenate([same & (row > c), same & (row >= c)], 1).astype(f))
    put("amask_f", (same & (row > c)).astype(f))
    put("amask_b", (same & (row < c)).astype(f))
    put("level", np.concatenate([((row >> (l + 1)) == (c >> (l + 1))) & ((row >> l) != (c >> l)) for l in range(LEVELS)], 1).astype(f))
    put("chunk", np.tile((np.arange(T) % C != 0).astype(f), (P, 1)))

    def order(L):
        return np.concatenate([np.arange(0, L, 2), np.arange(1, L, 2)]) if L == LS else np.arange(L)

    feats, decay = [], []
    lo, hi = np.log(1e-2) / 1.5, np.log(1e-2) / 0.3
    deltas = np.abs(np.linspace(lo, hi, E))
    for L in (LS, LP):
        pos = order(L).astype(np.float64)[:, None]
        t = pos / (L - 1)
        ang = (2 * np.pi / L) * pos * np.linspace(1e-4, 15, 16)[None, :]
        feats.append(np.concatenate([t, np.cos(ang), -np.sin(ang)], 1).T)
        decay.append(np.exp(-t * deltas))
    put("feats", np.concatenate(feats, 1))
    dft = np.zeros((P, DFT_N), np.float64)
    k = np.arange(LS // 2)
    i = np.arange(LS // 2)
    fwd, inv = [], []
    for fn in (np.cos, np.sin):
        for par in range(2):
            m = fn(np.pi * (2 * k[None, :] + 1) * (2 * i[:, None] + par) / (2 * LS))
            fwd.append(m.reshape(2, P, 256).transpose(1, 0, 2).reshape(P, 512))
            inv.append((m.T / LS).reshape(2, P, 256).transpose(1, 0, 2).reshape(P, 512))
    dft[:, slice(*DFT["fwd"])] = np.concatenate(fwd, 1)
    dft[:, slice(*DFT["inv"])] = np.concatenate(inv, 1)
    k = np.arange(LP)
    mp = [fn(np.pi * (2 * k[None, :] + 1) * k[:, None] / (2 * LP)) for fn in (np.cos, np.sin)]
    dft[:, slice(*DFT["fwdp"])] = np.concatenate(mp, 1)
    dft[:, slice(*DFT["invp"])] = np.concatenate([m.T / LP for m in mp], 1)
    return {"tab": tab.astype(f), "dft": dft.astype(f), "decay": np.concatenate(decay, 0).astype(f)}


STAGE = 2
SCRATCH = {"vx_d": [2, T, E], "g_d": [E, T], "y_d": [E, T], "x1_d": [T, D], "gate_d": [2, 2, D], "rkvz_d": [4, E, T]}
OUTS = {"y_prompt": [1, LP, D], "y_sample": [1, LS, D], "new_state_fwd": [1, 1, 32, 64, 64], "new_state_bwd": [1, 1, 32, 64, 64]}


def build(nc, shapes, marks, debug=()):
    A = {n: nc.dram_tensor(f"in_{n}", list(s), F32, kind="ExternalInput").ap() for n, s in shapes.items()}
    for n, s in SCRATCH.items():
        A[n] = nc.dram_tensor(f"scratch_{n}", s, F32, kind="ExternalOutput" if n in debug else "Internal").ap()
    for n, s in OUTS.items():
        A[n] = nc.dram_tensor(f"out_{n}", s, F32, kind="ExternalOutput").ap()
    program(nc, A, marks)


def kernel(**inputs):
    import concourse.bacc as bacc
    from concourse.bass_utils import run_bass_kernel_spmd

    arrays = {n: np.ascontiguousarray(a) for n, a in inputs.items()}
    arrays.update(constants())
    shapes = {n: a.shape for n, a in arrays.items()}
    marks = {}
    build(bacc.Bacc("TRN2", target_bir_lowering=False, num_devices=1), shapes, marks)
    marks["counted"] = True
    nc = bacc.Bacc("TRN2", target_bir_lowering=False, num_devices=1)
    build(nc, shapes, marks)
    r = run_bass_kernel_spmd(nc, [{f"in_{n}": a for n, a in arrays.items()}], core_ids=[0]).results[0]
    return tuple(r[f"out_{n}"] for n in OUTS)
```

```python
import concourse.bass as bass
from concourse import mybir
from contextlib import ExitStack
import numpy as np

F32 = mybir.dt.float32
ALU = mybir.AluOpType
ACT = mybir.ActivationFunctionType
MUL, ADD, SUB = ALU.mult, ALU.add, ALU.subtract

P = 128
D = 1024
E = 2048
LS, LP = 512, 128
T = LS + LP
NT = T // P
KD = D // P
KE = E // P
GRID = 64
ROWS = LS // GRID
HID = 64
EMB = 33
C = 64
NC = T // C
CS = LS // C
LEVELS = 6
CB = 512
NB = E // CB
EPS = 1e-6
GN_EPS = 64e-5
DECAY_MAX = float(np.exp(-0.5))

TAB = {}
_at = 0
for _name, _n in (("ident", P), ("heads", P), ("mk_f", 2 * P), ("mk_b", 2 * P),
                  ("between", LEVELS * P), ("chosen", LEVELS * P), ("chunk", T)):
    TAB[_name] = (_at, _at + _n)
    _at += _n
TAB_N = _at
DFT = {}
_at = 0
for _name, _n in (("fwd", 4 * 2 * 256), ("inv", 4 * 2 * 256), ("fwdp", 2 * P), ("invp", 2 * P)):
    DFT[_name] = (_at, _at + _n)
    _at += _n
DFT_N = _at


class Steps:

    def __init__(self, nc, stack, name, marks, by=1):
        self.sem = stack.enter_context(nc.semaphore(name))
        self.name, self.marks, self.n, self.by = name, marks, 0, by

    def note(self, label):
        if not self.marks.get("counted"):
            self.marks[self.name, label] = self.n

    def per(self):
        return self.marks.get((self.name, "round"), 0)

    def did(self, ins, label=None):
        ins.then_inc(self.sem, self.by)
        self.n += self.by
        if not self.marks.get("counted"):
            self.marks[self.name, "round"] = max(self.n, self.per())
            if label is not None:
                self.marks[self.name, label] = self.n
        return ins

    def mark(self, label):
        return self.marks.get((self.name, label), 0)

    def now(self, label, i=None):
        return self.mark(label) if i is None else i * self.per() + (self.per() + self.mark(label))

    def before(self, label, i):
        return i * self.per() + self.mark(label)

    def here(self, i=None):
        return self.n if i is None else i * self.per() + (self.per() + self.n)

    def start(self, eng):
        if self.per():
            eng.sem_inc(self.sem, self.per())


def make_ops(nc):
    def mm(out, lhsT, rhs, first=True, last=True):
        return nc.tensor.matmul(out, lhsT, rhs, start=first, stop=last)

    def stt(out, in0, scalar, in1, op0, op1):
        return nc.vector.scalar_tensor_tensor(out=out, in0=in0, scalar=scalar, in1=in1, op0=op0, op1=op1)

    def ts(out, in0, s1, s2, op0, op1=None):
        if op1 is None:
            return nc.vector.tensor_scalar(out, in0, s1, None, op0)
        return nc.vector.tensor_scalar(out, in0, s1, s2, op0, op1)

    def tt(out, a, b, op):
        return nc.vector.tensor_tensor(out, a, b, op)

    def act(out, in_, f, **kw):
        return nc.scalar.activation(out, in_, f, **kw)

    return mm, stt, ts, tt, act


def modulation(nc, A, G, M):
    mm, stt, ts, tt, act = make_ops(nc)
    ps, tab, col = G["ps"], G["tab"], G["col"]
    with ExitStack() as st:
        sb = lambda n, s: st.enter_context(nc.sbuf_tensor(n, s, F32))
        crow, csig, condT = sb("crow", [16, P]), sb("csig", [16, P]), sb("condT", [P, 16])
        rows = sb("vrows", [P, 4, P])
        frow = sb("frow", [4, HID])
        RING = 3
        aw = sb("aw", [P, RING, 3 * D])
        mrow = sb("mrow", [2, 2, 3 * D])
        abrow = sb("abrow", [2, 2, 3 * D])
        prow = sb("prow", [2, 2, D])
        s_small = st.enter_context(nc.semaphore("mod_vectors_loaded"))
        s_tab = st.enter_context(nc.semaphore("mod_tables_loaded"))
        s_aw = [st.enter_context(nc.semaphore(f"mod_weights_{k}")) for k in range(RING)]
        s_out = st.enter_context(nc.semaphore("mod_gate_stored"))
        pe_, ac_, dv_ = (Steps(nc, st, f"mod_{n}", M) for n in ("pe", "act", "dve"))
        nload = [0]

        with nc.Block() as block:
            @block.sync
            def _(sp):
                def small(dst, src):
                    sp.dma_start(dst, src).then_inc(s_small, 16)
                    nload[0] += 16
                nload[0] = 0
                sp.dma_start(tab[:, :], A["tab"]).then_inc(s_tab, 16)
                small(crow[0:8, :], A["c"].rearrange("a (k p) -> (a k) p", p=P))
                small(crow[8:16, :], A["c_ctx"].rearrange("(k p) -> k p", p=P))
                at = 0
                for a, n in ((A["norm_pre"].rearrange("l (k p) -> (l k) p", p=P), 16),
                             (A["hy_b_in"].rearrange("l (k p) -> (l k) p", p=P), 64),
                             (A["rw_mu"].rearrange("l m (k p) -> (l m k) p", p=P), 48),
                             (A["hy_conv_w"].rearrange("l j (k p) -> (l j k) p", p=P)[0:96, :], 96),
                             (None, 32),
                             (A["hy_conv_w"].rearrange("l j (k p) -> (l j k) p", p=P)[96:144, :], 48),
                             (A["hy_conv_b"].rearrange("l (k p) -> (l k) p", p=P), 48),
                             (A["rw_w0"].rearrange("l z (k p) -> (l z k) p", p=P), 32),
                             (A["rw_a0"].rearrange("l z (k p) -> (l z k) p", p=P), 32),
                             (A["rw_k_k"].rearrange("l (k p) -> (l k) p", p=P), 16),
                             (A["rw_k_a"].rearrange("l (k p) -> (l k) p", p=P), 16),
                             (A["rw_r_k"].rearrange("l z (k h) n -> (l z k) (h n)", h=2), 32),
                             (A["rw_gn_w"].rearrange("l (k p) -> (l k) p", p=P), 16),
                             (A["rw_gn_b"].rearrange("l (k p) -> (l k) p", p=P), 16)):
                    g, r = at // P, at % P
                    if a is not None:
                        small(rows[r:r + n, g, :], a)
                    else:
                        small(rows[r:r + n, g, :], A["hy_conv_b"].rearrange("l (k p) -> (l k) p", p=P)[0:n, :])
                    at += n
                for k, n in enumerate(("hy_f_b1", "hy_f_b2", "hy_f_b3", "hy_f_freq")):
                    small(frow[k:k + 1, :], A[n])
                for l in range(2):
                    for c in range(2):
                        small(abrow[c:c + 1, l, :], A["ada_b"][l:l + 1, :])
                        small(prow[c:c + 1, l, :], A["norm_post"][l:l + 1, :])
                for n in range(2 * KD):
                    l, k = n // KD, n % KD
                    if n >= RING:
                        sp.wait_ge(pe_.sem, pe_.now(("ada", n - RING)))
                    sp.dma_start(aw[:, n % RING, :], A["ada_w"][l, k * P:(k + 1) * P, :]).then_inc(s_aw[n % RING], 16)
                for l in range(2):
                    sp.wait_ge(dv_.sem, dv_.now(("gate", l)))
                    sp.dma_start(A["gate_d"][l], mrow[:, l, 2 * D:3 * D]).then_inc(s_out, 16)
                sp.wait_ge(s_out, 32)

            @block.scalar
            def _(a):
                a.wait_ge(s_small, nload[0])
                ac_.did(act(csig[:, :], crow[:, :], ACT.Sigmoid), "csig")

            @block.tensor
            def _(pe):
                pe.wait_ge(s_tab, 16)
                pe.wait_ge(s_small, nload[0])
                ident = tab[:, TAB["ident"][0]:TAB["ident"][1]]
                for g in range(4):
                    last = nc.tensor.transpose(ps[:, 6, g * P:(g + 1) * P], rows[:, g, :], ident)
                pe_.did(last, "cols")
                last = nc.tensor.transpose(ps[0:HID, 7, 0:4], frow[:, :], ident[0:4, 0:4])
                pe_.did(last, "fcols")
                pe.wait_ge(dv_.sem, dv_.now("fcols"))
                pe_.did(nc.tensor.transpose(ps[:, 7, 16:32], crow[:, :], ident[0:16, 0:16]), "condT")
                pe.wait_ge(dv_.sem, dv_.now("condT"))
                for l in range(2):
                    if l:
                        pe.wait_ge(dv_.sem, dv_.now(("row", l - 1)))
                    for k in range(KD):
                        n = l * KD + k
                        pe.wait_ge(s_aw[n % RING], 16 * (n // RING + 1))
                        for b in range(6):
                            last = mm(ps[0:2, b, :], condT[:, k:16:KD], aw[:, n % RING, b * 512:(b + 1) * 512], k == 0, k == KD - 1)
                        pe_.did(last, ("ada", n))
                    pe.wait_ge(dv_.sem, dv_.now(("row", l)))
                    if l:
                        pe.wait_ge(dv_.sem, dv_.now(("mcols", l - 1)))
                    for j in range(16):
                        last = nc.tensor.transpose(ps[:, 7, 64 + 2 * j:66 + 2 * j], mrow[:, l, j * P:(j + 1) * P], ident[0:2, 0:2])
                    pe_.did(last, ("mcols", l))

            @block.vector
            def _(v):
                def link(ins, label=None):
                    dv_.did(ins, label)
                    v.wait_ge(dv_.sem, dv_.here())
                v.wait_ge(ac_.sem, ac_.now("csig"))
                dv_.did(tt(crow[:, :], crow[:, :], csig[:, :], MUL), "silu")
                v.wait_ge(pe_.sem, pe_.now("cols"))
                dv_.did(nc.vector.tensor_copy(col[:, :, :], ps[:, 6, :].rearrange("p (g n) -> p g n", g=4)), "cols")
                v.wait_ge(pe_.sem, pe_.now("fcols"))
                dv_.did(nc.vector.tensor_copy(G["fcol"][:, :], ps[0:HID, 7, 0:4]), "fcols")
                v.wait_ge(pe_.sem, pe_.now("condT"))
                link(nc.vector.tensor_copy(condT[:, :], ps[:, 7, 16:32]), "condT")
                npre = col[:, 0, 0:16].rearrange("p (l k) -> p l k", l=2)
                for l in range(2):
                    v.wait_ge(pe_.sem, pe_.now(("ada", l * KD + KD - 1)))
                    link(tt(mrow[:, l, :], ps[0:2, 0:6, :].rearrange("p b n -> p (b n)"), abrow[:, l, :], ADD), ("row", l))
                    dv_.did(tt(mrow[:, l, 2 * D:3 * D], mrow[:, l, 2 * D:3 * D], prow[:, l, :], MUL), ("gate", l))
                    v.wait_ge(pe_.sem, pe_.now(("mcols", l)))
                    mc = ps[:, 7, 64:96].rearrange("p (j c) -> p j c", c=2)
                    dv_.did(nc.vector.tensor_copy(G["shf"][:, l, :, :], mc[:, 0:8, :]))
                    for c in range(2):
                        last = dv_.did(stt(G["scl"][:, l, :, c], mc[:, 8:16, c], 1.0, npre[:, l, :], ADD, MUL), ("mcols", l))


def load_norm(nc, A, G, M, l, hT):
    mm, stt, ts, tt, act = make_ops(nc)
    ps, tab = G["ps"], G["tab"]
    with ExitStack() as st:
        sb = lambda n, s: st.enter_context(nc.sbuf_tensor(f"{n}{l}", s, F32))
        x, sq, ss, rs = sb("nx", [P, NT, D]), sb("nsq", [P, D]), sb("nss", [P, NT]), sb("nrs", [P, NT])
        sx = [st.enter_context(nc.semaphore(f"norm{l}_x{j}")) for j in range(NT)]
        pe_, ac_, dv_ = (Steps(nc, st, f"norm{l}_{n}", M) for n in ("pe", "act", "dve"))
        with nc.Block() as block:
            @block.sync
            def _(sp):
                for j in range(NT):
                    src = A["x1_d"][j * P:(j + 1) * P, :] if l else (A["x_sample"][0, j * P:(j + 1) * P, :] if j < 4 else A["x_prompt"][0, :, :])
                    sp.dma_start(x[:, j, :], src).then_inc(sx[j], 16)

            @block.scalar
            def _(a):
                for j in range(NT):
                    a.wait_ge(sx[j], 16)
                    if j:
                        a.wait_ge(ac_.sem, ac_.here())
                    ac_.did(act(sq[:, :], x[:, j, :], ACT.Square, accum_out=ss[:, j:j + 1]), ("ss", j))
                a.wait_ge(dv_.sem, dv_.now("var"))
                ac_.did(act(rs[:, :], ss[:, :], ACT.Sqrt), "std")
                for k in range(KD):
                    a.wait_ge(pe_.sem, pe_.now(("tr", k)))
                    kw = lambda c: dict(scale=G["scl"][:, l, k, c:c + 1], bias=G["shf"][:, l, k, c:c + 1])
                    act(hT[:, k, 0:LS], ps[:, 2 * (k % 2), :], ACT.Identity, **kw(0))
                    ac_.did(act(hT[:, k, LS:T], ps[:, 2 * (k % 2) + 1, 0:LP], ACT.Identity, **kw(1)), ("h", k))

            @block.vector
            def _(v):
                def link(ins, label=None):
                    dv_.did(ins, label)
                    v.wait_ge(dv_.sem, dv_.here())
                v.wait_ge(ac_.sem, ac_.now(("ss", NT - 1)))
                dv_.did(ts(ss[:, :], ss[:, :], 1.0 / D, EPS, MUL, ADD), "var")
                v.wait_ge(ac_.sem, ac_.now("std"))
                link(nc.vector.reciprocal(rs[:, :], rs[:, :]))
                for j in range(NT):
                    dv_.did(ts(x[:, j, :], x[:, j, :], rs[:, j:j + 1], None, MUL), ("xn", j))

            @block.tensor
            def _(pe):
                ident = tab[:, TAB["ident"][0]:TAB["ident"][1]]
                pe.wait_ge(dv_.sem, dv_.now(("xn", NT - 1)))
                for k in range(KD):
                    if k >= 2:
                        pe.wait_ge(ac_.sem, ac_.now(("h", k - 2)))
                    for j in range(NT):
                        last = nc.tensor.transpose(ps[:, 2 * (k % 2) + j // 4, (j % 4) * P:(j % 4 + 1) * P], x[:, j, k * P:(k + 1) * P], ident)
                    pe_.did(last, ("tr", k))


def filter_hidden(nc, A, G, M):
    mm, stt, ts, tt, act = make_ops(nc)
    ps, tab, fcol, hid = G["ps"], G["tab"], G["fcol"], G["hid"]
    ROUND = 1.5 * 2 ** 23
    HI = 6.28125
    LO = 2 * np.pi - HI
    with ExitStack() as st:
        sb = lambda n, s: st.enter_context(nc.sbuf_tensor(n, s, F32))
        w = [sb("fw1", [EMB, HID]), sb("fw2", [HID, HID]), sb("fw3", [HID, HID])]
        feats = sb("feats", [EMB, T])
        arg, turn = sb("farg", [HID, T]), sb("fturn", [HID, T])
        s_w = st.enter_context(nc.semaphore("filter_weights_loaded"))
        pe_, ac_, dv_ = (Steps(nc, st, f"filter_{n}", M) for n in ("pe", "act", "dve"))
        psv = ps[0:HID, 0:2, :].rearrange("p b n -> p (b n)")
        with nc.Block() as block:
            @block.sync
            def _(sp):
                for k in range(3):
                    sp.dma_start(w[k][:, :], A[f"hy_f_w{k + 1}"][0]).then_inc(s_w, 16)
                sp.dma_start(feats[:, :], A["feats"]).then_inc(s_w, 16)

            @block.tensor
            def _(pe):
                pe.wait_ge(s_w, 64)
                for k in range(3):
                    src = feats[:, :] if k == 0 else hid[:, :]
                    if k:
                        pe.wait_ge(ac_.sem, ac_.now(("sin", k - 1)))
                    mm(psv[:, 0:LS], w[k][:, :], src[:, 0:LS])
                    pe_.did(mm(psv[:, LS:T], w[k][:, :], src[:, LS:T]), ("mm", k))

            @block.vector
            def _(v):
                def link(ins, label=None):
                    dv_.did(ins, label)
                    v.wait_ge(dv_.sem, dv_.here())
                for k in range(3):
                    v.wait_ge(pe_.sem, pe_.now(("mm", k)))
                    if k:
                        v.wait_ge(ac_.sem, ac_.now(("sin", k - 1)))
                    link(ts(arg[:, :], psv[:, 0:T], fcol[:, k:k + 1], fcol[:, 3:4], ADD, MUL))
                    link(ts(turn[:, :], arg[:, :], 1 / (2 * np.pi), ROUND, MUL, ADD))
                    link(ts(turn[:, :], turn[:, :], ROUND, None, SUB))
                    link(stt(arg[:, :], turn[:, :], -HI, arg[:, :], MUL, ADD))
                    link(stt(arg[:, :], turn[:, :], -LO, arg[:, :], MUL, ADD))
                    link(ts(arg[:, :], arg[:, :], 3.1415925, -3.1415925, ALU.min, ALU.max), ("arg", k))

            @block.scalar
            def _(a):
                for k in range(3):
                    a.wait_ge(dv_.sem, dv_.now(("arg", k)))
                    ac_.did(act(hid[:, :], arg[:, :], ACT.Sin), ("sin", k))


def hyena_in(nc, A, G, M, hT):
    mm, stt, ts, tt, act = make_ops(nc)
    ps, tab, col = G["ps"], G["tab"], G["col"]
    w_v = A["hy_w_in"][0].rearrange("(k p) n -> p k n", p=P)
    pair = [ps[:, 2 * q:2 * q + 2, :].rearrange("p b n -> p (b n)") for q in range(4)]
    with ExitStack() as st:
        sb = lambda n, s: st.enter_context(nc.sbuf_tensor(n, s, F32))
        w = [sb(f"hw{s}", [P, KD, P]) for s in range(4)]
        PADN = LS + LP + 3
        pad = [sb(f"hpad{s}", [P, PADN]) for s in range(3)]
        cv = [sb(f"hcv{s}", [P, T + 1]) for s in range(3)]
        out_t = [sb(f"hot{s}", [P, NT, P]) for s in range(2)]
        zsig, z, g = sb("hzs", [P, T]), sb("hz", [P, T]), sb("hg", [P, T])
        pc = sb("hpc", [P, 16])
        s_w = [st.enter_context(nc.semaphore(f"hy_weights_{s}")) for s in range(4)]
        s_o = [st.enter_context(nc.semaphore(f"hy_stored_{s}")) for s in range(3)]
        s_f = [st.enter_context(nc.semaphore(f"hy_store_buffer_free_{s}")) for s in range(3)]
        s_z = st.enter_context(nc.semaphore("hy_pad_cleared"))
        pe_, ac_, dv_ = (Steps(nc, st, f"hyin_{n}", M) for n in ("pe", "act", "dve"))
        with nc.Block() as block:
            @block.sync
            def _(sp):
                with sp.Fori(0, KE) as i:
                    for s in range(4):
                        sp.wait_ge(pe_.sem, pe_.before(("proj", s), i))
                        sp.dma_start(w[s][:, :, :], w_v[:, :, bass.ds(i * P + s * E, P)]).then_inc(s_w[s], 16)

            @block.gpsimd
            def _(po):
                for s in range(3):
                    nc.gpsimd.memset(pad[s][:, :], 0.0).then_inc(s_z, 1)
                    po.sem_inc(s_f[s], 1)
                with po.Fori(0, KE) as i:
                    for s in range(2):
                        po.wait_ge(ac_.sem, ac_.now(("vt", s), i))
                        po.dma_start(A["vx_d"][s].rearrange("(j p) n -> p j n", p=P)[:, :, bass.ds(i * P, P)], out_t[s][:, :, :]).then_inc(s_o[s], 16)
                    po.wait_ge(dv_.sem, dv_.now("g", i))
                    po.dma_start(A["g_d"][bass.ds(i * P, P), :], g[:, :]).then_inc(s_o[2], 16)
                    for s in range(3):
                        po.wait_ge(s_o[s], i * 16 + 16)
                        po.sem_inc(s_f[s], 1)
                for s in range(3):
                    po.wait_ge(s_o[s], 16 * KE)

            @block.tensor
            def _(pe):
                ident = tab[:, TAB["ident"][0]:TAB["ident"][1]]
                pe_.start(pe)

                def transpose(s, i):
                    pe.wait_ge(dv_.sem, dv_.now(("conv", s), i))
                    pe.wait_ge(ac_.sem, ac_.before(("vt", s), i))
                    for j in range(NT):
                        src = cv[s][:, j // 2 + 2 * P * (j % 2):min(j // 2 + 2 * P * (j % 2) + 2 * P, LS):2] if j < 4 else cv[s][:, LS + 1:T + 1]
                        last = nc.tensor.transpose(pair[2 + s][:, j * P:(j + 1) * P], src, ident)
                    pe_.did(last, ("tr", s))

                with pe.Fori(0, KE) as i:
                    for s in range(4):
                        pe.wait_ge(s_w[s], i * 16 + 16)
                        if s >= 2:
                            pe.wait_ge(ac_.sem, ac_.now(("pad", s - 2), i))
                        elif s == 0:
                            pe.wait_ge(ac_.sem, ac_.before(("pad", 2), i))
                        else:
                            pe.wait_ge(dv_.sem, dv_.before("z", i))
                        for k in range(KD):
                            mm(pair[s % 2][:, 0:LS], w[s][:, k, :], hT[:, k, 0:LS], k == 0, k == KD - 1)
                            last = mm(pair[s % 2][:, LS:T], w[s][:, k, :], hT[:, k, LS:T], k == 0, k == KD - 1)
                        pe_.did(last, ("proj", s))
                        if s in (1, 2):
                            transpose(s - 1, i)

            @block.scalar
            def _(a):
                ac_.start(a)
                a.wait_ge(s_z, 3)
                with a.Fori(0, KE) as i:
                    def to_pad(s):
                        a.wait_ge(pe_.sem, pe_.now(("proj", s), i))
                        a.wait_ge(dv_.sem, dv_.before(("conv", s), i))
                        act(pad[s][:, 1:LS + 1], pair[s % 2][:, 0:LS], ACT.Identity, bias=pc[:, s:s + 1])
                        ac_.did(act(pad[s][:, LS + 2:T + 2], pair[s % 2][:, LS:T], ACT.Identity, bias=pc[:, s:s + 1]), ("pad", s))

                    def turned(s):
                        a.wait_ge(pe_.sem, pe_.now(("tr", s), i))
                        a.wait_ge(s_f[s], i + 1)
                        ac_.did(act(out_t[s][:, :, :].rearrange("p j n -> p (j n)"), pair[2 + s][:, 0:T], ACT.Copy), ("vt", s))

                    a.wait_ge(dv_.sem, dv_.now("pc", i))
                    to_pad(0)
                    to_pad(1)
                    turned(0)
                    to_pad(2)
                    turned(1)
                    a.wait_ge(pe_.sem, pe_.now(("proj", 3), i))
                    a.wait_ge(dv_.sem, dv_.before("z", i))
                    ac_.did(act(zsig[:, :], pair[1][:, 0:T], ACT.Sigmoid, bias=pc[:, 3:4]), "zs")

            @block.vector
            def _(v):
                dv_.start(v)
                bin_c = col[:, 0, 16:80].rearrange("p (s k) -> p s k", s=4)
                cw01 = col[:, 1, 0:96].rearrange("p (j k) -> p j k", k=KE)
                cwb = col[:, 2, 0:96].rearrange("p (j k) -> p j k", k=KE)
                with v.Fori(0, KE) as i:
                    def link(ins, label=None):
                        dv_.did(ins, label)
                        v.wait_ge(dv_.sem, dv_.here(i))
                    v.wait_ge(ac_.sem, ac_.before("zs", i))
                    nc.vector.tensor_copy(pc[:, 0:4], bin_c[:, :, bass.ds(i, 1)].rearrange("p s o -> p (s o)"))
                    nc.vector.tensor_copy(pc[:, 4:10], cw01[:, :, bass.ds(i, 1)].rearrange("p s o -> p (s o)"))
                    link(nc.vector.tensor_copy(pc[:, 10:16], cwb[:, :, bass.ds(i, 1)].rearrange("p s o -> p (s o)")), "pc")
                    for s in range(3):
                        v.wait_ge(ac_.sem, ac_.now(("pad", s), i))
                        if s < 2:
                            v.wait_ge(pe_.sem, pe_.before(("tr", s), i))
                        link(ts(cv[s][:, :], pad[s][:, 1:T + 2], pc[:, 7 + s:8 + s], pc[:, 13 + s:14 + s], MUL, ADD))
                        link(stt(cv[s][:, :], pad[s][:, 0:T + 1], pc[:, 4 + s:5 + s], cv[s][:, :], MUL, ADD))
                        link(stt(cv[s][:, :], pad[s][:, 2:T + 3], pc[:, 10 + s:11 + s], cv[s][:, :], MUL, ADD), ("conv", s))
                    v.wait_ge(ac_.sem, ac_.now("zs", i))
                    link(stt(z[:, :], pair[1][:, 0:T], pc[:, 3:4], zsig[:, :], ADD, MUL), "z")
                    v.wait_ge(s_f[2], i + 1)
                    dv_.did(tt(g[:, 0:LS], z[:, 0:LS], cv[2][:, 0:LS], MUL))
                    dv_.did(tt(g[:, LS:T], z[:, LS:T], cv[2][:, LS + 1:T + 1], MUL), "g")


def hyena_conv(nc, A, G, M):
    mm, stt, ts, tt, act = make_ops(nc)
    ps, hid = G["ps"], G["hid"]
    pair = [ps[:, 2 * q:2 * q + 2, :] for q in range(4)]
    w4_v = A["hy_f_w4"][0].rearrange("k (g n) -> k g n", g=4)
    JOBS = [("filt", 0, j) for j in range(NT)] + [("fix", 0)] + [("H", 0, q) for q in range(5)] + [("X", 0, q) for q in range(5)] \
        + [("filt", 1, j) for j in range(NT)] + [("fix", 1)] + [("inv", 0, q) for q in range(3)] \
        + [("H", 1, q) for q in range(5)] + [("X", 1, q) for q in range(5)] + [("inv", 1, q) for q in range(4)]
    slot = {job: n % 4 for n, job in enumerate(JOBS)}
    with ExitStack() as st:
        sb = lambda n, s: st.enter_context(nc.sbuf_tensor(n, s, F32))
        dft = sb("dft", [P, DFT_N])
        vx = [sb("cv_v", [P, NT, CB]), sb("cv_x1", [P, NT, CB])]
        w4 = sb("w4", [HID, 4, CB])
        wsd = sb("wsd", [HID, 2, CB])
        dec = sb("dec", [P, NT, CB])
        bias = sb("fbias", [1, 2, CB])
        g = sb("cg", [P, 4, T])
        hsd = sb("hsd", [P, 2, NT, CB])
        H = sb("H", [P, 2, NT, CB])
        X = sb("X", [P, 2, NT, CB])
        Y = sb("Y", [P, 2, NT, CB])
        tmp = sb("ctmp", [P, NT, CB])
        osave = sb("osave", [P, 2, CB])
        yout = sb("yout", [P, 4, T])
        fwd = dft[:, DFT["fwd"][0]:DFT["fwd"][1]].rearrange("p (m t k) -> p m t k", m=4, t=2)
        inv = dft[:, DFT["inv"][0]:DFT["inv"][1]].rearrange("p (m k t) -> p m k t", m=4, k=2)
        fwdp = dft[:, DFT["fwdp"][0]:DFT["fwdp"][1]].rearrange("p (m k) -> p m k", m=2)
        invp = dft[:, DFT["invp"][0]:DFT["invp"][1]].rearrange("p (m t) -> p m t", m=2)
        loads = ("v", "x1", "w4", "dec", "bias", "g")
        s_l = {n: st.enter_context(nc.semaphore(f"conv_loaded_{n}")) for n in loads}
        s_dft = st.enter_context(nc.semaphore("conv_dft_loaded"))
        s_y = st.enter_context(nc.semaphore("conv_stored"))
        s_f = st.enter_context(nc.semaphore("conv_store_buffer_free"))
        pe_, ac_, dv_ = (Steps(nc, st, f"conv_{n}", M) for n in ("pe", "act", "dve"))

        with nc.Block() as block:
            @block.sync
            def _(sp):
                sp.dma_start(dft[:, :], A["dft"]).then_inc(s_dft, 16)
                with sp.Fori(0, NB) as i:
                    cs = bass.ds(i * CB, CB)
                    sp.wait_ge(pe_.sem, pe_.before(("fix", 1), i))
                    sp.wait_ge(dv_.sem, dv_.before(("w", 1), i))
                    sp.dma_start(w4[:, :, :], w4_v[:, :, cs]).then_inc(s_l["w4"], 16)
                    sp.wait_ge(dv_.sem, dv_.before(("ev", ("filt", 1, NT - 1)), i))
                    sp.dma_start(dec[:, :, :], A["decay"].rearrange("(j p) n -> p j n", p=P)[:, :, cs]).then_inc(s_l["dec"], 16)
                    sp.wait_ge(dv_.sem, dv_.before(("ev", ("fix", 1)), i))
                    sp.dma_start(bias[:, :, :], A["hy_fft_bias"][:, :, cs]).then_inc(s_l["bias"], 16)
                    sp.wait_ge(pe_.sem, pe_.before(("X", 1, 4), i))
                    for s, n in ((0, "v"), (1, "x1")):
                        sp.dma_start(vx[s][:, :, :], A["vx_d"][s].rearrange("(j p) n -> p j n", p=P)[:, :, cs]).then_inc(s_l[n], 16)
                    sp.wait_ge(dv_.sem, dv_.before(("ev", ("inv", 1, 3)), i))
                    sp.dma_start(g[:, :, :], A["g_d"][cs, :].rearrange("(c p) t -> p c t", p=P)).then_inc(s_l["g"], 16)

            @block.gpsimd
            def _(po):
                po.sem_inc(s_f, 1)
                with po.Fori(0, NB) as i:
                    po.wait_ge(dv_.sem, dv_.now(("ev", ("inv", 1, 3)), i))
                    po.dma_start(A["y_d"][bass.ds(i * CB, CB), :].rearrange("(c p) t -> p c t", p=P), yout[:, :, :]).then_inc(s_y, 16)
                    po.wait_ge(s_y, i * 16 + 16)
                    po.sem_inc(s_f, 1)
                po.wait_ge(s_y, 16 * NB)

            @block.tensor
            def _(pe):
                pe_.start(pe)
                pe.wait_ge(s_dft, 16)
                with pe.Fori(0, NB) as i:
                    for n, job in enumerate(JOBS):
                        if n >= 4:
                            pe.wait_ge(dv_.sem, dv_.now(("ev", JOBS[n - 4]), i))
                        else:
                            last_user = max(m for m in range(len(JOBS)) if m % 4 == n)
                            pe.wait_ge(dv_.sem, dv_.before(("ev", JOBS[last_user]), i))
                        q = pair[slot[job]]
                        kind, o = job[0], job[1]
                        if kind == "filt":
                            j = job[2]
                            if j == 0:
                                pe.wait_ge(dv_.sem, dv_.now(("w", o), i))
                            mm(q[:, 0, :], hid[:, j * P:(j + 1) * P], wsd[:, 0, :])
                            last = mm(q[:, 1, :], hid[:, j * P:(j + 1) * P], wsd[:, 1, :])
                        elif kind == "fix":
                            last = mm(q[:, 0, :], hid[:, 0:P], w4[:, 2 + o, :])
                        elif kind in ("H", "X"):
                            m = job[2]
                            if kind == "H":
                                src = [hsd[:, 0, :, :], hsd[:, 1, :, :]]
                                pe.wait_ge(dv_.sem, dv_.now(("row0", o), i))
                            elif o == 0:
                                src = [vx[0][:, :, :]] * 2
                                if m == 0:
                                    pe.wait_ge(s_l["v"], i * 16 + 16)
                            else:
                                src = [vx[0][:, :, :]] * 2
                                pe.wait_ge(dv_.sem, dv_.now(("ev", ("inv", 0, 2)), i))
                            if m < 4:
                                cs, kt = m // 2, m % 2
                                for par in range(2):
                                    for t in range(2):
                                        last = mm(q[:, par, :], fwd[:, 2 * cs + par, t, kt * P:(kt + 1) * P], src[cs][:, 2 * par + t, :], t == 0, t == 1)
                            else:
                                for cs in range(2):
                                    last = mm(q[:, cs, :], fwdp[:, cs, :], src[cs][:, 4, :])
                        elif o == 0:
                            m = job[2]
                            pe.wait_ge(dv_.sem, dv_.now(("comb", 0), i))
                            if m < 2:
                                for h in range(2):
                                    for kt in range(2):
                                        for cs in range(2):
                                            last = mm(q[:, h, :], inv[:, 2 * cs + m, kt, h * P:(h + 1) * P], X[:, cs, 2 * m + kt, :], kt + cs == 0, kt + cs == 2)
                            else:
                                for cs in range(2):
                                    last = mm(q[:, 0, :], invp[:, cs, :], Y[:, cs, 4, :], cs == 0, cs == 1)
                        else:
                            c4 = job[2]
                            ch = slice(c4 * P, (c4 + 1) * P)
                            pe.wait_ge(dv_.sem, dv_.now(("comb", 1), i))
                            for par in range(2):
                                for kt in range(2):
                                    for cs in range(2):
                                        mm(q[:, 0, par * 256:(par + 1) * 256], X[:, cs, 2 * par + kt, ch], inv[:, 2 * cs + par, kt, :], kt + cs == 0, kt + cs == 2)
                            for cs in range(2):
                                last = mm(q[:, 1, 0:P], Y[:, cs, 4, ch], invp[:, cs, :], cs == 0, cs == 1)
                        pe_.did(last, job)

            @block.scalar
            def _(a):
                ac_.start(a)
                with a.Fori(0, NB) as i:
                    todo = [j for j in JOBS if j[0] in ("H", "X") and j[2] < 4]
                    for n, job in enumerate(todo):
                        a.wait_ge(pe_.sem, pe_.now(job, i))
                        if n >= 2:
                            a.wait_ge(dv_.sem, dv_.now(("ev", todo[n - 2]), i))
                        else:
                            a.wait_ge(dv_.sem, dv_.before(("ev", todo[len(todo) - 2 + n]), i))
                        ac_.did(act(osave[:, n % 2, :], pair[slot[job]][:, 1, :], ACT.Copy), job)

            @block.vector
            def _(v):
                dv_.start(v)
                with v.Fori(0, NB) as i:
                    cnt = [0]

                    def link(ins, label=None):
                        dv_.did(ins, label)
                        v.wait_ge(dv_.sem, dv_.here(i))

                    def weights(o):
                        if o == 0:
                            v.wait_ge(s_l["w4"], i * 16 + 16)
                            v.wait_ge(pe_.sem, pe_.before(("filt", 1, NT - 1), i))
                        else:
                            v.wait_ge(pe_.sem, pe_.now(("filt", 0, NT - 1), i))
                        dv_.did(tt(wsd[:, 0, :], w4[:, o, :], w4[:, 2 + o, :], ADD))
                        dv_.did(tt(wsd[:, 1, :], w4[:, o, :], w4[:, 2 + o, :], SUB), ("w", o))

                    def filt(o):
                        if o == 0:
                            v.wait_ge(s_l["dec"], i * 16 + 16)
                            v.wait_ge(pe_.sem, pe_.before(("H", 1, 4), i))
                        else:
                            v.wait_ge(pe_.sem, pe_.now(("H", 0, 4), i))
                        for j in range(NT):
                            v.wait_ge(pe_.sem, pe_.now(("filt", o, j), i))
                            dj = dec[:, j:j + 1, :].to_broadcast([P, 2, CB])
                            link(tt(hsd[:, :, j, :], pair[slot["filt", o, j]][:, :, :], dj, MUL), ("ev", ("filt", o, j)))
                        v.wait_ge(pe_.sem, pe_.now(("fix", o), i))
                        if o == 0:
                            v.wait_ge(s_l["bias"], i * 16 + 16)
                        link(tt(tmp[0:1, 0, :], bias[:, o, :], pair[slot["fix", o]][0:1, 0, :], SUB), ("ev", ("fix", o)))
                        dv_.did(tt(hsd[0:1, 0, 0, :], hsd[0:1, 0, 0, :], tmp[0:1, 0, :], ADD))
                        link(tt(hsd[0:1, 0, 4, :], hsd[0:1, 0, 4, :], tmp[0:1, 0, :], ADD), ("row0", o))

                    def spectrum(kind, o, dst):
                        if kind == "X" and o == 0:
                            v.wait_ge(pe_.sem, pe_.before(("inv", 1, 3), i))
                        for m in range(5):
                            job = (kind, o, m)
                            q = pair[slot[job]]
                            if m < 4:
                                cs, kt = m // 2, m % 2
                                v.wait_ge(ac_.sem, ac_.now(job, i))
                                osv = osave[:, cnt[0] % 2, :]
                                cnt[0] += 1
                                dv_.did(tt(dst[:, cs, kt, :], q[:, 0, :], osv, ADD))
                                if cs == 0:
                                    link(tt(dst[:, cs, 2 + kt, :], q[:, 0, :], osv, SUB), ("ev", job))
                                else:
                                    link(tt(dst[:, cs, 2 + kt, :], osv, q[:, 0, :], SUB), ("ev", job))
                            else:
                                v.wait_ge(pe_.sem, pe_.now(job, i))
                                link(nc.vector.tensor_copy(dst[:, :, 4, :], q[:, :, :]), ("ev", job))

                    def product(o):
                        if o == 0:
                            v.wait_ge(pe_.sem, pe_.before(("inv", 1, 3), i))
                        else:
                            v.wait_ge(pe_.sem, pe_.now(("inv", 0, 2), i))
                        f = lambda a: a.rearrange("p j n -> p (j n)")
                        Xr, Xs, Hr, Hs = f(X[:, 0]), f(X[:, 1]), f(H[:, 0]), f(H[:, 1])
                        Yr, Ys, t_ = f(Y[:, 0]), f(Y[:, 1]), f(tmp[:, :, :])
                        dv_.did(tt(Yr, Xr, Hr, MUL))
                        link(tt(t_, Xs, Hs, MUL))
                        link(tt(Yr, Yr, t_, SUB))
                        dv_.did(tt(Ys, Xr, Hs, MUL))
                        link(tt(t_, Xs, Hr, MUL))
                        link(tt(Ys, Ys, t_, ADD))
                        dv_.did(tt(X[:, 0, 0:2, :], Y[:, 0, 0:2, :], Y[:, 0, 2:4, :], ADD))
                        dv_.did(tt(X[:, 0, 2:4, :], Y[:, 0, 0:2, :], Y[:, 0, 2:4, :], SUB))
                        dv_.did(tt(X[:, 1, 0:2, :], Y[:, 1, 0:2, :], Y[:, 1, 2:4, :], SUB))
                        link(tt(X[:, 1, 2:4, :], Y[:, 1, 0:2, :], Y[:, 1, 2:4, :], ADD), ("comb", o))

                    weights(0)
                    filt(0)
                    spectrum("H", 0, H)
                    spectrum("X", 0, X)
                    weights(1)
                    product(0)
                    filt(1)
                    for m in range(3):
                        job = ("inv", 0, m)
                        v.wait_ge(pe_.sem, pe_.now(job, i))
                        if m == 0:
                            v.wait_ge(s_l["x1"], i * 16 + 16)
                            v.wait_ge(pe_.sem, pe_.now(("X", 0, 4), i))
                        q = pair[slot[job]]
                        js = slice(2 * m, min(2 * m + 2, NT))
                        w_ = 2 if m < 2 else 1
                        link(tt(vx[0][:, js, :], q[:, 0:w_, :], vx[1][:, js, :], MUL), ("ev", job))
                    spectrum("H", 1, H)
                    spectrum("X", 1, X)
                    product(1)
                    v.wait_ge(s_l["g"], i * 16 + 16)
                    v.wait_ge(s_f, i + 1)
                    for c4 in range(4):
                        job = ("inv", 1, c4)
                        v.wait_ge(pe_.sem, pe_.now(job, i))
                        q = pair[slot[job]]
                        dst = yout[:, c4, 0:LS].rearrange("p (t r) -> p r t", r=2)
                        gg = g[:, c4, 0:LS].rearrange("p (t r) -> p r t", r=2)
                        dv_.did(tt(dst, q[:, 0, :].rearrange("p (r t) -> p r t", r=2), gg, MUL))
                        dv_.did(tt(yout[:, c4, LS:T], q[:, 1, 0:LP], g[:, c4, LS:T], MUL), ("ev", job))


def out_proj(nc, A, G, M, l, w_dram):
    mm, stt, ts, tt, act = make_ops(nc)
    ps = G["ps"]
    HALF = D // 2
    RING = 6
    with ExitStack() as st:
        sb = lambda n, s: st.enter_context(nc.sbuf_tensor(f"{n}{l}", s, F32))
        y = sb("oy", [P, KE, T])
        w = sb("ow", [P, RING, HALF])
        o = sb("oo", [P, NT, D])
        x = sb("ox", [P, NT, D])
        gate = sb("ogate", [P, 2, D])
        bo = sb("obias", [P, D]) if l == 0 else None
        sq, ss, rs = sb("osq", [P, D]), sb("oss", [P, NT]), sb("ors", [P, NT])
        s_y = [st.enter_context(nc.semaphore(f"out{l}_y{k}")) for k in range(4)]
        s_w = [st.enter_context(nc.semaphore(f"out{l}_w{k}")) for k in range(RING)]
        s_x = st.enter_context(nc.semaphore(f"out{l}_x_loaded"))
        s_o = st.enter_context(nc.semaphore(f"out{l}_stored"))
        pe_, ac_, dv_ = (Steps(nc, st, f"out{l}_{n}", M) for n in ("pe", "act", "dve"))
        n_x = [0]
        with nc.Block() as block:
            @block.sync
            def _(sp):
                for k4 in range(4):
                    sp.dma_start(y[:, 4 * k4:4 * k4 + 4, :], A["y_d"][k4 * CB:(k4 + 1) * CB, :].rearrange("(k p) t -> p k t", p=P)).then_inc(s_y[k4], 16)
                n_x[0] = 0
                def xl(dst, src):
                    sp.dma_start(dst, src).then_inc(s_x, 16)
                    n_x[0] += 16
                if l == 0:
                    xl(x[:, 0:4, :], A["x_sample"][0].rearrange("(j p) n -> p j n", p=P))
                    xl(x[:, 4, :], A["x_prompt"][0])
                    xl(bo[:, :], A["hy_b_out"][0:1, :].partition_broadcast(P))
                else:
                    xl(x[:, :, :], A["x1_d"].rearrange("(j p) n -> p j n", p=P))
                for c in range(2):
                    xl(gate[:, c, :], A["gate_d"][l, c:c + 1, :].partition_broadcast(P))
                for n in range(2 * KE):
                    h, k = n // KE, n % KE
                    if n >= RING:
                        sp.wait_ge(pe_.sem, pe_.now(("k", n - RING)))
                    sp.dma_start(w[:, n % RING, :], w_dram[0, k * P:(k + 1) * P, h * HALF:(h + 1) * HALF]).then_inc(s_w[n % RING], 16)
                for j in range(NT):
                    sp.wait_ge(dv_.sem, dv_.now(("x", j)))
                    dst = A["x1_d"][j * P:(j + 1) * P, :] if l == 0 else (A["y_sample"][0, j * P:(j + 1) * P, :] if j < 4 else A["y_prompt"][0])
                    sp.dma_start(dst, x[:, j, :]).then_inc(s_o, 16)
                sp.wait_ge(s_o, 16 * NT)

            @block.tensor
            def _(pe):
                for n in range(2 * KE):
                    h, k = n // KE, n % KE
                    if h == 0 and k % 4 == 0:
                        pe.wait_ge(s_y[k // 4], 16)
                    pe.wait_ge(s_w[n % RING], 16 * (n // RING + 1))
                    if h == 1 and k == 0:
                        pe.wait_ge(dv_.sem, dv_.now(("oj", 0, NT - 1)))
                    for j in range(NT):
                        last = mm(ps[:, j, :], y[:, k, j * P:(j + 1) * P], w[:, n % RING, :], k == 0, k == KE - 1)
                    pe_.did(last, ("k", n))

            @block.vector
            def _(v):
                def link(ins, label=None):
                    dv_.did(ins, label)
                    v.wait_ge(dv_.sem, dv_.here())
                v.wait_ge(s_x, n_x[0])
                for h in range(2):
                    v.wait_ge(pe_.sem, pe_.now(("k", (h + 1) * KE - 1)))
                    hs = slice(h * HALF, (h + 1) * HALF)
                    for j in range(NT):
                        if l == 0:
                            ins = tt(o[:, j, hs], ps[:, j, :], bo[:, hs], ADD)
                        else:
                            ins = nc.vector.tensor_copy(o[:, j, hs], ps[:, j, :])
                        dv_.did(ins, ("oj", h, j))
                v.wait_ge(ac_.sem, ac_.now("ss"))
                dv_.did(ts(ss[:, :], ss[:, :], 1.0 / D, EPS, MUL, ADD), "var")
                v.wait_ge(ac_.sem, ac_.now("std"))
                link(nc.vector.reciprocal(rs[:, :], rs[:, :]))
                for j in range(NT):
                    link(stt(o[:, j, :], o[:, j, :], rs[:, j:j + 1], gate[:, j // 4, :], MUL, MUL))
                    dv_.did(tt(x[:, j, :], x[:, j, :], o[:, j, :], ADD), ("x", j))

            @block.scalar
            def _(a):
                for j in range(NT):
                    a.wait_ge(dv_.sem, dv_.now(("oj", 1, j)))
                    if j:
                        a.wait_ge(ac_.sem, ac_.here())
                    ac_.did(act(sq[:, :], o[:, j, :], ACT.Square, accum_out=ss[:, j:j + 1]), "ss")
                a.wait_ge(dv_.sem, dv_.now("var"))
                ac_.did(act(rs[:, :], ss[:, :], ACT.Sqrt), "std")
def rwkv_in(nc, A, G, M, hT):
    mm, stt, ts, tt, act = make_ops(nc)
    ps, col = G["ps"], G["col"]
    pair = [ps[:, 2 * q:2 * q + 2, :].rearrange("p b n -> p (b n)") for q in range(4)]
    MIX = {"r": 0, "w": 1, "k": 2, "v": 3, "a": 4, "z": 5}
    BIG = ("r", "k", "v", "z")
    SEQ = ("w", "a") + BIG
    U = 4
    with ExitStack() as st:
        sb = lambda n, s: st.enter_context(nc.sbuf_tensor(n, s, F32))
        xx = sb("xx", [P, KD, T])
        mix = [sb(f"mix{b}", [P, KD, T]) for b in range(2)]
        lw = [sb(f"lora_w{b}", [P, KD, 2, HID]) for b in range(2)]
        w = [sb(f"rw{u}", [P, KD, P]) for u in range(U)]
        out = [sb(f"rout{u}", [P, T]) for u in range(U)]
        sig = sb("rsig", [P, T])
        s_lw = st.enter_context(nc.semaphore("rw_lora_loaded"))
        s_w = [st.enter_context(nc.semaphore(f"rw_weights_{u}")) for u in range(U)]
        s_o = [st.enter_context(nc.semaphore(f"rw_stored_{u}")) for u in range(U)]
        s_f = [st.enter_context(nc.semaphore(f"rw_store_buffer_free_{u}")) for u in range(U)]
        mx = Steps(nc, st, "rw_mixes", M)
        lo_pe, lo_ac = Steps(nc, st, "rw_lora_pe", M), Steps(nc, st, "rw_lora_act", M)
        pe_ = {b: Steps(nc, st, f"rw_pe_{b}", M) for b in BIG}
        ac_ = {b: Steps(nc, st, f"rw_act_{b}", M) for b in BIG}
        dv_ = Steps(nc, st, "rw_dve_z", M)
        ROUNDS = KE // U
        mu = col[:, 0, 80:128].rearrange("p (m k) -> p m k", m=6)

        with nc.Block() as block:
            @block.sync
            def _(sp):
                for b, n in enumerate(("rw_w1", "rw_a1")):
                    for z in range(2):
                        sp.dma_start(lw[b][:, :, z, :], A[n][0, z].rearrange("(k p) r -> p k r", p=P)).then_inc(s_lw, 16)
                for bi, b in enumerate(BIG):
                    w_v = A[f"rw_w_{b}"][0].rearrange("(k p) n -> p k n", p=P)
                    if bi:
                        sp.wait_ge(pe_[BIG[bi - 1]].sem, (ROUNDS + 1) * pe_[BIG[bi - 1]].per())
                    with sp.Fori(0, ROUNDS) as i:
                        for u in range(U):
                            sp.wait_ge(pe_[b].sem, pe_[b].before(("proj", u), i))
                            sp.dma_start(w[u][:, :, :], w_v[:, :, bass.ds(i * U * P + u * P, P)]).then_inc(s_w[u], 16)

            @block.vector
            def _(v):
                dv_.start(v)

                def link(ins, label=None):
                    mx.did(ins, label)
                    v.wait_ge(mx.sem, mx.here())
                link(ts(xx[:, :, :], hT[:, :, :], -1.0, None, MUL))
                grid = lambda a, k0: a[:, k0:k0 + 2, 0:LS].rearrange("p k (r c) -> p k r c", c=GRID)
                for k in range(2):
                    for k0, dst, src in ((0, (slice(None), slice(1, GRID)), (slice(None), slice(0, GRID - 1))),
                                         (2, (slice(None), slice(0, GRID - 1)), (slice(None), slice(1, GRID)))):
                        g = lambda a, sl: a[:, k0 + k, 0:LS].rearrange("p (r c) -> p r c", c=GRID)[:, sl[0], sl[1]]
                        mx.did(tt(g(xx, dst), g(xx, dst), g(hT, src), ADD))
                mx.did(tt(xx[:, 4:6, GRID:LS], xx[:, 4:6, GRID:LS], hT[:, 4:6, 0:LS - GRID], ADD))
                mx.did(tt(xx[:, 6:8, 0:LS - GRID], xx[:, 6:8, 0:LS - GRID], hT[:, 6:8, GRID:LS], ADD))
                mx.did(tt(xx[:, 0:4, LS + 1:T], xx[:, 0:4, LS + 1:T], hT[:, 0:4, LS:T - 1], ADD))
                link(tt(xx[:, 4:8, LS:T - 1], xx[:, 4:8, LS:T - 1], hT[:, 4:8, LS + 1:T], ADD))

                def make(n):
                    b = SEQ[n]
                    if n >= 2:
                        p_ = SEQ[n - 2]
                        if p_ in BIG:
                            v.wait_ge(pe_[p_].sem, (ROUNDS + 1) * pe_[p_].per())
                        else:
                            v.wait_ge(lo_pe.sem, lo_pe.now(p_))
                    for k in range(KD):
                        mx.did(stt(mix[n % 2][:, k, :], xx[:, k, :], mu[:, MIX[b], k:k + 1], hT[:, k, :], MUL, ADD), ("mix", b))
                for n in range(len(SEQ)):
                    make(n)
                with v.Fori(0, ROUNDS) as i:
                    for u in range(U):
                        v.wait_ge(ac_["z"].sem, ac_["z"].now(("sig", u), i))
                        v.wait_ge(s_f[u], 3 * ROUNDS + i + 1)
                        dv_.did(tt(out[u][:, :], pair[u][:, 0:T], sig[:, :], MUL), ("z", u))

            @block.tensor
            def _(pe):
                pe.wait_ge(s_lw, 64)
                for n, b in enumerate(SEQ):
                    pe.wait_ge(mx.sem, mx.now(("mix", b)))
                    m = mix[n % 2]
                    if b in ("w", "a"):
                        for k in range(KD):
                            lhsT = lw[n][:, k, :, :].rearrange("p z r -> p (z r)")
                            mm(pair[n][:, 0:LS], lhsT, m[:, k, 0:LS], k == 0, k == KD - 1)
                            last = mm(pair[n][:, LS:T], lhsT, m[:, k, LS:T], k == 0, k == KD - 1)
                        lo_pe.did(last, b)
                        continue
                    bi = BIG.index(b)
                    if bi == 0:
                        pe.wait_ge(lo_ac.sem, lo_ac.now("a"))
                    else:
                        pe.wait_ge(ac_[BIG[bi - 1]].sem, (ROUNDS + 1) * ac_[BIG[bi - 1]].per())
                    pe_[b].start(pe)
                    with pe.Fori(0, ROUNDS) as i:
                        for u in range(U):
                            pe.wait_ge(s_w[u], (bi * ROUNDS + i) * 16 + 16)
                            if b == "z":
                                pe.wait_ge(dv_.sem, dv_.before(("z", u), i))
                            else:
                                pe.wait_ge(ac_[b].sem, ac_[b].before(("out", u), i))
                            for k in range(KD):
                                mm(pair[u][:, 0:LS], w[u][:, k, :], m[:, k, 0:LS], k == 0, k == KD - 1)
                                last = mm(pair[u][:, LS:T], w[u][:, k, :], m[:, k, LS:T], k == 0, k == KD - 1)
                            pe_[b].did(last, ("proj", u))

            @block.scalar
            def _(a):
                for n, (b, f, dst) in enumerate((("w", ACT.Tanh, G["wlo"]), ("a", ACT.Copy, G["alo"]))):
                    a.wait_ge(lo_pe.sem, lo_pe.now(b))
                    lo_ac.did(act(dst[:, :], pair[n][:, 0:T], f), b)
                for bi, b in enumerate(BIG):
                    ac_[b].start(a)
                    with a.Fori(0, ROUNDS) as i:
                        for u in range(U):
                            a.wait_ge(pe_[b].sem, pe_[b].now(("proj", u), i))
                            if b == "z":
                                if u:
                                    a.wait_ge(dv_.sem, dv_.now(("z", u - 1), i))
                                else:
                                    a.wait_ge(dv_.sem, dv_.before(("z", U - 1), i))
                                ac_[b].did(act(sig[:, :], pair[u][:, 0:T], ACT.Sigmoid), ("sig", u))
                            else:
                                a.wait_ge(s_f[u], bi * ROUNDS + i + 1)
                                ac_[b].did(act(out[u][:, :], pair[u][:, 0:T], ACT.Copy), ("out", u))

            @block.gpsimd
            def _(po):
                for u in range(U):
                    po.sem_inc(s_f[u], 1)
                for bi, b in enumerate(BIG):
                    with po.Fori(0, ROUNDS) as i:
                        for u in range(U):
                            if b == "z":
                                po.wait_ge(dv_.sem, dv_.now(("z", u), i))
                            else:
                                po.wait_ge(ac_[b].sem, ac_[b].now(("out", u), i))
                            po.dma_start(A["rkvz_d"][bi, bass.ds(i * U * P + u * P, P), :], out[u][:, :]).then_inc(s_o[u], 16)
                        for u in range(U):
                            po.wait_ge(s_o[u], (bi * ROUNDS + i) * 16 + 16)
                            po.sem_inc(s_f[u], 1)
                for u in range(U):
                    po.wait_ge(s_o[u], 16 * ROUNDS * 4)


def rwkv_scan(nc, A, G, M):
    mm, stt, ts, tt, act = make_ops(nc)
    ps, tab, col = G["ps"], G["tab"], G["col"]
    T_ = lambda n: tab[:, TAB[n][0]:TAB[n][1]]
    ident, heads, chunk = T_("ident"), T_("heads"), T_("chunk")
    between = T_("between").rearrange("p (l n) -> p l n", l=LEVELS)
    chosen = T_("chosen").rearrange("p (l n) -> p l n", l=LEVELS)
    HALVES = (slice(0, 64), slice(64, 128))
    NU = 2 * NC
    GROUPS = [slice(4 * g, 4 * g + 4) for g in range(NU // 4)]
    PAIRS = [slice(2 * p, 2 * p + 2) for p in range(NU // 2)]
    G4 = [(0, 4), (4, 4), (8, 2)]
    RING = 6
    JOBS = [("V", g, "act") for g in range(3)]
    JOBS += [(n, g, "act") for n in ("tk", "ta") for g in range(5)]
    JOBS += [(n, p, "dve") for p in range(10) for n in ("Mb", "Mk")]
    JOBS += [("CT", g, "act") for g in range(3)]
    FILL = {(1, 0): [("tb", 0), ("tb", 1)], (1, 1): [("tb", 2), ("tb", 3)], (2, 0): [("tb", 4), ("XV", 0)], (2, 1): [("XV", 1)],
            (3, 0): [("XV", 2)], (3, 1): [("XV", 3)], (4, 0): [("XV", 4)]}
    for lv in range(1, LEVELS):
        JOBS += [((n, lv), g, "dve") for g in range(3) for n in "TY"] + [(n, g, "act") for n, g in FILL.get((lv, 0), [])]
        JOBS += [(("Z", lv), g, "dve") for g in range(3)] + [(n, g, "act") for n, g in FILL.get((lv, 1), [])]
    JOBS += [("TX", g, "act") for g in range(5)] + [("TA", g, "act") for g in range(5)]
    BANK = {(n, g): q % RING for q, (n, g, _) in enumerate(JOBS)}
    OWNER = {(n, g): e for n, g, e in JOBS}
    LORAS = [(1, 0), (1, 1), (0, 0), (0, 1)]
    unit = lambda d, c: d * NC + c
    CHAINS = [("s", 0, list(range(CS)), 0), ("s", 1, list(range(CS - 1, -1, -1)), 0),
              ("p", 0, list(range(CS, NC)), 0), ("p", 1, list(range(NC - 1, CS - 1, -1)), 2)]
    UB = {("s", 0): 0, ("s", 1): 1, ("p", 0): 4, ("p", 1): 4}
    SB = {("s", 0): 2, ("s", 1): 3, ("p", 0): 5, ("p", 1): 5}
    STEPS = [[(s, d, n - at, cs) for s, d, cs, at in CHAINS if 0 <= n - at < len(cs)] for n in range(CS)]

    with ExitStack() as st:
        sb = lambda n, s: st.enter_context(nc.sbuf_tensor(n, s, F32))
        r, k, v, z = (sb(f"e_{n}", [P, T]) for n in "rkvz")
        pcl, gpc = sb("e_pc", [P, 8]), sb("e_gpc", [P, 2])
        omka = sb("e_omka", [P, 1])
        lw2, la2 = sb("e_w2", [P, P]), sb("e_a2", [P, P])
        two = lambda n: [sb(f"e_{n}{d}", [P, T]) for d in range(2)]
        ld, kd = two("ld"), two("kd")
        e1, e2, e3 = two("e1"), two("e2"), two("e3")
        kk, kr, bon, o = (sb(f"e_{n}", [P, T]) for n in ("kk", "kr", "bon", "o"))
        osq, ostd = e3
        pcd = sb("e_pcd", [P, NU])
        BDar = sb("BDar", [P, NU, 2, P])
        BDb, BDk = sb("BDb", [P, NU, P]), sb("BDk", [P, NU, P])
        M2T, Y = BDk[:, 0:NC, :], BDk[:, NC:NU, :]
        At, Bt, Kt = (sb(f"e_{n}t", [P, NU, P]) for n in "abk")
        V = sb("e_Vt", [P, NC, P])
        QA, AK = sb("QA", [P, NU, 2, P]), sb("AK", [P, NU, 2, P])
        Q, Arb, Aak, Ark = QA[:, :, 0, :], QA[:, :, 1, :], AK[:, :, 0, :], AK[:, :, 1, :]
        BDv, S_at = Q, Aak
        F = Q[:, NC:NU, :]
        M1, CT, TX = sb("M1", [P, NC, P]), sb("CT", [P, NC, P]), sb("TX", [P, NU, P])
        C_ = M1
        TA = At
        Sd = sb("Sd", [P, 4, P])
        S0, Sfin = sb("S0", [P, 2, P]), sb("Sfin", [P, 2, P])
        st0, stn = sb("st0", [P, 2, P]), sb("stn", [P, 2, P])
        names = ("r", "k", "v", "z", "w2", "a2", "st")
        s_l = {n: st.enter_context(nc.semaphore(f"scan_loaded_{n}")) for n in names}
        s_y = st.enter_context(nc.semaphore("scan_y_stored"))
        s_n = st.enter_context(nc.semaphore("scan_state_stored"))
        s_fy = st.enter_context(nc.semaphore("scan_y_buffer_free"))
        s_fn = st.enter_context(nc.semaphore("scan_state_buffer_free"))
        s_z = st.enter_context(nc.semaphore("scan_cleared"))
        kinds = lambda what: {n: Steps(nc, st, f"scan_{what}_{n}", M) for n in ("pe", "act", "dve")}
        main, prep, post = kinds("main"), kinds("prep"), kinds("post")
        wide = ps[:, 6:8, :].rearrange("p b n -> p (b n)")
        half = lambda a, h: a[HALVES[h], :].rearrange("p (c t) -> p c t", t=C)
        def waits(eng):
            return lambda s, label, i: eng.wait_ge(s.sem, s.now(label, i))

        def rounds(eng, body):
            body(0, False, True)
            with eng.Fori(1, KE - 1) as i:
                body(i, True, True)
            body(KE - 1, True, False)

        def begin(*steps):
            for s in steps:
                s.n = 0

        def skip(eng, s, n):
            eng.sem_inc(s.sem, n)
            s.n += n

        with nc.Block() as block:
            @block.sync
            def _(sp):
                sp.wait_ge(s_z, 5)

                def load_keys(j):
                    ch = bass.ds(j * P, P)
                    rows = A["rkvz_d"]
                    sp.wait_ge(prep["dve"].sem, prep["dve"].before("BDar", j))
                    sp.dma_start(k[:, :], rows[1, ch, :]).then_inc(s_l["k"], 16)
                    for n, src, dst in (("w2", "rw_w2", lw2), ("a2", "rw_a2", la2)):
                        sp.dma_start(dst[:, :], A[src][0].rearrange("z r e -> (z r) e")[:, ch]).then_inc(s_l[n], 16)

                def load_rest(j, i=None):
                    ch = bass.ds(j * P, P)
                    rows = A["rkvz_d"]
                    if i is not None:
                        sp.wait_ge(post["dve"].sem, post["dve"].now("bonus", i))
                    sp.dma_start(v[:, :], rows[2, ch, :]).then_inc(s_l["v"], 16)
                    sp.dma_start(r[:, :], rows[0, ch, :]).then_inc(s_l["r"], 16)
                    for d, src in enumerate(("state_rwkv_fwd", "state_rwkv_bwd")):
                        state = A[src][0, 0].rearrange("h v k -> (h v) k")
                        for h in range(2):
                            sp.dma_start(st0[HALVES[h], d, HALVES[h]], state[bass.ds(j * P + 64 * h, 64), :]).then_inc(s_l["st"], 16)

                def body(i, has_post, has_prep):
                    if has_prep:
                        load_keys(i + 1)
                    if has_post:
                        sp.wait_ge(post["dve"].sem, post["dve"].now("y", i))
                    sp.dma_start(z[:, :], A["rkvz_d"][3, bass.ds(i * P, P), :]).then_inc(s_l["z"], 16)
                    if has_prep:
                        load_rest(i + 1, i)
                load_keys(0)
                load_rest(0)
                rounds(sp, body)

            @block.gpsimd
            def _(po):
                for a in (BDar[:, :, :, :].rearrange("p c q n -> p (c q n)"), BDb[:, :, :].rearrange("p c n -> p (c n)"),
                          BDk[:, :, :].rearrange("p c n -> p (c n)"), st0[:, :, :].rearrange("p c n -> p (c n)"),
                          QA[:, :, :, :].rearrange("p c q n -> p (c q n)")):
                    nc.gpsimd.memset(a, 0.0).then_inc(s_z, 1)
                po.sem_inc(s_fy, 1)
                po.sem_inc(s_fn, 1)

                def store_y(i):
                    po.wait_ge(post["dve"].sem, post["dve"].now("y", i))
                    po.dma_start(A["y_d"][bass.ds((i - 1) * P, P), :], o[:, :]).then_inc(s_y, 16)
                    po.wait_ge(s_y, i * 16)
                    po.sem_inc(s_fy, 1)

                def body(i, has_post, has_prep):
                    if has_post:
                        store_y(i)
                    po.wait_ge(main["act"].sem, main["act"].now("stn", i))
                    for d, n in enumerate(("new_state_fwd", "new_state_bwd")):
                        rows = A[n][0, 0].rearrange("h v k -> (h v) k")
                        for h in range(2):
                            po.dma_start(rows[bass.ds(i * P + 64 * h, 64), :], stn[HALVES[h], d, HALVES[h]]).then_inc(s_n, 16)
                    po.wait_ge(s_n, i * 64 + 64)
                    po.sem_inc(s_fn, 1)
                rounds(po, body)
                store_y(KE)
                po.wait_ge(s_y, 16 * KE)
                po.wait_ge(s_n, 64 * KE)

            @block.tensor
            def _(pe):
                wait = waits(pe)
                for s in (main, prep, post):
                    s["pe"].start(pe)
                pe.wait_ge(s_z, 5)

                def lora(q, d, j):
                    w_, lo = ((lw2, "wlo"), (la2, "alo"))[q]
                    mm(wide[:, 0:LS], w_[HALVES[d], :], G[lo][HALVES[d], 0:LS])
                    prep["pe"].did(mm(wide[:, LS:T], w_[HALVES[d], :], G[lo][HALVES[d], LS:T]), ("lora", q, d))

                def norms(j):
                    wait(prep["dve"], "kk2", j)
                    mm(wide[:, 0:LS], heads, e2[1][:, 0:LS])
                    prep["pe"].did(mm(wide[:, LS:T], heads, e2[1][:, LS:T]), "ss")

                def states(j):
                    wait(prep["act"], "norm", j)
                    pe.wait_ge(s_l["st"], j * 64 + 64)
                    for d in range(2):
                        last = nc.tensor.transpose(ps[:, 6, d * P:(d + 1) * P], st0[:, d, :], ident)
                    prep["pe"].did(last, "S0")

                def head_sum(src, label):
                    mm(wide[:, 0:LS], heads, src[:, 0:LS])
                    post["pe"].did(mm(wide[:, LS:T], heads, src[:, LS:T]), label)

                def body(i, has_post, has_prep):
                    j = i + 1
                    D_ = lambda label: wait(main["dve"], label, i)
                    A_ = lambda label: wait(main["act"], label, i)

                    def last_of(waits):
                        for e in ("dve", "act"):
                            labels = [label for owner, label in waits if owner == e]
                            if labels:
                                wait(main[e], max(labels, key=main[e].mark), i)

                    def job(n, g, units, fill, after=()):
                        after = list(after)
                        q = JOBS.index((n, g, OWNER[n, g]))
                        if q == 0:
                            pe.wait_ge(main["dve"].sem, main["dve"].before("O", i))
                            pe.wait_ge(main["act"].sem, main["act"].before("stn", i))
                        elif q >= RING:
                            pn, pg, owner = JOBS[q - RING]
                            after.append((owner, (pn, pg)))
                        last_of(after)
                        width = 256 if n in ("Mb", "Mk") else P
                        for c, u in enumerate(range(units.start, units.stop)):
                            last = fill(ps[:, BANK[n, g], c * width:(c + 1) * width], u)
                        main["pe"].did(last, (n, g))

                    wait(prep["dve"], "BDv", i)
                    for g, (c0, n) in enumerate(G4):
                        job("V", g, slice(c0, c0 + n), lambda out, u: nc.tensor.transpose(out, BDv[:, u, :], ident))
                    wait(prep["dve"], "BDbk", i)
                    for n, src in (("tk", BDk[:, :, :]), ("ta", BDar[:, :, 0, :])):
                        if n == "ta":
                            wait(prep["dve"], "BDar", i)
                        for g, us in enumerate(GROUPS):
                            job(n, g, us, lambda out, u, src=src: nc.tensor.transpose(out, src[:, u, :], ident))
                    for p, us in enumerate(PAIRS):
                        job("Mb", p, us, lambda out, u: mm(out, BDb[:, u, :], BDar[:, u, :, :].rearrange("p q n -> p (q n)")))
                        job("Mk", p, us, lambda out, u: mm(out, BDk[:, u, :], BDar[:, u, :, :].rearrange("p q n -> p (q n)")))
                    chunks = [slice(c0, c0 + n) for c0, n in G4]
                    for g, cs in enumerate(chunks):
                        job("CT", g, cs, lambda out, c: nc.tensor.transpose(out, C_[:, c, :], ident), (("dve", "C"),))

                    def fill(lv, part):
                        for n, g in FILL.get((lv, part), []):
                            if n == "tb":
                                job(n, g, GROUPS[g], lambda out, u: nc.tensor.transpose(out, BDb[:, u, :], ident))
                            else:
                                job(n, g, GROUPS[g], lambda out, u: mm(out, Aak[:, u, :], V[:, u % NC, :]), (("act", ("V", 2)),))
                        if (lv, part) == (1, 1) and has_prep:
                            wait(prep["act"], "S0", i)
                            pe.wait_ge(s_l["w2"], j * 16 + 16)
                            pe.wait_ge(s_l["a2"], j * 16 + 16)
                            lora(1, 0, j)
                        if (lv, part) == (2, 0) and has_prep:
                            wait(prep["act"], ("lora", 1, 0), j)
                            lora(1, 1, j)
                        if (lv, part) == (2, 1):
                            if has_post:
                                if has_prep:
                                    wait(prep["act"], ("lora", 1, 1), j)
                                else:
                                    wait(prep["act"], "S0", i)
                                head_sum(o, "mean")
                            else:
                                skip(pe, post["pe"], 2)
                        if (lv, part) == (3, 1) and has_post:
                            wait(post["act"], "sq", i)
                            head_sum(osq, "var")
                        if (lv, part) == (4, 0) and has_prep:
                            if has_post:
                                wait(post["dve"], "varv", i)
                            else:
                                wait(prep["act"], ("lora", 1, 1), j)
                            lora(0, 0, j)
                        if (lv, part) == (4, 1) and has_prep:
                            wait(prep["act"], ("lora", 0, 0), j)
                            lora(0, 1, j)
                        if (lv, part) == (5, 1):
                            if has_prep:
                                wait(prep["act"], ("lora", 0, 1), j)
                            wait(post["dve"], "bonus_in", i)
                            head_sum(bon, "bonus")

                    for lv in range(1, LEVELS):
                        for g, cs in enumerate(chunks):
                            job(("T", lv), g, cs, lambda out, c: nc.tensor.transpose(out, F[:, c, :], ident),
                                (("dve", "F0" if lv == 1 else (("Z", lv - 1), g)),))
                            job(("Y", lv), g, cs, lambda out, c: mm(out, CT[:, c, :], M1[:, c, :]),
                                (("dve", ("M1", lv, g)), ("act", ("CT", g))))
                        fill(lv, 0)
                        for g, cs in enumerate(chunks):
                            job(("Z", lv), g, cs, lambda out, c: mm(out, M2T[:, c, :], Y[:, c, :]),
                                (("dve", (("T", lv), g)), ("dve", (("Y", lv), g))))
                        fill(lv, 1)
                    for g, us in enumerate(GROUPS):
                        job("TX", g, us, lambda out, u: mm(out, Q[:, u, :], TX[:, u, :]), (("dve", ("Q", g)), ("act", ("XV", g))))
                    for g, us in enumerate(GROUPS):
                        job("TA", g, us, lambda out, u: mm(out, At[:, u, :], Q[:, u, :]))
                    if has_prep:
                        wait(post["dve"], "bonus", i)
                        norms(j)
                    A_(("TA", 4))
                    for n, chains in enumerate(STEPS):
                        for s, d, m, cs in chains:
                            if m == 0 and s == "p":
                                continue
                            if m:
                                D_(("S", s, d, m - 1))
                            state = S0[:, d, :] if m == 0 else S_at[:, unit(d, cs[m]), :]
                            main["pe"].did(mm(ps[:, UB[s, d], 0:P], TA[:, unit(d, cs[m]), :], state), ("U", s, d, m))
                        for s, d, m, cs in chains:
                            if s == "s" and m == CS - 1:
                                continue
                            if m == 0 and (s, d) == ("p", 1):
                                D_(("S", "p", 0, 1))
                            mm(ps[:, SB[s, d], 0:P], Kt[:, unit(d, cs[m]), :], V[:, cs[m], :], True, False)
                        for s, d, m, cs in chains:
                            if s == "s" and m == CS - 1:
                                continue
                            if not (m == 0 and s == "p"):
                                D_(("U", s, d, m))
                            last = mm(ps[:, SB[s, d], 0:P], Bt[:, unit(d, cs[m]), :], TX[:, unit(d, cs[m]), :], False, True)
                            main["pe"].did(last, ("S", s, d, m))
                    for g, (c0, n) in enumerate(G4):
                        last_of((("dve", ("U", "s", 1, CS - 1)), ("dve", ("S", "p", 1, 1))))
                        for c in range(c0, c0 + n):
                            out = ps[:, g, (c - c0) * P:(c - c0 + 1) * P]
                            terms = []
                            for d in range(2):
                                u = unit(d, c)
                                first = [cs[0] for s, dd, cs, _ in CHAINS if dd == d and c in cs][0] == c
                                if not first:
                                    terms.append((S_at[:, u, :], BDar[:, u, 1, :]))
                                elif c < CS:
                                    terms.append((S0[:, d, :], BDar[:, u, 1, :]))
                                terms.append((TX[:, u, :], Arb[:, u, :]))
                                terms.append((V[:, c, :], Ark[:, u, :]))
                            for q, (a, b) in enumerate(terms):
                                last = mm(out, a, b, q == 0, q == len(terms) - 1)
                        main["pe"].did(last, ("O", g))
                    for d in range(2):
                        last = nc.tensor.transpose(ps[:, 5, d * P:(d + 1) * P], Sfin[:, d, :], ident)
                    main["pe"].did(last, "stn")
                    if has_prep:
                        states(j)

                pe.wait_ge(s_l["w2"], 16)
                pe.wait_ge(s_l["a2"], 16)
                for n, (q, d) in enumerate(LORAS):
                    if n:
                        wait(prep["act"], ("lora", *LORAS[n - 1]), 0)
                    lora(q, d, 0)
                wait(prep["act"], ("lora", *LORAS[-1]), 0)
                norms(0)
                states(0)

                def counted(i, has_post, has_prep):
                    begin(main["pe"], post["pe"], prep["pe"])
                    body(i, has_post, has_prep)
                rounds(pe, counted)
                begin(post["pe"])
                pe.wait_ge(main["dve"].sem, main["dve"].now("O", KE - 1))
                head_sum(o, "mean")
                wait(post["act"], "sq", KE)
                head_sum(osq, "var")

            @block.scalar
            def _(a):
                wait = waits(a)
                for s in (main, prep, post):
                    s["act"].start(a)
                flat = lambda x: x.rearrange("p c n -> p (c n)")

                def sigmoid(q, d, j):
                    wait(prep["pe"], ("lora", q, d), j)
                    wait(prep["dve"], "pcl", j)
                    dst = (ld, kd)[q][d]
                    prep["act"].did(act(dst[:, :], wide[:, 0:T], ACT.Sigmoid, bias=pcl[:, 2 * q + d:2 * q + d + 1]), ("lora", q, d))

                def norm(j):
                    wait(prep["pe"], "ss", j)
                    prep["act"].did(act(e2[0][:, :], wide[:, 0:T], ACT.Sqrt), "norm")

                def exps(j):
                    for d in range(2):
                        wait(prep["dve"], ("c", d), j)
                        if d == 0:
                            wait(prep["dve"], "kk", j)
                        prep["act"].did(act(e2[d][:, :], e1[d][:, :], ACT.Exp, scale=-1.0))
                        prep["act"].did(act(e3[d][:, :], e3[d][:, :], ACT.Exp))
                        a.wait_ge(prep["act"].sem, prep["act"].here(j))
                        prep["act"].did(act(e1[d][:, :], e1[d][:, :], ACT.Exp), ("exp", d))

                def states(j):
                    wait(prep["pe"], "S0", j)
                    prep["act"].did(act(flat(S0[:, :, :]), ps[:, 6, 0:2 * P], ACT.Copy), "S0")

                def body(i, has_post, has_prep):
                    begin(main["act"], post["act"], prep["act"])
                    j = i + 1

                    def take(n, g, dst):
                        wait(main["pe"], (n, g), i)
                        size = dst.shape[1] * P
                        main["act"].did(act(dst, ps[:, BANK[n, g], 0:size].rearrange("p (c n) -> p c n", n=P), ACT.Copy), (n, g))

                    for g, (c0, n) in enumerate(G4):
                        take("V", g, V[:, c0:c0 + n, :])
                    for n, dst in (("tk", Kt), ("ta", At)):
                        for g, us in enumerate(GROUPS):
                            take(n, g, dst[:, us, :])
                    for g, (c0, n) in enumerate(G4):
                        take("CT", g, CT[:, c0:c0 + n, :])
                    if not has_post:
                        skip(a, post["act"], 2)
                    for lv in range(1, LEVELS):
                        for part in range(2):
                            for n, g in FILL.get((lv, part), []):
                                take(n, g, {"tb": Bt, "XV": TX}[n][:, GROUPS[g], :])
                            if has_prep:
                                for at, (q, d) in zip(((1, 1), (2, 0), (4, 0), (4, 1)), LORAS):
                                    if (lv, part) == at:
                                        sigmoid(q, d, j)
                            if has_post and (lv, part) == (2, 1):
                                wait(post["dve"], "oc", i)
                                post["act"].did(act(osq[:, :], o[:, :], ACT.Square), "sq")
                            if has_post and (lv, part) == (3, 1):
                                wait(post["dve"], "varv", i)
                                post["act"].did(act(ostd[:, :], ostd[:, :], ACT.Sqrt), "gstd")
                    for g, us in enumerate(GROUPS):
                        take("TX", g, TX[:, us, :])
                    for g, us in enumerate(GROUPS):
                        take("TA", g, TA[:, us, :])
                    if has_prep:
                        norm(j)
                        exps(j)
                    wait(main["pe"], "stn", i)
                    a.wait_ge(s_fn, i + 1)
                    main["act"].did(act(flat(stn[:, :, :]), ps[:, 5, 0:2 * P], ACT.Copy), "stn")
                    if has_prep:
                        states(j)

                for q, d in LORAS:
                    sigmoid(q, d, 0)
                norm(0)
                exps(0)
                states(0)
                rounds(a, body)
                begin(post["act"])
                wait(post["dve"], "oc", KE)
                post["act"].did(act(osq[:, :], o[:, :], ACT.Square), "sq")
                wait(post["dve"], "varv", KE)
                post["act"].did(act(ostd[:, :], ostd[:, :], ACT.Sqrt), "gstd")

            @block.vector
            def _(v_):
                wait = waits(v_)
                for s in (main, prep, post):
                    s["dve"].start(v_)
                w0a0 = col[:, 2, 96:128].rearrange("p (q k) -> p q k", k=KE)
                rest = col[:, 3, :].rearrange("p (q k) -> p q k", k=KE)
                vec = nc.vector
                column = lambda a, j: a[:, :, bass.ds(j, 1)].rearrange("p s o -> p (s o)")
                v_.wait_ge(s_z, 5)

                def linker(s, i):
                    def link(ins, label=None):
                        s["dve"].did(ins, label)
                        v_.wait_ge(s["dve"].sem, s["dve"].here(i))
                    return link

                def columns(j):
                    link = linker(prep, j)
                    prep["dve"].did(vec.tensor_copy(pcl[:, 0:2], column(w0a0, j)))
                    link(vec.tensor_copy(pcl[:, 2:8], column(rest[:, 0:6, :], j)), "pcl")
                    prep["dve"].did(ts(omka[:, :], pcl[:, 5:6], -1.0, 1.0, MUL, ADD))
                    v_.wait_ge(s_l["k"], j * 16 + 16)
                    link(ts(kk[:, :], k[:, :], pcl[:, 4:5], None, MUL))
                    prep["dve"].did(tt(e2[1][:, :], kk[:, :], kk[:, :], MUL), "kk2")

                def sums(j, d):
                    link = linker(prep, j)
                    wait(prep["act"], ("lora", 0, d), j)
                    link(ts(ld[d][:, :], ld[d][:, :], -DECAY_MAX, None, MUL))
                    link(vec.tensor_tensor_scan(e1[d][:, :], chunk, ld[d][:, :], 0.0, MUL, ADD))
                    if d == 0:
                        link(tt(e3[d][:, :], e1[d][:, :], ld[d][:, :], SUB), ("c", d))
                    else:
                        c3 = e1[d][:, :].rearrange("p (c t) -> p c t", t=C)
                        tot = c3[:, :, C - 1:C].to_broadcast([P, NC, C])
                        link(tt(e3[d][:, :].rearrange("p (c t) -> p c t", t=C), tot, c3, SUB))
                        link(tt(e1[d][:, :], e3[d][:, :], ld[d][:, :], ADD), ("c", d))

                def keys(j):
                    link = linker(prep, j)
                    wait(prep["act"], "norm", j)
                    link(ts(e2[0][:, :], e2[0][:, :], 1e-12, None, ALU.max))
                    link(vec.reciprocal(e2[0][:, :], e2[0][:, :]))
                    link(tt(kk[:, :], kk[:, :], e2[0][:, :], MUL), "kk")

                def key_dir(j, d):
                    link = linker(prep, j)
                    wait(prep["act"], ("lora", 1, d), j)
                    link(tt(ld[d][:, :], kk[:, :], kd[d][:, :], MUL))
                    link(ts(kd[d][:, :], kd[d][:, :], pcl[:, 5:6], omka[:, :], MUL, ADD))
                    link(tt(kd[d][:, :], kd[d][:, :], k[:, :], MUL), "kd")
                    if d == 0:
                        link(ts(kr[:, :], kd[d][:, :], pcl[:, 6:7], None, MUL))
                    else:
                        link(stt(kr[:, :], kd[d][:, :], pcl[:, 7:8], kr[:, :], MUL, ADD))

                def blocks_bkv(j):
                    v_.wait_ge(s_l["v"], j * 16 + 16)
                    for h in range(2):
                        prep["dve"].did(vec.tensor_copy(BDv[HALVES[h], 0:NC, HALVES[h]], half(v, h)), "BDv")
                    for d in range(2):
                        wait(prep["act"], ("exp", d), j)
                        end = e1[d][:, :].rearrange("p (c t) -> p c t", t=C)[:, :, (C - 1 if d == 0 else 0)]
                        prep["dve"].did(vec.tensor_copy(pcd[:, d * NC:(d + 1) * NC], end))
                        us = slice(d * NC, (d + 1) * NC)
                        for h in range(2):
                            hh = HALVES[h]
                            prep["dve"].did(tt(BDb[hh, us, hh], half(ld[d], h), half(e2[d], h), MUL))
                            prep["dve"].did(tt(BDk[hh, us, hh], half(kd[d], h), half(e2[d], h), MUL), "BDbk")

                def blocks_ar(j):
                    v_.wait_ge(s_l["r"], j * 16 + 16)
                    for d in range(2):
                        us = slice(d * NC, (d + 1) * NC)
                        for h in range(2):
                            hh = HALVES[h]
                            prep["dve"].did(stt(BDar[hh, us, 0, hh], half(kk, h), -1.0, half(e3[d], h), MUL, MUL))
                            prep["dve"].did(tt(BDar[hh, us, 1, hh], half(r, h), half(e1[d], h), MUL), "BDar")

                def norm_mean(i):
                    link = linker(post, i)
                    wait(post["pe"], "mean", i)
                    post["dve"].did(vec.tensor_copy(gpc[:, :], column(rest[:, 6:8, :], i - 1)))
                    link(stt(o[:, :], wide[:, 0:T], -1.0 / 64, o[:, :], MUL, ADD), "oc")

                def norm_var(i):
                    wait(post["pe"], "var", i)
                    post["dve"].did(ts(ostd[:, :], wide[:, 0:T], 1.0 / 64, GN_EPS, MUL, ADD), "varv")

                def norm_rstd(i):
                    wait(post["act"], "gstd", i)
                    linker(post, i)(vec.reciprocal(ostd[:, :], ostd[:, :]))

                def norm_out(i):
                    link = linker(post, i)
                    link(tt(o[:, :], o[:, :], ostd[:, :], MUL))
                    link(ts(o[:, :], o[:, :], gpc[:, 0:1], gpc[:, 1:2], MUL, ADD))
                    link(tt(o[:, :], o[:, :], bon[:, :], ADD))
                    v_.wait_ge(s_l["z"], i * 16)
                    post["dve"].did(tt(o[:, :], o[:, :], z[:, :], MUL), "y")

                def body(i, has_post, has_prep):
                    begin(main["dve"], post["dve"], prep["dve"])
                    j = i + 1
                    md = main["dve"]
                    link = linker(main, i)

                    def wide_mask(m, n):
                        return m.rearrange("p (o n) -> p o n", o=1).to_broadcast([P, n, m.shape[1]])

                    def take_scores(n, p, us):
                        wait(main["pe"], (n, p), i)
                        dst = {"Mb": QA, "Mk": AK}[n][:, us, :, :].rearrange("p c q n -> p c (q n)")
                        src = ps[:, BANK[n, p], :].rearrange("p (c n) -> p c n", c=2)
                        md.did(tt(dst, src, wide_mask(T_(("mk_f", "mk_b")[us.start // NC]), 2), MUL), (n, p))

                    def product(n, g):
                        wait(main["pe"], (n, g), i)
                        c0, cnt = G4[g]
                        return slice(c0, c0 + cnt), ps[:, BANK[n, g], 0:cnt * P].rearrange("p (c n) -> p c n", c=cnt)

                    def choose(lv, g):
                        cs = slice(G4[g][0], G4[g][0] + G4[g][1])
                        md.did(tt(M1[:, cs, :], F[:, cs, :], wide_mask(chosen[:, lv, :], G4[g][1]), MUL), ("M1", lv, g))

                    for p, us in enumerate(PAIRS):
                        take_scores("Mb", p, us)
                        take_scores("Mk", p, us)
                    v_.wait_ge(md.sem, md.here(i))
                    link(tt(C_[:, :, :], Q[:, 0:NC, :], F, ADD), "C")
                    link(tt(F, C_[:, :, :], wide_mask(between[:, 0, :], NC), MUL))
                    link(tt(F, F, wide_mask(ident, NC), ADD), "F0")
                    wait(main["pe"], ("CT", 2), i)
                    for g in range(3):
                        choose(1, g)
                    if has_prep:
                        columns(j)
                    for lv in range(1, LEVELS):
                        for g in range(3):
                            cs, src = product(("T", lv), g)
                            md.did(tt(M2T[:, cs, :], src, wide_mask(chosen[:, lv, :], src.shape[1]), MUL), (("T", lv), g))
                            cs, src = product(("Y", lv), g)
                            md.did(tt(Y[:, cs, :], src, wide_mask(between[:, lv, :], src.shape[1]), MUL), (("Y", lv), g))
                        for g in range(3):
                            cs, src = product(("Z", lv), g)
                            md.did(tt(F[:, cs, :], F[:, cs, :], src, ADD), (("Z", lv), g))
                            if lv < LEVELS - 1 and g:
                                v_.wait_ge(md.sem, md.now((("Z", lv), g - 1), i))
                                choose(lv + 1, g - 1)
                        v_.wait_ge(md.sem, md.here(i))
                        if lv < LEVELS - 1:
                            choose(lv + 1, 2)
                        if lv == 2 and has_post:
                            norm_mean(i)
                        if lv == 3 and has_post:
                            norm_var(i)
                        if lv == 4:
                            if has_post:
                                norm_rstd(i)
                                norm_out(i)
                            else:
                                skip(v_, post["dve"], POST_STEPS)
                            post["dve"].did(tt(bon[:, :], kr[:, :], r[:, :], MUL), "bonus_in")
                    for d in range(2):
                        for g, (c0, cnt) in enumerate(G4):
                            us = slice(d * NC + c0, d * NC + c0 + cnt)
                            md.did(tt(Q[:, us, :], F[:, c0:c0 + cnt, :], wide_mask(T_(("mk_f", "mk_b")[d])[:, P:2 * P], cnt), MUL),
                                   ("Q", us.stop // 4 - 1))
                    wait(post["pe"], "bonus", i)
                    linker(post, i)(tt(bon[:, :], wide[:, 0:T], v[:, :], MUL), "bonus")
                    if has_prep:
                        sums(j, 0)
                        sums(j, 1)
                        keys(j)
                        key_dir(j, 0)
                        key_dir(j, 1)
                    wait(main["act"], ("TX", 4), i)
                    for n, chains in enumerate(STEPS):
                        slot = {(s, d): q for q, (s, d, m, cs) in enumerate(chains)}
                        for s, d, m, cs in chains:
                            u = unit(d, cs[m])
                            if (m == 0 and s == "p") or (s == "s" and m == CS - 1):
                                continue
                            if m == 0:
                                wait(prep["act"], "S0", i)
                            state = S0[:, d, :] if m == 0 else S_at[:, u, :]
                            md.did(ts(Sd[:, slot[s, d], :], state, pcd[:, u:u + 1], None, MUL))
                        for s, d, m, cs in chains:
                            u = unit(d, cs[m])
                            if m == 0 and s == "p":
                                continue
                            wait(main["pe"], ("U", s, d, m), i)
                            md.did(tt(TX[:, u, :], ps[:, UB[s, d], 0:P], TX[:, u, :], ADD), ("U", s, d, m))
                        for s, d, m, cs in chains:
                            u = unit(d, cs[m])
                            if s == "s" and m == CS - 1:
                                continue
                            wait(main["pe"], ("S", s, d, m), i)
                            nxt = S_at[:, unit(d, cs[m + 1]), :] if m + 1 < len(cs) else Sfin[:, d, :]
                            if m == 0 and s == "p":
                                link(ts(nxt, ps[:, SB[s, d], 0:P], pcd[:, u:u + 1], None, MUL), ("S", s, d, m))
                            else:
                                link(stt(nxt, ps[:, SB[s, d], 0:P], pcd[:, u:u + 1], Sd[:, slot[s, d], :], MUL, ADD), ("S", s, d, m))
                    if has_prep:
                        blocks_bkv(j)
                    v_.wait_ge(s_fy, i + 1)
                    for g, (c0, n) in enumerate(G4):
                        wait(main["pe"], ("O", g), i)
                        for h in range(2):
                            dst = o[HALVES[h], c0 * C:(c0 + n) * C].rearrange("p (c t) -> p c t", t=C)
                            src = ps[HALVES[h], g, 0:n * P].rearrange("p (c t) -> p c t", c=n)[:, :, HALVES[h]]
                            md.did(vec.tensor_copy(dst, src), "O")
                    if has_prep:
                        blocks_ar(j)

                POST_STEPS = 8
                columns(0)
                sums(0, 0)
                sums(0, 1)
                keys(0)
                key_dir(0, 0)
                key_dir(0, 1)
                blocks_bkv(0)
                blocks_ar(0)
                rounds(v_, body)
                begin(post["dve"])
                norm_mean(KE)
                norm_var(KE)
                norm_rstd(KE)
                norm_out(KE)


def rwkv(nc, A, G, M):
    with ExitStack() as st:
        for n in ("wlo", "alo"):
            G[n] = st.enter_context(nc.sbuf_tensor(n, [P, T], F32))
        with nc.sbuf_tensor("hT1", [P, KD, T], F32) as hT:
            load_norm(nc, A, G, M, 1, hT)
            rwkv_in(nc, A, G, M, hT)
        rwkv_scan(nc, A, G, M)


def program(nc, A, M):
    with ExitStack() as st:
        G = {}
        G["ps"] = st.enter_context(nc.psum_tensor("ps", [P, 8, 512], F32))
        for n, s in (("tab", [P, TAB_N]), ("col", [P, 4, P]), ("fcol", [HID, 4]),
                     ("scl", [P, 2, KD, 2]), ("shf", [P, 2, KD, 2])):
            G[n] = st.enter_context(nc.sbuf_tensor(n, s, F32))
        modulation(nc, A, G, M)
        with ExitStack() as s1:
            G["hid"] = s1.enter_context(nc.sbuf_tensor("hid", [HID, T], F32))
            filter_hidden(nc, A, G, M)
            with nc.sbuf_tensor("hT0", [P, KD, T], F32) as hT:
                load_norm(nc, A, G, M, 0, hT)
                hyena_in(nc, A, G, M, hT)
            hyena_conv(nc, A, G, M)
        out_proj(nc, A, G, M, 0, A["hy_w_out"])
        if STAGE == 1:
            return
        rwkv(nc, A, G, M)
        out_proj(nc, A, G, M, 1, A["rw_w_o"])


def constants():
    f = np.float32
    tab = np.zeros((P, TAB_N), np.float64)
    put = lambda n, a: tab.__setitem__((slice(0, a.shape[0]), slice(*TAB[n])), a)
    r = np.arange(P)
    row, c = r[:, None], r[None, :]
    same = row // 64 == c // 64
    put("ident", np.eye(P))
    put("heads", same.astype(f))
    for d, less in (("f", row < c), ("b", row > c)):
        put(f"mk_{d}", np.concatenate([same & less, same & (less | (row == c))], 1).astype(f))
    levels = range(LEVELS)
    put("between", np.concatenate([((row >> (l + 1)) == (c >> (l + 1))) & ((row >> l) != (c >> l)) for l in levels], 1).astype(f))
    put("chosen", np.concatenate([((row >> l) == (c >> l)) & np.where((row >> l) % 2 == 1, row <= c, row >= c) for l in levels], 1).astype(f))
    put("chunk", np.tile((np.arange(T) % C != 0).astype(f), (P, 1)))

    def order(L):
        return np.concatenate([np.arange(0, L, 2), np.arange(1, L, 2)]) if L == LS else np.arange(L)

    feats, decay = [], []
    lo, hi = np.log(1e-2) / 1.5, np.log(1e-2) / 0.3
    deltas = np.abs(np.linspace(lo, hi, E))
    for L in (LS, LP):
        pos = order(L).astype(np.float64)[:, None]
        t = pos / (L - 1)
        ang = (2 * np.pi / L) * pos * np.linspace(1e-4, 15, 16)[None, :]
        feats.append(np.concatenate([t, np.cos(ang), -np.sin(ang)], 1).T)
        decay.append(np.exp(-t * deltas))
    dft = np.zeros((P, DFT_N), np.float64)
    k = np.arange(LS // 2)
    i = np.arange(LS // 2)
    fwd, inv = [], []
    for fn in (np.cos, np.sin):
        for par in range(2):
            m = fn(np.pi * (2 * k[None, :] + 1) * (2 * i[:, None] + par) / (2 * LS))
            fwd.append(m.reshape(2, P, 256).transpose(1, 0, 2).reshape(P, 512))
            inv.append((m.T / LS).reshape(2, P, 256).transpose(1, 0, 2).reshape(P, 512))
    dft[:, slice(*DFT["fwd"])] = np.concatenate(fwd, 1)
    dft[:, slice(*DFT["inv"])] = np.concatenate(inv, 1)
    k = np.arange(LP)
    mp = [fn(np.pi * (2 * k[None, :] + 1) * k[:, None] / (2 * LP)) for fn in (np.cos, np.sin)]
    dft[:, slice(*DFT["fwdp"])] = np.concatenate(mp, 1)
    dft[:, slice(*DFT["invp"])] = np.concatenate([m.T / LP for m in mp], 1)
    return {"tab": tab.astype(f), "dft": dft.astype(f), "feats": np.concatenate(feats, 1).astype(f), "decay": np.concatenate(decay, 0).astype(f)}


STAGE = 2
SCRATCH = {"vx_d": [2, T, E], "g_d": [E, T], "y_d": [E, T], "x1_d": [T, D], "gate_d": [2, 2, D], "rkvz_d": [4, E, T]}
OUTS = {"y_prompt": [1, LP, D], "y_sample": [1, LS, D], "new_state_fwd": [1, 1, 32, 64, 64], "new_state_bwd": [1, 1, 32, 64, 64]}


def build(nc, shapes, marks, debug=()):
    A = {n: nc.dram_tensor(f"in_{n}", list(s), F32, kind="ExternalInput").ap() for n, s in shapes.items()}
    for n, s in SCRATCH.items():
        A[n] = nc.dram_tensor(f"scratch_{n}", s, F32, kind="ExternalOutput" if n in debug else "Internal").ap()
    for n, s in OUTS.items():
        A[n] = nc.dram_tensor(f"out_{n}", s, F32, kind="ExternalOutput").ap()
    program(nc, A, marks)


def kernel(**inputs):
    import concourse.bacc as bacc
    from concourse.bass_utils import run_bass_kernel_spmd

    arrays = {n: np.ascontiguousarray(a) for n, a in inputs.items()}
    arrays.update(constants())
    shapes = {n: a.shape for n, a in arrays.items()}
    marks = {}
    build(bacc.Bacc("TRN2", target_bir_lowering=False, num_devices=1), shapes, marks)
    marks["counted"] = True
    nc = bacc.Bacc("TRN2", target_bir_lowering=False, num_devices=1)
    build(nc, shapes, marks)
    r = run_bass_kernel_spmd(nc, [{f"in_{n}": a for n, a in arrays.items()}], core_ids=[0]).results[0]
    return tuple(r[f"out_{n}"] for n in OUTS)
```

```python
import concourse.bass as bass
from concourse import mybir
from contextlib import ExitStack
import numpy as np

F32 = mybir.dt.float32
ALU = mybir.AluOpType
ACT = mybir.ActivationFunctionType
MUL, ADD, SUB = ALU.mult, ALU.add, ALU.subtract

P = 128
D = 1024
E = 2048
LS, LP = 512, 128
T = LS + LP
NT = T // P
KD = D // P
KE = E // P
GRID = 64
ROWS = LS // GRID
HID = 64
EMB = 33
C = 64
NC = T // C
CS = LS // C
LEVELS = 6
CB = 512
NB = E // CB
EPS = 1e-6
GN_EPS = 64e-5
DECAY_MAX = float(np.exp(-0.5))

TAB = {}
_at = 0
for _name, _n in (("ident", P), ("heads", P), ("mk_f", 2 * P), ("mk_b", 2 * P),
                  ("between", LEVELS * P), ("chosen", LEVELS * P), ("chunk", T)):
    TAB[_name] = (_at, _at + _n)
    _at += _n
TAB_N = _at
DFT = {}
_at = 0
for _name, _n in (("fwd", 4 * 2 * 256), ("inv", 4 * 2 * 256), ("fwdp", 2 * P), ("invp", 2 * P)):
    DFT[_name] = (_at, _at + _n)
    _at += _n
DFT_N = _at


class Steps:

    def __init__(self, nc, stack, name, marks, by=1):
        self.sem = stack.enter_context(nc.semaphore(name))
        self.name, self.marks, self.n, self.by = name, marks, 0, by

    def note(self, label):
        if not self.marks.get("counted"):
            self.marks[self.name, label] = self.n

    def per(self):
        return self.marks.get((self.name, "round"), 0)

    def did(self, ins, label=None):
        ins.then_inc(self.sem, self.by)
        self.n += self.by
        if not self.marks.get("counted"):
            self.marks[self.name, "round"] = max(self.n, self.per())
            if label is not None:
                self.marks[self.name, label] = self.n
        return ins

    def mark(self, label):
        return self.marks.get((self.name, label), 0)

    def now(self, label, i=None):
        return self.mark(label) if i is None else i * self.per() + (self.per() + self.mark(label))

    def before(self, label, i):
        return i * self.per() + self.mark(label)

    def here(self, i=None):
        return self.n if i is None else i * self.per() + (self.per() + self.n)

    def start(self, eng):
        if self.per():
            eng.sem_inc(self.sem, self.per())


def make_ops(nc):
    def mm(out, lhsT, rhs, first=True, last=True):
        return nc.tensor.matmul(out, lhsT, rhs, start=first, stop=last)

    def stt(out, in0, scalar, in1, op0, op1):
        return nc.vector.scalar_tensor_tensor(out=out, in0=in0, scalar=scalar, in1=in1, op0=op0, op1=op1)

    def ts(out, in0, s1, s2, op0, op1=None):
        if op1 is None:
            return nc.vector.tensor_scalar(out, in0, s1, None, op0)
        return nc.vector.tensor_scalar(out, in0, s1, s2, op0, op1)

    def tt(out, a, b, op):
        return nc.vector.tensor_tensor(out, a, b, op)

    def act(out, in_, f, **kw):
        return nc.scalar.activation(out, in_, f, **kw)

    return mm, stt, ts, tt, act


def modulation(nc, A, G, M):
    mm, stt, ts, tt, act = make_ops(nc)
    ps, tab, col = G["ps"], G["tab"], G["col"]
    with ExitStack() as st:
        sb = lambda n, s: st.enter_context(nc.sbuf_tensor(n, s, F32))
        crow, csig, condT = sb("crow", [16, P]), sb("csig", [16, P]), sb("condT", [P, 16])
        rows = sb("vrows", [P, 4, P])
        frow = sb("frow", [4, HID])
        RING = 3
        aw = sb("aw", [P, RING, 3 * D])
        mrow = sb("mrow", [2, 2, 3 * D])
        abrow = sb("abrow", [2, 2, 3 * D])
        prow = sb("prow", [2, 2, D])
        s_small = st.enter_context(nc.semaphore("mod_vectors_loaded"))
        s_tab = st.enter_context(nc.semaphore("mod_tables_loaded"))
        s_aw = [st.enter_context(nc.semaphore(f"mod_weights_{k}")) for k in range(RING)]
        s_out = st.enter_context(nc.semaphore("mod_gate_stored"))
        pe_, ac_, dv_ = (Steps(nc, st, f"mod_{n}", M) for n in ("pe", "act", "dve"))
        nload = [0]

        with nc.Block() as block:
            @block.sync
            def _(sp):
                def small(dst, src):
                    sp.dma_start(dst, src).then_inc(s_small, 16)
                    nload[0] += 16
                nload[0] = 0
                sp.dma_start(tab[:, :], A["tab"]).then_inc(s_tab, 16)
                small(crow[0:8, :], A["c"].rearrange("a (k p) -> (a k) p", p=P))
                small(crow[8:16, :], A["c_ctx"].rearrange("(k p) -> k p", p=P))
                at = 0
                for a, n in ((A["norm_pre"].rearrange("l (k p) -> (l k) p", p=P), 16),
                             (A["hy_b_in"].rearrange("l (k p) -> (l k) p", p=P), 64),
                             (A["rw_mu"].rearrange("l m (k p) -> (l m k) p", p=P), 48),
                             (A["hy_conv_w"].rearrange("l j (k p) -> (l j k) p", p=P)[0:96, :], 96),
                             (None, 32),
                             (A["hy_conv_w"].rearrange("l j (k p) -> (l j k) p", p=P)[96:144, :], 48),
                             (A["hy_conv_b"].rearrange("l (k p) -> (l k) p", p=P), 48),
                             (A["rw_w0"].rearrange("l z (k p) -> (l z k) p", p=P), 32),
                             (A["rw_a0"].rearrange("l z (k p) -> (l z k) p", p=P), 32),
                             (A["rw_k_k"].rearrange("l (k p) -> (l k) p", p=P), 16),
                             (A["rw_k_a"].rearrange("l (k p) -> (l k) p", p=P), 16),
                             (A["rw_r_k"].rearrange("l z (k h) n -> (l z k) (h n)", h=2), 32),
                             (A["rw_gn_w"].rearrange("l (k p) -> (l k) p", p=P), 16),
                             (A["rw_gn_b"].rearrange("l (k p) -> (l k) p", p=P), 16)):
                    g, r = at // P, at % P
                    if a is not None:
                        small(rows[r:r + n, g, :], a)
                    else:
                        small(rows[r:r + n, g, :], A["hy_conv_b"].rearrange("l (k p) -> (l k) p", p=P)[0:n, :])
                    at += n
                for k, n in enumerate(("hy_f_b1", "hy_f_b2", "hy_f_b3", "hy_f_freq")):
                    small(frow[k:k + 1, :], A[n])
                for l in range(2):
                    for c in range(2):
                        small(abrow[c:c + 1, l, :], A["ada_b"][l:l + 1, :])
                        small(prow[c:c + 1, l, :], A["norm_post"][l:l + 1, :])
                for n in range(2 * KD):
                    l, k = n // KD, n % KD
                    if n >= RING:
                        sp.wait_ge(pe_.sem, pe_.now(("ada", n - RING)))
                    sp.dma_start(aw[:, n % RING, :], A["ada_w"][l, k * P:(k + 1) * P, :]).then_inc(s_aw[n % RING], 16)
                for l in range(2):
                    sp.wait_ge(dv_.sem, dv_.now(("gate", l)))
                    sp.dma_start(A["gate_d"][l], mrow[:, l, 2 * D:3 * D]).then_inc(s_out, 16)
                sp.wait_ge(s_out, 32)

            @block.scalar
            def _(a):
                a.wait_ge(s_small, nload[0])
                ac_.did(act(csig[:, :], crow[:, :], ACT.Sigmoid), "csig")

            @block.tensor
            def _(pe):
                pe.wait_ge(s_tab, 16)
                pe.wait_ge(s_small, nload[0])
                ident = tab[:, TAB["ident"][0]:TAB["ident"][1]]
                for g in range(4):
                    last = nc.tensor.transpose(ps[:, 6, g * P:(g + 1) * P], rows[:, g, :], ident)
                pe_.did(last, "cols")
                last = nc.tensor.transpose(ps[0:HID, 7, 0:4], frow[:, :], ident[0:4, 0:4])
                pe_.did(last, "fcols")
                pe.wait_ge(dv_.sem, dv_.now("fcols"))
                pe_.did(nc.tensor.transpose(ps[:, 7, 16:32], crow[:, :], ident[0:16, 0:16]), "condT")
                pe.wait_ge(dv_.sem, dv_.now("condT"))
                for l in range(2):
                    if l:
                        pe.wait_ge(dv_.sem, dv_.now(("row", l - 1)))
                    for k in range(KD):
                        n = l * KD + k
                        pe.wait_ge(s_aw[n % RING], 16 * (n // RING + 1))
                        for b in range(6):
                            last = mm(ps[0:2, b, :], condT[:, k:16:KD], aw[:, n % RING, b * 512:(b + 1) * 512], k == 0, k == KD - 1)
                        pe_.did(last, ("ada", n))
                    pe.wait_ge(dv_.sem, dv_.now(("row", l)))
                    if l:
                        pe.wait_ge(dv_.sem, dv_.now(("mcols", l - 1)))
                    for j in range(16):
                        last = nc.tensor.transpose(ps[:, 7, 64 + 2 * j:66 + 2 * j], mrow[:, l, j * P:(j + 1) * P], ident[0:2, 0:2])
                    pe_.did(last, ("mcols", l))

            @block.vector
            def _(v):
                def link(ins, label=None):
                    dv_.did(ins, label)
                    v.wait_ge(dv_.sem, dv_.here())
                v.wait_ge(ac_.sem, ac_.now("csig"))
                dv_.did(tt(crow[:, :], crow[:, :], csig[:, :], MUL), "silu")
                v.wait_ge(pe_.sem, pe_.now("cols"))
                dv_.did(nc.vector.tensor_copy(col[:, :, :], ps[:, 6, :].rearrange("p (g n) -> p g n", g=4)), "cols")
                v.wait_ge(pe_.sem, pe_.now("fcols"))
                dv_.did(nc.vector.tensor_copy(G["fcol"][:, :], ps[0:HID, 7, 0:4]), "fcols")
                v.wait_ge(pe_.sem, pe_.now("condT"))
                link(nc.vector.tensor_copy(condT[:, :], ps[:, 7, 16:32]), "condT")
                npre = col[:, 0, 0:16].rearrange("p (l k) -> p l k", l=2)
                for l in range(2):
                    v.wait_ge(pe_.sem, pe_.now(("ada", l * KD + KD - 1)))
                    link(tt(mrow[:, l, :], ps[0:2, 0:6, :].rearrange("p b n -> p (b n)"), abrow[:, l, :], ADD), ("row", l))
                    dv_.did(tt(mrow[:, l, 2 * D:3 * D], mrow[:, l, 2 * D:3 * D], prow[:, l, :], MUL), ("gate", l))
                    v.wait_ge(pe_.sem, pe_.now(("mcols", l)))
                    mc = ps[:, 7, 64:96].rearrange("p (j c) -> p j c", c=2)
                    dv_.did(nc.vector.tensor_copy(G["shf"][:, l, :, :], mc[:, 0:8, :]))
                    for c in range(2):
                        last = dv_.did(stt(G["scl"][:, l, :, c], mc[:, 8:16, c], 1.0, npre[:, l, :], ADD, MUL), ("mcols", l))


def load_norm(nc, A, G, M, l, hT, x):
    mm, stt, ts, tt, act = make_ops(nc)
    ps, tab = G["ps"], G["tab"]
    with ExitStack() as st:
        sb = lambda n, s: st.enter_context(nc.sbuf_tensor(f"{n}{l}", s, F32))
        sq, ss, rs = sb("nsq", [P, D]), sb("nss", [P, NT]), sb("nrs", [P, NT])
        sx = [st.enter_context(nc.semaphore(f"norm{l}_x{j}")) for j in range(NT)]
        pe_, ac_, dv_ = (Steps(nc, st, f"norm{l}_{n}", M) for n in ("pe", "act", "dve"))
        with nc.Block() as block:
            @block.sync
            def _(sp):
                if l == 0:
                    for j in range(NT):
                        src = A["x_sample"][0, j * P:(j + 1) * P, :] if j < 4 else A["x_prompt"][0, :, :]
                        sp.dma_start(x[:, j, :], src).then_inc(sx[j], 16)

            @block.scalar
            def _(a):
                for j in range(NT):
                    if l == 0:
                        a.wait_ge(sx[j], 16)
                    if j:
                        a.wait_ge(ac_.sem, ac_.here())
                    ac_.did(act(sq[:, :], x[:, j, :], ACT.Square, accum_out=ss[:, j:j + 1]), ("ss", j))
                a.wait_ge(dv_.sem, dv_.now("var"))
                ac_.did(act(rs[:, :], ss[:, :], ACT.Sqrt), "std")
                for k in range(KD):
                    a.wait_ge(pe_.sem, pe_.now(("tr", k)))
                    kw = lambda c: dict(scale=G["scl"][:, l, k, c:c + 1], bias=G["shf"][:, l, k, c:c + 1])
                    act(hT[:, k, 0:LS], ps[:, 2 * (k % 2), :], ACT.Identity, **kw(0))
                    ac_.did(act(hT[:, k, LS:T], ps[:, 2 * (k % 2) + 1, 0:LP], ACT.Identity, **kw(1)), ("h", k))

            @block.vector
            def _(v):
                def link(ins, label=None):
                    dv_.did(ins, label)
                    v.wait_ge(dv_.sem, dv_.here())
                v.wait_ge(ac_.sem, ac_.now(("ss", NT - 1)))
                dv_.did(ts(ss[:, :], ss[:, :], 1.0 / D, EPS, MUL, ADD), "var")
                v.wait_ge(ac_.sem, ac_.now("std"))
                link(nc.vector.reciprocal(rs[:, :], rs[:, :]))
                for j in range(NT):
                    dv_.did(ts(x[:, j, :], x[:, j, :], rs[:, j:j + 1], None, MUL), ("xn", j))

            @block.tensor
            def _(pe):
                ident = tab[:, TAB["ident"][0]:TAB["ident"][1]]
                pe.wait_ge(dv_.sem, dv_.now(("xn", NT - 1)))
                for k in range(KD):
                    if k >= 2:
                        pe.wait_ge(ac_.sem, ac_.now(("h", k - 2)))
                    for j in range(NT):
                        last = nc.tensor.transpose(ps[:, 2 * (k % 2) + j // 4, (j % 4) * P:(j % 4 + 1) * P], x[:, j, k * P:(k + 1) * P], ident)
                    pe_.did(last, ("tr", k))


def filter_hidden(nc, A, G, M):
    mm, stt, ts, tt, act = make_ops(nc)
    ps, tab, fcol, hid = G["ps"], G["tab"], G["fcol"], G["hid"]
    ROUND = 1.5 * 2 ** 23
    HI = 6.28125
    LO = 2 * np.pi - HI
    with ExitStack() as st:
        sb = lambda n, s: st.enter_context(nc.sbuf_tensor(n, s, F32))
        w = [sb("fw1", [EMB, HID]), sb("fw2", [HID, HID]), sb("fw3", [HID, HID])]
        feats = sb("feats", [EMB, T])
        arg, turn = sb("farg", [HID, T]), sb("fturn", [HID, T])
        s_w = st.enter_context(nc.semaphore("filter_weights_loaded"))
        pe_, ac_, dv_ = (Steps(nc, st, f"filter_{n}", M) for n in ("pe", "act", "dve"))
        psv = ps[0:HID, 0:2, :].rearrange("p b n -> p (b n)")
        with nc.Block() as block:
            @block.sync
            def _(sp):
                for k in range(3):
                    sp.dma_start(w[k][:, :], A[f"hy_f_w{k + 1}"][0]).then_inc(s_w, 16)
                sp.dma_start(feats[:, :], A["feats"]).then_inc(s_w, 16)

            @block.tensor
            def _(pe):
                pe.wait_ge(s_w, 64)
                for k in range(3):
                    src = feats[:, :] if k == 0 else hid[:, :]
                    if k:
                        pe.wait_ge(ac_.sem, ac_.now(("sin", k - 1)))
                    mm(psv[:, 0:LS], w[k][:, :], src[:, 0:LS])
                    pe_.did(mm(psv[:, LS:T], w[k][:, :], src[:, LS:T]), ("mm", k))

            @block.vector
            def _(v):
                def link(ins, label=None):
                    dv_.did(ins, label)
                    v.wait_ge(dv_.sem, dv_.here())
                for k in range(3):
                    v.wait_ge(pe_.sem, pe_.now(("mm", k)))
                    if k:
                        v.wait_ge(ac_.sem, ac_.now(("sin", k - 1)))
                    link(ts(arg[:, :], psv[:, 0:T], fcol[:, k:k + 1], fcol[:, 3:4], ADD, MUL))
                    link(ts(turn[:, :], arg[:, :], 1 / (2 * np.pi), ROUND, MUL, ADD))
                    link(ts(turn[:, :], turn[:, :], ROUND, None, SUB))
                    link(stt(arg[:, :], turn[:, :], -HI, arg[:, :], MUL, ADD))
                    link(stt(arg[:, :], turn[:, :], -LO, arg[:, :], MUL, ADD))
                    link(ts(arg[:, :], arg[:, :], 3.1415925, -3.1415925, ALU.min, ALU.max), ("arg", k))

            @block.scalar
            def _(a):
                for k in range(3):
                    a.wait_ge(dv_.sem, dv_.now(("arg", k)))
                    ac_.did(act(hid[:, :], arg[:, :], ACT.Sin), ("sin", k))


def hyena_in(nc, A, G, M, hT):
    mm, stt, ts, tt, act = make_ops(nc)
    ps, tab, col = G["ps"], G["tab"], G["col"]
    w_v = A["hy_w_in"][0].rearrange("(k p) n -> p k n", p=P)
    pair = [ps[:, 2 * q:2 * q + 2, :].rearrange("p b n -> p (b n)") for q in range(4)]
    with ExitStack() as st:
        sb = lambda n, s: st.enter_context(nc.sbuf_tensor(n, s, F32))
        w = [sb(f"hw{s}", [P, KD, P]) for s in range(4)]
        PADN = LS + LP + 3
        pad = [sb(f"hpad{s}", [P, PADN]) for s in range(3)]
        cv = [sb(f"hcv{s}", [P, T + 1]) for s in range(3)]
        out_t = [sb(f"hot{s}", [P, NT, P]) for s in range(2)]
        zsig, z, g = sb("hzs", [P, T]), sb("hz", [P, T]), sb("hg", [P, T])
        pc = sb("hpc", [P, 16])
        s_w = [st.enter_context(nc.semaphore(f"hy_weights_{s}")) for s in range(4)]
        s_o = [st.enter_context(nc.semaphore(f"hy_stored_{s}")) for s in range(3)]
        s_f = [st.enter_context(nc.semaphore(f"hy_store_buffer_free_{s}")) for s in range(3)]
        s_z = st.enter_context(nc.semaphore("hy_pad_cleared"))
        pe_, ac_, dv_ = (Steps(nc, st, f"hyin_{n}", M) for n in ("pe", "act", "dve"))
        with nc.Block() as block:
            @block.sync
            def _(sp):
                with sp.Fori(0, KE) as i:
                    for s in range(4):
                        sp.wait_ge(pe_.sem, pe_.before(("proj", s), i))
                        sp.dma_start(w[s][:, :, :], w_v[:, :, bass.ds(i * P + s * E, P)]).then_inc(s_w[s], 16)

            @block.gpsimd
            def _(po):
                for s in range(3):
                    nc.gpsimd.memset(pad[s][:, :], 0.0).then_inc(s_z, 1)
                    po.sem_inc(s_f[s], 1)
                with po.Fori(0, KE) as i:
                    for s in range(2):
                        po.wait_ge(ac_.sem, ac_.now(("vt", s), i))
                        po.dma_start(A["vx_d"][s].rearrange("(j p) n -> p j n", p=P)[:, :, bass.ds(i * P, P)], out_t[s][:, :, :]).then_inc(s_o[s], 16)
                    po.wait_ge(dv_.sem, dv_.now("g", i))
                    po.dma_start(A["g_d"][bass.ds(i * P, P), :], g[:, :]).then_inc(s_o[2], 16)
                    for s in range(3):
                        po.wait_ge(s_o[s], i * 16 + 16)
                        po.sem_inc(s_f[s], 1)
                for s in range(3):
                    po.wait_ge(s_o[s], 16 * KE)

            @block.tensor
            def _(pe):
                ident = tab[:, TAB["ident"][0]:TAB["ident"][1]]
                pe_.start(pe)

                def transpose(s, i):
                    pe.wait_ge(dv_.sem, dv_.now(("conv", s), i))
                    pe.wait_ge(ac_.sem, ac_.before(("vt", s), i))
                    for j in range(NT):
                        src = cv[s][:, j // 2 + 2 * P * (j % 2):min(j // 2 + 2 * P * (j % 2) + 2 * P, LS):2] if j < 4 else cv[s][:, LS + 1:T + 1]
                        last = nc.tensor.transpose(pair[2 + s][:, j * P:(j + 1) * P], src, ident)
                    pe_.did(last, ("tr", s))

                with pe.Fori(0, KE) as i:
                    for s in range(4):
                        pe.wait_ge(s_w[s], i * 16 + 16)
                        if s >= 2:
                            pe.wait_ge(ac_.sem, ac_.now(("pad", s - 2), i))
                        elif s == 0:
                            pe.wait_ge(ac_.sem, ac_.before(("pad", 2), i))
                        else:
                            pe.wait_ge(dv_.sem, dv_.before("z", i))
                        for k in range(KD):
                            mm(pair[s % 2][:, 0:LS], w[s][:, k, :], hT[:, k, 0:LS], k == 0, k == KD - 1)
                            last = mm(pair[s % 2][:, LS:T], w[s][:, k, :], hT[:, k, LS:T], k == 0, k == KD - 1)
                        pe_.did(last, ("proj", s))
                        if s in (1, 2):
                            transpose(s - 1, i)

            @block.scalar
            def _(a):
                ac_.start(a)
                a.wait_ge(s_z, 3)
                with a.Fori(0, KE) as i:
                    def to_pad(s):
                        a.wait_ge(pe_.sem, pe_.now(("proj", s), i))
                        a.wait_ge(dv_.sem, dv_.before(("conv", s), i))
                        act(pad[s][:, 1:LS + 1], pair[s % 2][:, 0:LS], ACT.Identity, bias=pc[:, s:s + 1])
                        ac_.did(act(pad[s][:, LS + 2:T + 2], pair[s % 2][:, LS:T], ACT.Identity, bias=pc[:, s:s + 1]), ("pad", s))

                    def turned(s):
                        a.wait_ge(pe_.sem, pe_.now(("tr", s), i))
                        a.wait_ge(s_f[s], i + 1)
                        ac_.did(act(out_t[s][:, :, :].rearrange("p j n -> p (j n)"), pair[2 + s][:, 0:T], ACT.Copy), ("vt", s))

                    a.wait_ge(dv_.sem, dv_.now("pc", i))
                    to_pad(0)
                    to_pad(1)
                    turned(0)
                    to_pad(2)
                    turned(1)
                    a.wait_ge(pe_.sem, pe_.now(("proj", 3), i))
                    a.wait_ge(dv_.sem, dv_.before("z", i))
                    ac_.did(act(zsig[:, :], pair[1][:, 0:T], ACT.Sigmoid, bias=pc[:, 3:4]), "zs")

            @block.vector
            def _(v):
                dv_.start(v)
                bin_c = col[:, 0, 16:80].rearrange("p (s k) -> p s k", s=4)
                cw01 = col[:, 1, 0:96].rearrange("p (j k) -> p j k", k=KE)
                cwb = col[:, 2, 0:96].rearrange("p (j k) -> p j k", k=KE)
                with v.Fori(0, KE) as i:
                    def link(ins, label=None):
                        dv_.did(ins, label)
                        v.wait_ge(dv_.sem, dv_.here(i))
                    v.wait_ge(ac_.sem, ac_.before("zs", i))
                    nc.vector.tensor_copy(pc[:, 0:4], bin_c[:, :, bass.ds(i, 1)].rearrange("p s o -> p (s o)"))
                    nc.vector.tensor_copy(pc[:, 4:10], cw01[:, :, bass.ds(i, 1)].rearrange("p s o -> p (s o)"))
                    link(nc.vector.tensor_copy(pc[:, 10:16], cwb[:, :, bass.ds(i, 1)].rearrange("p s o -> p (s o)")), "pc")
                    for s in range(3):
                        v.wait_ge(ac_.sem, ac_.now(("pad", s), i))
                        if s < 2:
                            v.wait_ge(pe_.sem, pe_.before(("tr", s), i))
                        link(ts(cv[s][:, :], pad[s][:, 1:T + 2], pc[:, 7 + s:8 + s], pc[:, 13 + s:14 + s], MUL, ADD))
                        link(stt(cv[s][:, :], pad[s][:, 0:T + 1], pc[:, 4 + s:5 + s], cv[s][:, :], MUL, ADD))
                        link(stt(cv[s][:, :], pad[s][:, 2:T + 3], pc[:, 10 + s:11 + s], cv[s][:, :], MUL, ADD), ("conv", s))
                    v.wait_ge(ac_.sem, ac_.now("zs", i))
                    link(stt(z[:, :], pair[1][:, 0:T], pc[:, 3:4], zsig[:, :], ADD, MUL), "z")
                    v.wait_ge(s_f[2], i + 1)
                    dv_.did(tt(g[:, 0:LS], z[:, 0:LS], cv[2][:, 0:LS], MUL))
                    dv_.did(tt(g[:, LS:T], z[:, LS:T], cv[2][:, LS + 1:T + 1], MUL), "g")


def hyena_conv(nc, A, G, M):
    mm, stt, ts, tt, act = make_ops(nc)
    ps, hid = G["ps"], G["hid"]
    pair = [ps[:, 2 * q:2 * q + 2, :] for q in range(4)]
    w4_v = A["hy_f_w4"][0].rearrange("k (g n) -> k g n", g=4)
    first = [("filt", 0, j) for j in range(NT)] + [("fix", 0)] + [("H", 0, q) for q in range(5)]
    own = [("X", 0, q) for q in range(5)] + [("filt", 1, j) for j in range(NT)] + [("fix", 1)] + [("H", 1, q) for q in range(5)] \
        + [("inv", 0, q) for q in range(3)] + [("X", 1, q) for q in range(5)]
    last_ = [("inv", 1, q) for q in range(4)]
    JOBS = own + first + last_
    slot = {job: n % 4 for n, job in enumerate(JOBS)}
    SAVED = [j for j in JOBS if j[0] in ("H", "X") and j[2] < 4]
    side = {job: n % 2 for n, job in enumerate(SAVED)}
    is_next = lambda job: job[0] in ("filt", "fix", "H") and job[1] == 0
    with ExitStack() as st:
        sb = lambda n, s: st.enter_context(nc.sbuf_tensor(n, s, F32))
        dft = sb("dft", [P, DFT_N])
        vx = [sb("cv_v", [P, NT, CB]), sb("cv_x1", [P, NT, CB])]
        w4 = sb("w4", [HID, 4, CB])
        wsd = sb("wsd", [HID, 2, CB])
        dec = sb("dec", [P, NT, CB])
        bias = sb("fbias", [1, 2, CB])
        g = sb("cg", [P, 4, T])
        hsd = sb("hsd", [P, 2, NT, CB])
        H = [sb(f"H{o}", [P, 2, NT, CB]) for o in range(2)]
        X = sb("X", [P, 2, NT, CB])
        Y = sb("Y", [P, 2, 2, CB])
        Yp = sb("Yp", [P, 2, 1, CB])
        tmp = sb("ctmp", [P, 2, CB])
        skip_row = sb("skip_row", [1, CB])
        osave = sb("osave", [P, 2, CB])
        yout = sb("yout", [P, 4, T])
        fwd = dft[:, DFT["fwd"][0]:DFT["fwd"][1]].rearrange("p (m t k) -> p m t k", m=4, t=2)
        inv = dft[:, DFT["inv"][0]:DFT["inv"][1]].rearrange("p (m k t) -> p m k t", m=4, k=2)
        fwdp = dft[:, DFT["fwdp"][0]:DFT["fwdp"][1]].rearrange("p (m k) -> p m k", m=2)
        invp = dft[:, DFT["invp"][0]:DFT["invp"][1]].rearrange("p (m t) -> p m t", m=2)
        loads = ("v", "x1", "w4", "dec", "bias", "g")
        s_l = {n: st.enter_context(nc.semaphore(f"conv_loaded_{n}")) for n in loads}
        s_dft = st.enter_context(nc.semaphore("conv_dft_loaded"))
        s_y = st.enter_context(nc.semaphore("conv_stored"))
        s_f = st.enter_context(nc.semaphore("conv_store_buffer_free"))
        own_ = {n: Steps(nc, st, f"conv_{n}", M) for n in ("pe", "act", "dve")}
        nxt_ = {n: Steps(nc, st, f"conv_first_{n}", M) for n in ("pe", "act", "dve")}
        of = lambda eng, job, i: (nxt_[eng], i + 1) if is_next(job) else (own_[eng], i)
        pe_, ac_, dv_ = own_["pe"], own_["act"], own_["dve"]
        fpe, fdv = nxt_["pe"], nxt_["dve"]

        def wait_job(eng, of_engine, job, i, label=None):
            steps, index = of(of_engine, job, i)
            eng.wait_ge(steps.sem, steps.now(job if label is None else label, index))

        def blocks(eng, body):
            with eng.Fori(0, NB - 1) as i:
                body(i, own + first + last_)
            body(NB - 1, own + last_)

        def before(jobs, n, place):
            found = [j for j in jobs[:n] if place(j) == place(jobs[n])]
            return found[-1] if found else None

        with nc.Block() as block:
            @block.sync
            def _(sp):
                def load_filter(j):
                    cs = bass.ds(j * CB, CB)
                    sp.dma_start(w4[:, :, :], w4_v[:, :, cs]).then_inc(s_l["w4"], 16)
                    sp.dma_start(dec[:, :, :], A["decay"].rearrange("(j p) n -> p j n", p=P)[:, :, cs]).then_inc(s_l["dec"], 16)
                    sp.dma_start(bias[:, :, :], A["hy_fft_bias"][:, :, cs]).then_inc(s_l["bias"], 16)

                def load_stream(j, s_, n):
                    src = A["vx_d"][s_].rearrange("(j p) n -> p j n", p=P)[:, :, bass.ds(j * CB, CB)]
                    sp.dma_start(vx[s_][:, :, :], src).then_inc(s_l[n], 16)

                def load_gate(j):
                    sp.dma_start(g[:, :, :], A["g_d"][bass.ds(j * CB, CB), :].rearrange("(c p) t -> p c t", p=P)).then_inc(s_l["g"], 16)
                load_filter(0)
                sp.dma_start(dft[:, :], A["dft"]).then_inc(s_dft, 16)
                load_stream(0, 0, "v")
                load_stream(0, 1, "x1")
                load_gate(0)
                with sp.Fori(0, NB - 1) as i:
                    sp.wait_ge(dv_.sem, dv_.now(("ev", ("fix", 1)), i))
                    load_filter(i + 1)
                    sp.wait_ge(dv_.sem, dv_.now(("ev", ("inv", 0, 2)), i))
                    load_stream(i + 1, 1, "x1")
                    sp.wait_ge(pe_.sem, pe_.now(("X", 1, 4), i))
                    load_stream(i + 1, 0, "v")
                    sp.wait_ge(dv_.sem, dv_.now(("ev", ("inv", 1, 3)), i))
                    load_gate(i + 1)

            @block.gpsimd
            def _(po):
                po.sem_inc(s_f, 1)
                with po.Fori(0, NB) as i:
                    po.wait_ge(dv_.sem, dv_.now(("ev", ("inv", 1, 3)), i))
                    po.dma_start(A["y_d"][bass.ds(i * CB, CB), :].rearrange("(c p) t -> p c t", p=P), yout[:, :, :]).then_inc(s_y, 16)
                    po.wait_ge(s_y, i * 16 + 16)
                    po.sem_inc(s_f, 1)
                po.wait_ge(s_y, 16 * NB)

            @block.tensor
            def _(pe):
                pe_.start(pe)
                fpe.start(pe)

                def make(job, i):
                    q = pair[slot[job]]
                    kind, o = job[0], job[1]
                    if kind == "filt":
                        j = job[2]
                        if j == 0:
                            wait_job(pe, "dve", job, i, ("w", o))
                        mm(q[:, 0, :], hid[:, j * P:(j + 1) * P], wsd[:, 0, :])
                        last = mm(q[:, 1, :], hid[:, j * P:(j + 1) * P], wsd[:, 1, :])
                    elif kind == "fix":
                        last = mm(q[:, 0, :], hid[:, 0:P], w4[:, 2 + o, :])
                    elif kind in ("H", "X"):
                        m = job[2]
                        if kind == "H":
                            src = [hsd[:, 0, :, :], hsd[:, 1, :, :]]
                            wait_job(pe, "dve", job, i, ("row0", o))
                        else:
                            src = [vx[0][:, :, :]] * 2
                            if o == 1:
                                pe.wait_ge(dv_.sem, dv_.now(("ev", ("inv", 0, 2)), i))
                            elif m == 0:
                                pe.wait_ge(s_l["v"], i * 16 + 16)
                        if m < 4:
                            kt, cs = m // 2, m % 2
                            for par in range(2):
                                for t in range(2):
                                    last = mm(q[:, par, :], fwd[:, 2 * cs + par, t, kt * P:(kt + 1) * P], src[cs][:, 2 * par + t, :], t == 0, t == 1)
                        else:
                            for cs in range(2):
                                last = mm(q[:, cs, :], fwdp[:, cs, :], src[cs][:, 4, :])
                    elif o == 0:
                        m = job[2]
                        pe.wait_ge(dv_.sem, dv_.now(("comb", 0, 1 if m < 2 else 2), i))
                        if m < 2:
                            for h in range(2):
                                for kt in range(2):
                                    for cs in range(2):
                                        last = mm(q[:, h, :], inv[:, 2 * cs + m, kt, h * P:(h + 1) * P], X[:, cs, 2 * m + kt, :], kt + cs == 0, kt + cs == 2)
                        else:
                            for cs in range(2):
                                last = mm(q[:, 0, :], invp[:, cs, :], Yp[:, cs, 0, :], cs == 0, cs == 1)
                    else:
                        ch = slice(job[2] * P, (job[2] + 1) * P)
                        pe.wait_ge(dv_.sem, dv_.now(("comb", 1, 2), i))
                        for par in range(2):
                            for kt in range(2):
                                for cs in range(2):
                                    mm(q[:, 0, par * 256:(par + 1) * 256], X[:, cs, 2 * par + kt, ch], inv[:, 2 * cs + par, kt, :], kt + cs == 0, kt + cs == 2)
                        for cs in range(2):
                            last = mm(q[:, 1, 0:P], Yp[:, cs, 0, ch], invp[:, cs, :], cs == 0, cs == 1)
                    of("pe", job, i)[0].did(last, job)

                def body(i, jobs):
                    pe_.n = fpe.n = 0
                    for n, job in enumerate(jobs):
                        p_ = before(jobs, n, slot.get)
                        if p_:
                            wait_job(pe, "dve", p_, i, ("ev", p_))
                        else:
                            p_ = [j for j in JOBS if slot[j] == slot[job]][-1]
                            pe.wait_ge(dv_.sem, dv_.before(("ev", p_), i))
                        make(job, i)

                for n, job in enumerate(first):
                    p_ = before(first, n, slot.get)
                    if p_:
                        wait_job(pe, "dve", p_, -1, ("ev", p_))
                    if job == ("H", 0, 0):
                        pe.wait_ge(s_dft, 16)
                    make(job, -1)
                pe.wait_ge(fdv.sem, fdv.now(("ev", first[-1]), 0))
                blocks(pe, body)

            @block.scalar
            def _(a):
                ac_.start(a)
                nxt_["act"].start(a)

                def save(jobs, n, i):
                    job = jobs[n]
                    wait_job(a, "pe", job, i)
                    p_ = before(jobs, n, side.get)
                    if p_:
                        wait_job(a, "dve", p_, i, ("ev", p_))
                    of("act", job, i)[0].did(act(osave[:, side[job], :], pair[slot[job]][:, 1, :], ACT.Copy), job)

                def body(i, jobs):
                    ac_.n = nxt_["act"].n = 0
                    jobs = [j for j in jobs if j in SAVED]
                    p_ = [j for j in SAVED if not is_next(j)][-1]
                    a.wait_ge(dv_.sem, dv_.before(("ev", p_), i))
                    a.wait_ge(fdv.sem, fdv.now(("ev", [j for j in SAVED if is_next(j)][-1]), i))
                    for n in range(len(jobs)):
                        save(jobs, n, i)
                saved = [j for j in first if j in SAVED]
                for n in range(len(saved)):
                    save(saved, n, -1)
                blocks(a, body)

            @block.vector
            def _(v):
                dv_.start(v)
                fdv.start(v)

                def linker(s_, i):
                    def link(ins, label=None):
                        s_.did(ins, label)
                        v.wait_ge(s_.sem, s_.here(i))
                    return link

                def weights(o, i):
                    s_, j = (dv_, i) if o else (fdv, i + 1)
                    if o == 0:
                        v.wait_ge(s_l["w4"], j * 16 + 16)
                        v.wait_ge(pe_.sem, pe_.before(("filt", 1, NT - 1), j))
                    else:
                        v.wait_ge(fpe.sem, fpe.now(("filt", 0, NT - 1), i))
                    s_.did(tt(wsd[:, 0, :], w4[:, o, :], w4[:, 2 + o, :], ADD))
                    s_.did(tt(wsd[:, 1, :], w4[:, o, :], w4[:, 2 + o, :], SUB), ("w", o))

                def take(job, i):
                    kind, o = job[0], job[1]
                    s_, j = of("dve", job, i)
                    link = linker(s_, j)
                    q = pair[slot[job]]
                    wait_job(v, "pe", job, i)
                    if kind == "filt":
                        if job[2] == 0:
                            if o == 0:
                                v.wait_ge(s_l["dec"], j * 16 + 16)
                                v.wait_ge(pe_.sem, pe_.before(("H", 1, 4), j))
                            else:
                                v.wait_ge(fpe.sem, fpe.now(("H", 0, 4), i))
                        dj = dec[:, job[2]:job[2] + 1, :].to_broadcast([P, 2, CB])
                        link(tt(hsd[:, :, job[2], :], q[:, :, :], dj, MUL), ("ev", job))
                    elif kind == "fix":
                        if o == 0:
                            v.wait_ge(s_l["bias"], j * 16 + 16)
                        link(tt(skip_row[:, :], bias[:, o, :], q[0:1, 0, :], SUB), ("ev", job))
                        s_.did(tt(hsd[0:1, 0, 0, :], hsd[0:1, 0, 0, :], skip_row[:, :], ADD))
                        link(tt(hsd[0:1, 0, 4, :], hsd[0:1, 0, 4, :], skip_row[:, :], ADD), ("row0", o))
                    elif kind in ("H", "X"):
                        dst, m = H[o] if kind == "H" else X, job[2]
                        if m < 4:
                            kt, cs = m // 2, m % 2
                            wait_job(v, "act", job, i)
                            half = osave[:, side[job], :]
                            s_.did(tt(dst[:, cs, kt, :], q[:, 0, :], half, ADD))
                            x, y = (q[:, 0, :], half) if cs == 0 else (half, q[:, 0, :])
                            link(tt(dst[:, cs, 2 + kt, :], x, y, SUB), ("ev", job))
                        else:
                            link(nc.vector.tensor_copy(dst[:, :, 4, :], q[:, :, :]), ("ev", job))
                    elif o == 0:
                        m = job[2]
                        if m == 0:
                            v.wait_ge(s_l["x1"], i * 16 + 16)
                        js = slice(2 * m, min(2 * m + 2, NT))
                        link(tt(vx[0][:, js, :], q[:, 0:js.stop - js.start, :], vx[1][:, js, :], MUL), ("ev", job))
                    else:
                        c4 = job[2]
                        if c4 == 0:
                            v.wait_ge(s_l["g"], i * 16 + 16)
                            v.wait_ge(s_f, i + 1)
                        dst = yout[:, c4, 0:LS].rearrange("p (t r) -> p r t", r=2)
                        gg = g[:, c4, 0:LS].rearrange("p (t r) -> p r t", r=2)
                        s_.did(tt(dst, q[:, 0, :].rearrange("p (r t) -> p r t", r=2), gg, MUL))
                        s_.did(tt(yout[:, c4, LS:T], q[:, 1, 0:LP], g[:, c4, LS:T], MUL), ("ev", job))

                def product(o, i):
                    link = linker(dv_, i)
                    for piece in range(3):
                        tiles = slice(piece, piece + 3, 2) if piece < 2 else slice(4, 5)
                        w_ = 2 if piece < 2 else 1
                        Xr, Xs, Hr, Hs = X[:, 0, tiles, :], X[:, 1, tiles, :], H[o][:, 0, tiles, :], H[o][:, 1, tiles, :]
                        out = Y if piece < 2 else Yp
                        Yr, Ys, t_ = out[:, 0, :, :], out[:, 1, :, :], tmp[:, 0:w_, :]
                        v.wait_ge(dv_.sem, dv_.here(i))
                        dv_.did(tt(Yr, Xr, Hr, MUL))
                        yield
                        link(tt(t_, Xs, Hs, MUL))
                        yield
                        link(tt(Yr, Yr, t_, SUB))
                        yield
                        dv_.did(tt(Ys, Xr, Hs, MUL))
                        yield
                        link(tt(t_, Xs, Hr, MUL))
                        yield
                        link(tt(Ys, Ys, t_, ADD), ("comb", o, 2) if piece == 2 else None)
                        yield
                        if piece < 2:
                            for c, op in ((0, ADD), (1, SUB)):
                                dv_.did(tt(X[:, c, piece, :], Y[:, c, 0, :], Y[:, c, 1, :], op))
                                yield
                                last = tt(X[:, c, piece + 2, :], Y[:, c, 0, :], Y[:, c, 1, :], SUB if op == ADD else ADD)
                                dv_.did(last, ("comb", o, piece))
                                yield

                def body(i, jobs):
                    dv_.n = fdv.n = 0
                    weights(1, i)
                    steps = iter(())
                    for job in jobs:
                        if job in (("inv", 0, 0), ("inv", 1, 0)):
                            for _ in steps:
                                pass
                        if job == ("X", 1, 0) and first[0] in jobs:
                            weights(0, i)
                        take(job, i)
                        if job[0] == "X" and job[2] == 1:
                            steps = product(job[1], i)
                        for _ in range({"X": 3, "H": 4}.get(job[0], 0)):
                            next(steps, None)

                weights(0, -1)
                for job in first:
                    take(job, -1)
                blocks(v, body)


def out_proj(nc, A, G, M, l, w_dram, x):
    mm, stt, ts, tt, act = make_ops(nc)
    ps = G["ps"]
    HALF = D // 2
    RING = 6
    with ExitStack() as st:
        sb = lambda n, s: st.enter_context(nc.sbuf_tensor(f"{n}{l}", s, F32))
        y = sb("oy", [P, KE, T])
        w = sb("ow", [P, RING, HALF])
        o = sb("oo", [P, NT, D])
        gate = sb("ogate", [P, 2, D])
        bo = sb("obias", [P, D]) if l == 0 else None
        sq, ss, rs = sb("osq", [P, D]), sb("oss", [P, NT]), sb("ors", [P, NT])
        Y_PARTS = [slice(0, 1), slice(1, 4), slice(4, 8), slice(8, 12), slice(12, KE)]
        s_y = [st.enter_context(nc.semaphore(f"out{l}_y{k}")) for k in range(len(Y_PARTS))]
        s_w = [st.enter_context(nc.semaphore(f"out{l}_w{k}")) for k in range(RING)]
        s_x = st.enter_context(nc.semaphore(f"out{l}_x_loaded"))
        s_o = st.enter_context(nc.semaphore(f"out{l}_stored"))
        pe_, ac_, dv_ = (Steps(nc, st, f"out{l}_{n}", M) for n in ("pe", "act", "dve"))
        n_x = [0]
        with nc.Block() as block:
            @block.sync
            def _(sp):
                y_v = A["y_d"].rearrange("(k p) t -> p k t", p=P)

                def load_y(part):
                    ks = Y_PARTS[part]
                    sp.dma_start(y[:, ks, :], y_v[:, ks, :]).then_inc(s_y[part], 16)

                def load_w(n):
                    h, k = n // KE, n % KE
                    if n >= RING:
                        sp.wait_ge(pe_.sem, pe_.now(("k", n - RING)))
                    sp.dma_start(w[:, n % RING, :], w_dram[0, k * P:(k + 1) * P, h * HALF:(h + 1) * HALF]).then_inc(s_w[n % RING], 16)
                load_w(0)
                load_y(0)
                for n in range(1, RING):
                    load_w(n)
                    if n < len(Y_PARTS):
                        load_y(n)
                n_x[0] = 0
                def xl(dst, src):
                    sp.dma_start(dst, src).then_inc(s_x, 16)
                    n_x[0] += 16
                if l == 0:
                    xl(x[:, 0:4, :], A["x_sample"][0].rearrange("(j p) n -> p j n", p=P))
                    xl(x[:, 4, :], A["x_prompt"][0])
                    xl(bo[:, :], A["hy_b_out"][0:1, :].partition_broadcast(P))
                else:
                    xl(x[:, :, :], A["x1_d"].rearrange("(j p) n -> p j n", p=P))
                for c in range(2):
                    xl(gate[:, c, :], A["gate_d"][l, c:c + 1, :].partition_broadcast(P))
                for n in range(RING, 2 * KE):
                    load_w(n)
                for j in range(NT):
                    sp.wait_ge(dv_.sem, dv_.now(("x", j)))
                    dst = A["x1_d"][j * P:(j + 1) * P, :] if l == 0 else (A["y_sample"][0, j * P:(j + 1) * P, :] if j < 4 else A["y_prompt"][0])
                    sp.dma_start(dst, x[:, j, :]).then_inc(s_o, 16)
                sp.wait_ge(s_o, 16 * NT)

            @block.tensor
            def _(pe):
                for n in range(2 * KE):
                    h, k = n // KE, n % KE
                    if h == 0 and k in [ks.start for ks in Y_PARTS]:
                        pe.wait_ge(s_y[[ks.start for ks in Y_PARTS].index(k)], 16)
                    pe.wait_ge(s_w[n % RING], 16 * (n // RING + 1))
                    if h == 1 and k == 0:
                        pe.wait_ge(dv_.sem, dv_.now(("oj", 0, NT - 1)))
                    for j in range(NT):
                        last = mm(ps[:, j, :], y[:, k, j * P:(j + 1) * P], w[:, n % RING, :], k == 0, k == KE - 1)
                    pe_.did(last, ("k", n))

            @block.vector
            def _(v):
                def link(ins, label=None):
                    dv_.did(ins, label)
                    v.wait_ge(dv_.sem, dv_.here())
                v.wait_ge(s_x, n_x[0])
                for h in range(2):
                    v.wait_ge(pe_.sem, pe_.now(("k", (h + 1) * KE - 1)))
                    hs = slice(h * HALF, (h + 1) * HALF)
                    for j in range(NT):
                        if l == 0:
                            ins = tt(o[:, j, hs], ps[:, j, :], bo[:, hs], ADD)
                        else:
                            ins = nc.vector.tensor_copy(o[:, j, hs], ps[:, j, :])
                        dv_.did(ins, ("oj", h, j))
                v.wait_ge(ac_.sem, ac_.now("ss"))
                dv_.did(ts(ss[:, :], ss[:, :], 1.0 / D, EPS, MUL, ADD), "var")
                v.wait_ge(ac_.sem, ac_.now("std"))
                link(nc.vector.reciprocal(rs[:, :], rs[:, :]))
                for j in range(NT):
                    link(stt(o[:, j, :], o[:, j, :], rs[:, j:j + 1], gate[:, j // 4, :], MUL, MUL))
                    dv_.did(tt(x[:, j, :], x[:, j, :], o[:, j, :], ADD), ("x", j))

            @block.scalar
            def _(a):
                for j in range(NT):
                    a.wait_ge(dv_.sem, dv_.now(("oj", 1, j)))
                    if j:
                        a.wait_ge(ac_.sem, ac_.here())
                    ac_.did(act(sq[:, :], o[:, j, :], ACT.Square, accum_out=ss[:, j:j + 1]), "ss")
                a.wait_ge(dv_.sem, dv_.now("var"))
                ac_.did(act(rs[:, :], ss[:, :], ACT.Sqrt), "std")
def rwkv_in(nc, A, G, M, hT):
    mm, stt, ts, tt, act = make_ops(nc)
    ps, col = G["ps"], G["col"]
    pair = [ps[:, 2 * q:2 * q + 2, :].rearrange("p b n -> p (b n)") for q in range(4)]
    MIX = {"r": 0, "w": 1, "k": 2, "v": 3, "a": 4, "z": 5}
    BIG = ("r", "k", "v", "z")
    SEQ = ("w", "a") + BIG
    U = 4
    with ExitStack() as st:
        sb = lambda n, s: st.enter_context(nc.sbuf_tensor(n, s, F32))
        xx = sb("xx", [P, KD, T])
        mix = [sb(f"mix{b}", [P, KD, T]) for b in range(2)]
        lw = [sb(f"lora_w{b}", [P, KD, 2, HID]) for b in range(2)]
        w = [sb(f"rw{u}", [P, KD, P]) for u in range(U)]
        out = [sb(f"rout{u}", [P, T]) for u in range(U)]
        sig = sb("rsig", [P, T])
        s_lw = st.enter_context(nc.semaphore("rw_lora_loaded"))
        s_w = [st.enter_context(nc.semaphore(f"rw_weights_{u}")) for u in range(U)]
        s_o = [st.enter_context(nc.semaphore(f"rw_stored_{u}")) for u in range(U)]
        s_f = [st.enter_context(nc.semaphore(f"rw_store_buffer_free_{u}")) for u in range(U)]
        mx = Steps(nc, st, "rw_mixes", M)
        lo_pe, lo_ac = Steps(nc, st, "rw_lora_pe", M), Steps(nc, st, "rw_lora_act", M)
        pe_ = {b: Steps(nc, st, f"rw_pe_{b}", M) for b in BIG}
        ac_ = {b: Steps(nc, st, f"rw_act_{b}", M) for b in BIG}
        dv_ = Steps(nc, st, "rw_dve_z", M)
        ROUNDS = KE // U
        mu = col[:, 0, 80:128].rearrange("p (m k) -> p m k", m=6)

        with nc.Block() as block:
            @block.sync
            def _(sp):
                for b, n in enumerate(("rw_w1", "rw_a1")):
                    for z in range(2):
                        sp.dma_start(lw[b][:, :, z, :], A[n][0, z].rearrange("(k p) r -> p k r", p=P)).then_inc(s_lw, 16)
                for bi, b in enumerate(BIG):
                    w_v = A[f"rw_w_{b}"][0].rearrange("(k p) n -> p k n", p=P)
                    if bi:
                        sp.wait_ge(pe_[BIG[bi - 1]].sem, (ROUNDS + 1) * pe_[BIG[bi - 1]].per())
                    with sp.Fori(0, ROUNDS) as i:
                        for u in range(U):
                            sp.wait_ge(pe_[b].sem, pe_[b].before(("proj", u), i))
                            sp.dma_start(w[u][:, :, :], w_v[:, :, bass.ds(i * U * P + u * P, P)]).then_inc(s_w[u], 16)

            @block.vector
            def _(v):
                dv_.start(v)

                def link(ins, label=None):
                    mx.did(ins, label)
                    v.wait_ge(mx.sem, mx.here())
                link(ts(xx[:, :, :], hT[:, :, :], -1.0, None, MUL))
                grid = lambda a, k0: a[:, k0:k0 + 2, 0:LS].rearrange("p k (r c) -> p k r c", c=GRID)
                for k in range(2):
                    for k0, dst, src in ((0, (slice(None), slice(1, GRID)), (slice(None), slice(0, GRID - 1))),
                                         (2, (slice(None), slice(0, GRID - 1)), (slice(None), slice(1, GRID)))):
                        g = lambda a, sl: a[:, k0 + k, 0:LS].rearrange("p (r c) -> p r c", c=GRID)[:, sl[0], sl[1]]
                        mx.did(tt(g(xx, dst), g(xx, dst), g(hT, src), ADD))
                mx.did(tt(xx[:, 4:6, GRID:LS], xx[:, 4:6, GRID:LS], hT[:, 4:6, 0:LS - GRID], ADD))
                mx.did(tt(xx[:, 6:8, 0:LS - GRID], xx[:, 6:8, 0:LS - GRID], hT[:, 6:8, GRID:LS], ADD))
                mx.did(tt(xx[:, 0:4, LS + 1:T], xx[:, 0:4, LS + 1:T], hT[:, 0:4, LS:T - 1], ADD))
                link(tt(xx[:, 4:8, LS:T - 1], xx[:, 4:8, LS:T - 1], hT[:, 4:8, LS + 1:T], ADD))

                def make(n):
                    b = SEQ[n]
                    if n >= 2:
                        p_ = SEQ[n - 2]
                        if p_ in BIG:
                            v.wait_ge(pe_[p_].sem, (ROUNDS + 1) * pe_[p_].per())
                        else:
                            v.wait_ge(lo_pe.sem, lo_pe.now(p_))
                    for k in range(KD):
                        mx.did(stt(mix[n % 2][:, k, :], xx[:, k, :], mu[:, MIX[b], k:k + 1], hT[:, k, :], MUL, ADD), ("mix", b))
                for n in range(len(SEQ)):
                    make(n)
                with v.Fori(0, ROUNDS) as i:
                    for u in range(U):
                        v.wait_ge(ac_["z"].sem, ac_["z"].now(("sig", u), i))
                        v.wait_ge(s_f[u], 3 * ROUNDS + i + 1)
                        dv_.did(tt(out[u][:, :], pair[u][:, 0:T], sig[:, :], MUL), ("z", u))

            @block.tensor
            def _(pe):
                pe.wait_ge(s_lw, 64)
                for n, b in enumerate(SEQ):
                    pe.wait_ge(mx.sem, mx.now(("mix", b)))
                    m = mix[n % 2]
                    if b in ("w", "a"):
                        for k in range(KD):
                            lhsT = lw[n][:, k, :, :].rearrange("p z r -> p (z r)")
                            mm(pair[n][:, 0:LS], lhsT, m[:, k, 0:LS], k == 0, k == KD - 1)
                            last = mm(pair[n][:, LS:T], lhsT, m[:, k, LS:T], k == 0, k == KD - 1)
                        lo_pe.did(last, b)
                        continue
                    bi = BIG.index(b)
                    if bi == 0:
                        pe.wait_ge(lo_ac.sem, lo_ac.now("a"))
                    else:
                        pe.wait_ge(ac_[BIG[bi - 1]].sem, (ROUNDS + 1) * ac_[BIG[bi - 1]].per())
                    pe_[b].start(pe)
                    with pe.Fori(0, ROUNDS) as i:
                        for u in range(U):
                            pe.wait_ge(s_w[u], (bi * ROUNDS + i) * 16 + 16)
                            if b == "z":
                                pe.wait_ge(dv_.sem, dv_.before(("z", u), i))
                            else:
                                pe.wait_ge(ac_[b].sem, ac_[b].before(("out", u), i))
                            for k in range(KD):
                                mm(pair[u][:, 0:LS], w[u][:, k, :], m[:, k, 0:LS], k == 0, k == KD - 1)
                                last = mm(pair[u][:, LS:T], w[u][:, k, :], m[:, k, LS:T], k == 0, k == KD - 1)
                            pe_[b].did(last, ("proj", u))

            @block.scalar
            def _(a):
                for n, (b, f, dst) in enumerate((("w", ACT.Tanh, G["wlo"]), ("a", ACT.Copy, G["alo"]))):
                    a.wait_ge(lo_pe.sem, lo_pe.now(b))
                    lo_ac.did(act(dst[:, :], pair[n][:, 0:T], f), b)
                for bi, b in enumerate(BIG):
                    ac_[b].start(a)
                    with a.Fori(0, ROUNDS) as i:
                        for u in range(U):
                            a.wait_ge(pe_[b].sem, pe_[b].now(("proj", u), i))
                            if b == "z":
                                if u:
                                    a.wait_ge(dv_.sem, dv_.now(("z", u - 1), i))
                                else:
                                    a.wait_ge(dv_.sem, dv_.before(("z", U - 1), i))
                                ac_[b].did(act(sig[:, :], pair[u][:, 0:T], ACT.Sigmoid), ("sig", u))
                            else:
                                a.wait_ge(s_f[u], bi * ROUNDS + i + 1)
                                ac_[b].did(act(out[u][:, :], pair[u][:, 0:T], ACT.Copy), ("out", u))

            @block.gpsimd
            def _(po):
                for u in range(U):
                    po.sem_inc(s_f[u], 1)
                for bi, b in enumerate(BIG):
                    with po.Fori(0, ROUNDS) as i:
                        for u in range(U):
                            if b == "z":
                                po.wait_ge(dv_.sem, dv_.now(("z", u), i))
                            else:
                                po.wait_ge(ac_[b].sem, ac_[b].now(("out", u), i))
                            po.dma_start(A["rkvz_d"][bi, bass.ds(i * U * P + u * P, P), :], out[u][:, :]).then_inc(s_o[u], 16)
                        for u in range(U):
                            po.wait_ge(s_o[u], (bi * ROUNDS + i) * 16 + 16)
                            po.sem_inc(s_f[u], 1)
                for u in range(U):
                    po.wait_ge(s_o[u], 16 * ROUNDS * 4)


def rwkv_scan(nc, A, G, M):
    mm, stt, ts, tt, act = make_ops(nc)
    ps, tab, col = G["ps"], G["tab"], G["col"]
    T_ = lambda n: tab[:, TAB[n][0]:TAB[n][1]]
    ident, heads, chunk = T_("ident"), T_("heads"), T_("chunk")
    between = T_("between").rearrange("p (l n) -> p l n", l=LEVELS)
    chosen = T_("chosen").rearrange("p (l n) -> p l n", l=LEVELS)
    HALVES = (slice(0, 64), slice(64, 128))
    NU = 2 * NC
    GROUPS = [slice(4 * g, 4 * g + 4) for g in range(NU // 4)]
    G4 = [(0, 4), (4, 4), (8, 2)]
    SIDES = [slice(d * NC + c0, d * NC + c0 + n) for d in range(2) for c0, n in G4]
    SIDE_ORDER = (0, 3, 1, 4, 2, 5)
    side_of = lambda u: [u < us.stop for us in SIDES].index(True)
    RING = 6
    JOBS = [("V", g, "act") for g in range(3)]
    JOBS += [(n, g, "act") for n in ("tb", "tk", "ta") for g in range(5)]
    JOBS += [(n, g, "dve") for g in SIDE_ORDER for n in ("Mb", "Mk")]
    JOBS += [("XV", g, "act") for g in range(5)] + [("CT", g, "act") for g in range(3)]
    for lv in range(1, LEVELS):
        JOBS += [((n, lv), g, "dve") for g in range(3) for n in "TY"]
        JOBS += [(("Z", lv), g, "dve") for g in range(3)]
    JOBS += [("TX", g, "act") for g in range(5)] + [("TA", g, "act") for g in range(5)]
    BANK = {(n, g): q % RING for q, (n, g, _) in enumerate(JOBS)}
    OWNER = {(n, g): e for n, g, e in JOBS}
    LORAS = [(1, 0), (1, 1), (0, 0), (0, 1)]
    LORA_AT = [(3, 1), (4, 0), (4, 1), (5, 0)]
    unit = lambda d, c: d * NC + c
    CHAINS = [("s", 0, list(range(CS)), 0), ("s", 1, list(range(CS - 1, -1, -1)), 0),
              ("p", 0, list(range(CS, NC)), 0), ("p", 1, list(range(NC - 1, CS - 1, -1)), 2)]
    UB = {("s", 0): (3, 0), ("s", 1): (3, 1), ("p", 0): (3, 2), ("p", 1): (3, 2)}
    SB = {("s", 0): (4, 0), ("s", 1): (5, 0), ("p", 0): (5, 1), ("p", 1): (5, 1)}
    place = lambda ps, at: ps[:, at[0], at[1] * P:(at[1] + 1) * P]
    O_QUOTA = 3
    has_u = lambda s, m: not (s == "p" and m == 0)
    has_s = lambda s, m: not (s == "s" and m == CS - 1)
    STEPS = [[(s, d, n - at, cs) for s, d, cs, at in CHAINS if 0 <= n - at < len(cs)] for n in range(CS)]

    with ExitStack() as st:
        sb = lambda n, s: st.enter_context(nc.sbuf_tensor(n, s, F32))
        r, k, v, z = (sb(f"e_{n}", [P, T]) for n in "rkvz")
        pcl, gpc = sb("e_pc", [P, 8]), sb("e_gpc", [P, 2])
        omka = sb("e_omka", [P, 1])
        lw2, la2 = sb("e_w2", [P, P]), sb("e_a2", [P, P])
        two = lambda n: [sb(f"e_{n}{d}", [P, T]) for d in range(2)]
        ld, kd = two("ld"), two("kd")
        decays = sb("e_decays", [P, 2, 2, T])
        e3, e1 = ([decays[:, q, d, :] for d in range(2)] for q in range(2))
        e2 = two("e2")
        kk, kr, bon, o = (sb(f"e_{n}", [P, T]) for n in ("kk", "kr", "bon", "o"))
        osq, ostd = e3
        pcd, pcd_next = sb("e_pcd", [P, NU]), sb("e_pcd_next", [P, NU])
        BDar = sb("BDar", [P, NU, 2, P])
        BDb, BDk = sb("BDb", [P, NU, P]), sb("BDk", [P, NU, P])
        M2T, Y = BDk[:, 0:NC, :], BDk[:, NC:NU, :]
        At, Bt, Kt = (sb(f"e_{n}t", [P, NU, P]) for n in "abk")
        V = sb("e_Vt", [P, NC, P])
        QA, AK = sb("QA", [P, NU, 2, P]), sb("AK", [P, NU, 2, P])
        Q, Arb, Aak, Ark = QA[:, :, 0, :], QA[:, :, 1, :], AK[:, :, 0, :], AK[:, :, 1, :]
        BDv, S_at = Q, Aak
        F = Q[:, NC:NU, :]
        M1, CT, TX = sb("M1", [P, NC, P]), sb("CT", [P, NC, P]), sb("TX", [P, NU, P])
        C_ = M1
        TA = At
        Sd = sb("Sd", [P, 4, P])
        S0, Sfin = sb("S0", [P, 2, P]), sb("Sfin", [P, 2, P])
        st0, stn = sb("st0", [P, 2, P]), sb("stn", [P, 2, P])
        names = ("r", "k", "v", "z", "w2", "a2", "st")
        s_l = {n: st.enter_context(nc.semaphore(f"scan_loaded_{n}")) for n in names}
        s_y = st.enter_context(nc.semaphore("scan_y_stored"))
        s_n = st.enter_context(nc.semaphore("scan_state_stored"))
        s_fy = st.enter_context(nc.semaphore("scan_y_buffer_free"))
        s_fn = st.enter_context(nc.semaphore("scan_state_buffer_free"))
        s_z = st.enter_context(nc.semaphore("scan_cleared"))
        kinds = lambda what: {n: Steps(nc, st, f"scan_{what}_{n}", M) for n in ("pe", "act", "dve")}
        main, prep, post = kinds("main"), kinds("prep"), kinds("post")
        wide = ps[:, 6:8, :].rearrange("p b n -> p (b n)")
        half = lambda a, h: a[HALVES[h], :].rearrange("p (c t) -> p c t", t=C)
        def waits(eng):
            return lambda s, label, i: eng.wait_ge(s.sem, s.now(label, i))

        def rounds(eng, body):
            body(0, False, True)
            with eng.Fori(1, KE - 1) as i:
                body(i, True, True)
            body(KE - 1, True, False)

        def begin(*steps):
            for s in steps:
                s.n = 0

        def skip(eng, s, n):
            eng.sem_inc(s.sem, n)
            s.n += n

        with nc.Block() as block:
            @block.sync
            def _(sp):
                sp.wait_ge(s_z, 6)

                def load_keys(j):
                    ch = bass.ds(j * P, P)
                    rows = A["rkvz_d"]
                    sp.wait_ge(prep["dve"].sem, prep["dve"].before("ar", j))
                    sp.dma_start(k[:, :], rows[1, ch, :]).then_inc(s_l["k"], 16)
                    for n, src, dst in (("w2", "rw_w2", lw2), ("a2", "rw_a2", la2)):
                        sp.dma_start(dst[:, :], A[src][0].rearrange("z r e -> (z r) e")[:, ch]).then_inc(s_l[n], 16)

                def load_rest(j, i=None):
                    ch = bass.ds(j * P, P)
                    rows = A["rkvz_d"]
                    if i is not None:
                        sp.wait_ge(post["dve"].sem, post["dve"].now("bonus", i))
                    sp.dma_start(v[:, :], rows[2, ch, :]).then_inc(s_l["v"], 16)
                    sp.dma_start(r[:, :], rows[0, ch, :]).then_inc(s_l["r"], 16)
                    for d, src in enumerate(("state_rwkv_fwd", "state_rwkv_bwd")):
                        state = A[src][0, 0].rearrange("h v k -> (h v) k")
                        for h in range(2):
                            sp.dma_start(st0[HALVES[h], d, HALVES[h]], state[bass.ds(j * P + 64 * h, 64), :]).then_inc(s_l["st"], 16)

                def body(i, has_post, has_prep):
                    if has_prep:
                        load_keys(i + 1)
                    if has_post:
                        sp.wait_ge(post["dve"].sem, post["dve"].now("y", i))
                    sp.dma_start(z[:, :], A["rkvz_d"][3, bass.ds(i * P, P), :]).then_inc(s_l["z"], 16)
                    if has_prep:
                        load_rest(i + 1, i)
                load_keys(0)
                load_rest(0)
                rounds(sp, body)

            @block.gpsimd
            def _(po):
                for a in (BDar[:, :, :, :].rearrange("p c q n -> p (c q n)"), BDb[:, :, :].rearrange("p c n -> p (c n)"),
                          BDk[:, :, :].rearrange("p c n -> p (c n)"), st0[:, :, :].rearrange("p c n -> p (c n)"),
                          QA[:, :, :, :].rearrange("p c q n -> p (c q n)"), AK[:, :, :, :].rearrange("p c q n -> p (c q n)")):
                    nc.gpsimd.memset(a, 0.0).then_inc(s_z, 1)
                po.sem_inc(s_fy, 1)
                po.sem_inc(s_fn, 1)

                def store_y(i):
                    po.wait_ge(post["dve"].sem, post["dve"].now("y", i))
                    po.dma_start(A["y_d"][bass.ds((i - 1) * P, P), :], o[:, :]).then_inc(s_y, 16)
                    po.wait_ge(s_y, i * 16)
                    po.sem_inc(s_fy, 1)

                def body(i, has_post, has_prep):
                    if has_post:
                        store_y(i)
                    po.wait_ge(main["act"].sem, main["act"].now("stn", i))
                    for d, n in enumerate(("new_state_fwd", "new_state_bwd")):
                        rows = A[n][0, 0].rearrange("h v k -> (h v) k")
                        for h in range(2):
                            po.dma_start(rows[bass.ds(i * P + 64 * h, 64), :], stn[HALVES[h], d, HALVES[h]]).then_inc(s_n, 16)
                    po.wait_ge(s_n, i * 64 + 64)
                    po.sem_inc(s_fn, 1)
                rounds(po, body)
                store_y(KE)
                po.wait_ge(s_y, 16 * KE)
                po.wait_ge(s_n, 64 * KE)

            @block.tensor
            def _(pe):
                wait = waits(pe)
                for s in (main, prep, post):
                    s["pe"].start(pe)
                pe.wait_ge(s_z, 6)

                def lora(q, d, j):
                    w_, lo = ((lw2, "wlo"), (la2, "alo"))[q]
                    mm(wide[:, 0:LS], w_[HALVES[d], :], G[lo][HALVES[d], 0:LS])
                    prep["pe"].did(mm(wide[:, LS:T], w_[HALVES[d], :], G[lo][HALVES[d], LS:T]), ("lora", q, d))

                def norms(j):
                    wait(prep["act"], "kk2", j)
                    mm(wide[:, 0:LS], heads, e2[1][:, 0:LS])
                    prep["pe"].did(mm(wide[:, LS:T], heads, e2[1][:, LS:T]), "ss")

                def states(j):
                    wait(prep["act"], "norm", j)
                    pe.wait_ge(s_l["st"], j * 64 + 64)
                    for d in range(2):
                        last = nc.tensor.transpose(ps[:, 6, d * P:(d + 1) * P], st0[:, d, :], ident)
                    prep["pe"].did(last, "S0")

                def head_sum(src, label):
                    mm(wide[:, 0:LS], heads, src[:, 0:LS])
                    post["pe"].did(mm(wide[:, LS:T], heads, src[:, LS:T]), label)

                def body(i, has_post, has_prep):
                    j = i + 1
                    D_ = lambda label: wait(main["dve"], label, i)
                    A_ = lambda label: wait(main["act"], label, i)

                    def last_of(waits):
                        for e in ("dve", "act"):
                            labels = [label for owner, label in waits if owner == e]
                            if labels:
                                wait(main[e], max(labels, key=main[e].mark), i)

                    def job(n, g, units, fill, after=()):
                        after = list(after)
                        q = JOBS.index((n, g, OWNER[n, g]))
                        if q == 0:
                            pe.wait_ge(main["dve"].sem, main["dve"].before("O", i))
                            pe.wait_ge(main["act"].sem, main["act"].before("stn", i))
                        elif q >= RING:
                            pn, pg, owner = JOBS[q - RING]
                            after.append((owner, (pn, pg)))
                        last_of(after)
                        width = P
                        for c, u in enumerate(range(units.start, units.stop)):
                            last = fill(ps[:, BANK[n, g], c * width:(c + 1) * width], u)
                        main["pe"].did(last, (n, g))

                    wait(prep["act"], "BDv", i)
                    for g, (c0, n) in enumerate(G4):
                        job("V", g, slice(c0, c0 + n), lambda out, u: nc.tensor.transpose(out, BDv[:, u, :], ident))
                    for n, src in (("tb", BDb[:, :, :]), ("tk", BDk[:, :, :]), ("ta", BDar[:, :, 0, :])):
                        wait(prep["dve" if n == "tk" else "act"], {"tb": "BDb", "tk": "BDk", "ta": "BDa"}[n], i)
                        for g, us in enumerate(GROUPS):
                            job(n, g, us, lambda out, u, src=src: nc.tensor.transpose(out, src[:, u, :], ident))
                    wait(prep["dve"], "ar", i)
                    both = lambda u: decays[:, :, u // NC, u % NC * C:(u % NC + 1) * C]
                    for g in SIDE_ORDER:
                        us = SIDES[g]
                        job("Mb", g, us, lambda out, u: mm(out, BDb[:, u, :], both(u)))
                        job("Mk", g, us, lambda out, u: mm(out, BDk[:, u, :], both(u)))

                    def scores_v(g):
                        job("XV", g, GROUPS[g], lambda out, u: mm(out, Aak[:, u, :], V[:, u % NC, :]),
                            (("act", ("V", 2)), ("dve", ("Mk", side_of(4 * g))), ("dve", ("Mk", side_of(4 * g + 3)))))

                    for g in range(5):
                        scores_v(g)
                    chunks = [slice(c0, c0 + n) for c0, n in G4]
                    for g, cs in enumerate(chunks):
                        job("CT", g, cs, lambda out, c: nc.tensor.transpose(out, C_[:, c, :], ident), (("dve", ("C", g)),))

                    def fill(lv, part):
                        if (lv, part) == (1, 1):
                            if has_post:
                                wait(prep["act"], "S0", i)
                                head_sum(o, "mean")
                            else:
                                skip(pe, post["pe"], 2)
                        if (lv, part) == (2, 1) and has_post:
                            wait(post["act"], "sq", i)
                            head_sum(osq, "var")
                        if (lv, part) in LORA_AT and has_prep:
                            n = LORA_AT.index((lv, part))
                            if n:
                                wait(prep["act"], ("lora", *LORAS[n - 1]), j)
                            else:
                                if has_post:
                                    wait(post["dve"], "varv", i)
                                else:
                                    wait(prep["act"], "S0", i)
                                pe.wait_ge(s_l["w2"], j * 16 + 16)
                                pe.wait_ge(s_l["a2"], j * 16 + 16)
                            lora(*LORAS[n], j)

                    for lv in range(1, LEVELS):
                        for g, cs in enumerate(chunks):
                            job(("T", lv), g, cs, lambda out, c: nc.tensor.transpose(out, F[:, c, :], ident),
                                (("dve", "F0" if lv == 1 else (("Z", lv - 1), g)),))
                            job(("Y", lv), g, cs, lambda out, c: mm(out, CT[:, c, :], M1[:, c, :]),
                                (("dve", ("M1", lv, g)), ("act", ("CT", g))))
                        fill(lv, 0)
                        for g, cs in enumerate(chunks):
                            job(("Z", lv), g, cs, lambda out, c: mm(out, M2T[:, c, :], Y[:, c, :]),
                                (("dve", (("T", lv), g)), ("dve", (("Y", lv), g))))
                        fill(lv, 1)
                    for g, us in enumerate(GROUPS):
                        job("TX", g, us, lambda out, u: mm(out, Q[:, u, :], TX[:, u, :]), (("dve", ("Q", g)), ("act", ("XV", g))))
                    if has_prep:
                        wait(prep["act"], ("lora", *LORAS[-1]), j)
                    wait(post["dve"], "bonus_in", i)
                    head_sum(bon, "bonus")
                    for g, us in enumerate(GROUPS):
                        job("TA", g, us, lambda out, u: mm(out, At[:, u, :], Q[:, u, :]))
                    if has_prep:
                        wait(post["dve"], "bonus", i)
                        norms(j)
                    A_(("TA", 4))
                    terms = []
                    for n, chains in enumerate(STEPS):
                        for s, d, m, cs in chains:
                            c, u = cs[m], unit(d, cs[m])
                            terms.append((0, c, V[:, c, :], Ark[:, u, :]))
                            terms.append((0 if m == 0 and s == "p" else 2 * n + 1, c, TX[:, u, :], Arb[:, u, :]))
                            if m:
                                terms.append((2 * n, c, S_at[:, u, :], BDar[:, u, 1, :]))
                            elif s == "s":
                                terms.append((0, c, S0[:, d, :], BDar[:, u, 1, :]))
                    terms.sort(key=lambda x: x[0])
                    opened, left = set(), [x[1] // 4 for x in terms]

                    def o_terms(now, most):
                        while terms and terms[0][0] <= now and most:
                            _, c, a, b = terms.pop(0)
                            left.pop(0)
                            bank = c // 4
                            last = mm(ps[:, bank, (c % 4) * P:(c % 4 + 1) * P], a, b, bank not in opened, bank not in left)
                            opened.add(bank)
                            most -= 1
                            if bank not in left:
                                main["pe"].did(last, ("O", bank))

                    wait(prep["act"], "BDr", i)
                    for n, chains in enumerate(STEPS):
                        if n:
                            D_([("S", s, d, m) for s, d, m, cs in STEPS[n - 1] if has_s(s, m)][-1])
                        for s, d, m, cs in chains:
                            if has_u(s, m):
                                state = S0[:, d, :] if m == 0 else S_at[:, unit(d, cs[m]), :]
                                main["pe"].did(mm(place(ps, UB[s, d]), TA[:, unit(d, cs[m]), :], state), ("U", s, d, m))
                        new = [(s, d, m, cs) for s, d, m, cs in chains if has_s(s, m)]
                        banks = [SB[s, d][0] for s, d, _, _ in new]
                        for q, (s, d, m, cs) in enumerate(new):
                            mm(place(ps, SB[s, d]), Kt[:, unit(d, cs[m]), :], V[:, cs[m], :], banks[q] not in banks[:q], False)
                        o_terms(2 * n, O_QUOTA)
                        for q, (s, d, m, cs) in enumerate(new):
                            if has_u(s, m):
                                D_(("U", s, d, m))
                            last = mm(place(ps, SB[s, d]), Bt[:, unit(d, cs[m]), :], TX[:, unit(d, cs[m]), :], False, banks[q] not in banks[q + 1:])
                            main["pe"].did(last, ("S", s, d, m))
                        if n == CS - 1:
                            last_of((("dve", ("U", "s", 1, CS - 1)), ("dve", ("S", "p", 1, 1))))
                        o_terms(2 * n + 1, O_QUOTA)
                    o_terms(2 * CS, len(terms))
                    for d in range(2):
                        last = nc.tensor.transpose(ps[:, 5, d * P:(d + 1) * P], Sfin[:, d, :], ident)
                    main["pe"].did(last, "stn")
                    if has_prep:
                        states(j)

                pe.wait_ge(s_l["w2"], 16)
                pe.wait_ge(s_l["a2"], 16)
                for n, (q, d) in enumerate(LORAS):
                    if n:
                        wait(prep["act"], ("lora", *LORAS[n - 1]), 0)
                    lora(q, d, 0)
                wait(prep["act"], ("lora", *LORAS[-1]), 0)
                norms(0)
                states(0)

                def counted(i, has_post, has_prep):
                    begin(main["pe"], post["pe"], prep["pe"])
                    body(i, has_post, has_prep)
                rounds(pe, counted)
                begin(post["pe"])
                pe.wait_ge(main["dve"].sem, main["dve"].now("O", KE - 1))
                head_sum(o, "mean")
                wait(post["act"], "sq", KE)
                head_sum(osq, "var")

            @block.scalar
            def _(a):
                wait = waits(a)
                for s in (main, prep, post):
                    s["act"].start(a)
                flat = lambda x: x.rearrange("p c n -> p (c n)")

                def sigmoid(q, d, j):
                    wait(prep["pe"], ("lora", q, d), j)
                    wait(prep["dve"], "pcl", j)
                    dst = (ld, kd)[q][d]
                    prep["act"].did(act(dst[:, :], wide[:, 0:T], ACT.Sigmoid, bias=pcl[:, 2 * q + d:2 * q + d + 1]), ("lora", q, d))

                def norm(j):
                    wait(prep["pe"], "ss", j)
                    wait(post["dve"], "bonus_in", j - 1)
                    prep["act"].did(act(kr[:, :], wide[:, 0:T], ACT.Sqrt), "norm")

                def scaled_keys(j):
                    wait(prep["dve"], "pcl", j)
                    a.wait_ge(s_l["k"], j * 16 + 16)
                    prep["act"].did(act(kk[:, :], k[:, :], ACT.Copy, scale=pcl[:, 4:5]), "kx")
                    prep["act"].did(act(e2[1][:, :], k[:, :], ACT.Square, scale=pcl[:, 4:5]), "kk2")

                def exps(j):
                    for d in range(2):
                        wait(prep["dve"], ("c", d), j)
                        prep["act"].did(act(e2[d][:, :], e1[d][:, :], ACT.Exp, scale=DECAY_MAX))
                        prep["act"].did(act(e3[d][:, :], e3[d][:, :], ACT.Exp, scale=-DECAY_MAX))
                        a.wait_ge(prep["act"].sem, prep["act"].here(j))
                        prep["act"].did(act(e1[d][:, :], e1[d][:, :], ACT.Exp, scale=-DECAY_MAX), ("exp", d))

                def values(j):
                    a.wait_ge(s_l["v"], j * 16 + 16)
                    for h in range(2):
                        prep["act"].did(act(BDv[HALVES[h], 0:NC, HALVES[h]], half(v, h), ACT.Copy), "BDv")

                def expand(label, dst, src, after, j):
                    for d in range(2):
                        wait(prep["dve"], (after, d), j)
                        us = slice(d * NC, (d + 1) * NC)
                        for h in range(2):
                            prep["act"].did(act(dst[HALVES[h], us, HALVES[h]], src(d, h), ACT.Copy), label)

                def blocks(j):
                    expand("BDb", BDb, lambda d, h: half(ld[d], h), "b", j)
                    expand("BDa", BDar[:, :, 0, :], lambda d, h: half(e3[d], h), "a", j)

                def blocks_r(j):
                    expand("BDr", BDar[:, :, 1, :], lambda d, h: half(e1[d], h), "r", j)

                def states(j):
                    wait(prep["pe"], "S0", j)
                    prep["act"].did(act(flat(S0[:, :, :]), ps[:, 6, 0:2 * P], ACT.Copy), "S0")

                def body(i, has_post, has_prep):
                    begin(main["act"], post["act"], prep["act"])
                    j = i + 1

                    def take(n, g, dst):
                        wait(main["pe"], (n, g), i)
                        size = dst.shape[1] * P
                        main["act"].did(act(dst, ps[:, BANK[n, g], 0:size].rearrange("p (c n) -> p c n", n=P), ACT.Copy), (n, g))

                    for g, (c0, n) in enumerate(G4):
                        take("V", g, V[:, c0:c0 + n, :])
                    for n, dst in (("tb", Bt), ("tk", Kt), ("ta", At)):
                        for g, us in enumerate(GROUPS):
                            take(n, g, dst[:, us, :])
                    for g in range(5):
                        take("XV", g, TX[:, GROUPS[g], :])
                    for g, (c0, n) in enumerate(G4):
                        take("CT", g, CT[:, c0:c0 + n, :])
                    if has_prep:
                        scaled_keys(j)
                    if not has_post:
                        skip(a, post["act"], 2)
                    for lv in range(1, LEVELS):
                        for part in range(2):
                            if has_post and (lv, part) == (1, 1):
                                wait(post["dve"], "oc", i)
                                post["act"].did(act(osq[:, :], o[:, :], ACT.Square), "sq")
                            if has_post and (lv, part) == (2, 1):
                                wait(post["dve"], "varv", i)
                                post["act"].did(act(ostd[:, :], ostd[:, :], ACT.Sqrt), "gstd")
                            if has_prep and (lv, part) in LORA_AT:
                                sigmoid(*LORAS[LORA_AT.index((lv, part))], j)
                    for g, us in enumerate(GROUPS):
                        take("TX", g, TX[:, us, :])
                    for g, us in enumerate(GROUPS):
                        take("TA", g, TA[:, us, :])
                    if has_prep:
                        norm(j)
                        exps(j)
                        values(j)
                        blocks(j)
                    wait(main["pe"], "stn", i)
                    a.wait_ge(s_fn, i + 1)
                    main["act"].did(act(flat(stn[:, :, :]), ps[:, 5, 0:2 * P], ACT.Copy), "stn")
                    if has_prep:
                        blocks_r(j)
                        states(j)

                scaled_keys(0)
                for q, d in LORAS:
                    sigmoid(q, d, 0)
                wait(prep["pe"], "ss", 0)
                prep["act"].did(act(kr[:, :], wide[:, 0:T], ACT.Sqrt), "norm")
                exps(0)
                values(0)
                blocks(0)
                blocks_r(0)
                states(0)
                rounds(a, body)
                begin(post["act"])
                wait(post["dve"], "oc", KE)
                post["act"].did(act(osq[:, :], o[:, :], ACT.Square), "sq")
                wait(post["dve"], "varv", KE)
                post["act"].did(act(ostd[:, :], ostd[:, :], ACT.Sqrt), "gstd")

            @block.vector
            def _(v_):
                wait = waits(v_)
                for s in (main, prep, post):
                    s["dve"].start(v_)
                w0a0 = col[:, 2, 96:128].rearrange("p (q k) -> p q k", k=KE)
                rest = col[:, 3, :].rearrange("p (q k) -> p q k", k=KE)
                vec = nc.vector
                column = lambda a, j: a[:, :, bass.ds(j, 1)].rearrange("p s o -> p (s o)")
                v_.wait_ge(s_z, 6)

                def linker(s, i):
                    def link(ins, label=None):
                        s["dve"].did(ins, label)
                        v_.wait_ge(s["dve"].sem, s["dve"].here(i))
                    return link

                def columns(j):
                    link = linker(prep, j)
                    prep["dve"].did(vec.tensor_copy(pcl[:, 0:2], column(w0a0, j)))
                    link(vec.tensor_copy(pcl[:, 2:8], column(rest[:, 0:6, :], j)), "pcl")
                    prep["dve"].did(ts(omka[:, :], pcl[:, 5:6], -1.0, 1.0, MUL, ADD))

                def sums(j, d):
                    link = linker(prep, j)
                    wait(prep["act"], ("lora", 0, d), j)
                    link(vec.tensor_tensor_scan(e1[d][:, :], chunk, ld[d][:, :], 0.0, MUL, ADD))
                    if d == 0:
                        link(tt(e3[d][:, :], e1[d][:, :], ld[d][:, :], SUB), ("c", d))
                    else:
                        c3 = e1[d][:, :].rearrange("p (c t) -> p c t", t=C)
                        tot = c3[:, :, C - 1:C].to_broadcast([P, NC, C])
                        link(tt(e3[d][:, :].rearrange("p (c t) -> p c t", t=C), tot, c3, SUB))
                        link(tt(e1[d][:, :], e3[d][:, :], ld[d][:, :], ADD), ("c", d))

                def keys(j):
                    wait(prep["act"], "norm", j)
                    link = linker(prep, j)
                    link(ts(kr[:, :], kr[:, :], 1e-12, None, ALU.max))
                    for q in range(4):
                        cols = slice(q * T // 4, (q + 1) * T // 4)
                        prep["dve"].did(vec.reciprocal(kr[:, cols], kr[:, cols]))
                        yield
                    v_.wait_ge(prep["dve"].sem, prep["dve"].here(j))
                    link(tt(kk[:, :], kk[:, :], kr[:, :], MUL), "kk")
                    yield

                def key_steps(j):
                    yield from keys(j)
                    for d in range(2):
                        yield from key_dir(j, d)
                        yield from tilde_bk(j, d)
                    yield from tilde_ar(j)

                def key_dir(j, d):
                    link = linker(prep, j)
                    wait(prep["act"], ("lora", 1, d), j)
                    link(tt(ld[d][:, :], kk[:, :], kd[d][:, :], MUL))
                    yield
                    link(ts(kd[d][:, :], kd[d][:, :], pcl[:, 5:6], omka[:, :], MUL, ADD))
                    v_.wait_ge(s_l["k"], j * 16 + 16)
                    link(tt(kd[d][:, :], kd[d][:, :], k[:, :], MUL), "kd")
                    yield
                    if d == 0:
                        link(ts(kr[:, :], kd[d][:, :], pcl[:, 6:7], None, MUL))
                    else:
                        link(stt(kr[:, :], kd[d][:, :], pcl[:, 7:8], kr[:, :], MUL, ADD))
                    yield

                def tilde_bk(j, d):
                    wait(prep["act"], ("exp", d), j)
                    end = e1[d][:, :].rearrange("p (c t) -> p c t", t=C)[:, :, (C - 1 if d == 0 else 0)]
                    prep["dve"].did(vec.tensor_copy(pcd_next[:, d * NC:(d + 1) * NC], end), "end")
                    prep["dve"].did(tt(ld[d][:, :], ld[d][:, :], e2[d][:, :], MUL), ("b", d))
                    yield
                    for h in range(2):
                        prep["dve"].did(tt(BDk[HALVES[h], d * NC:(d + 1) * NC, HALVES[h]], half(kd[d], h), half(e2[d], h), MUL), "BDk")
                        yield

                def ends(j):
                    wait(prep["dve"], "end", j)
                    linker(prep, j)(vec.tensor_copy(pcd[:, :], pcd_next[:, :]))

                def tilde_ar(j):
                    v_.wait_ge(s_l["r"], j * 16 + 16)
                    for d in range(2):
                        prep["dve"].did(stt(e3[d][:, :], kk[:, :], -1.0, e3[d][:, :], MUL, MUL), ("a", d))
                        yield
                    wait(prep["dve"], "end", j)
                    for d in range(2):
                        prep["dve"].did(tt(e1[d][:, :], r[:, :], e1[d][:, :], MUL), ("r", d))
                        yield
                    prep["dve"].note("ar")

                def norm_mean(i):
                    link = linker(post, i)
                    wait(post["pe"], "mean", i)
                    post["dve"].did(vec.tensor_copy(gpc[:, :], column(rest[:, 6:8, :], i - 1)))
                    link(stt(o[:, :], wide[:, 0:T], -1.0 / 64, o[:, :], MUL, ADD), "oc")

                def norm_var(i):
                    wait(post["pe"], "var", i)
                    post["dve"].did(ts(ostd[:, :], wide[:, 0:T], 1.0 / 64, GN_EPS, MUL, ADD), "varv")

                def norm_rstd(i, part):
                    wait(post["act"], "gstd", i)
                    cols = slice(part * T // 2, (part + 1) * T // 2)
                    post["dve"].did(vec.reciprocal(ostd[:, cols], ostd[:, cols]))

                def norm_scale(i):
                    link = linker(post, i)
                    v_.wait_ge(post["dve"].sem, post["dve"].here(i))
                    link(tt(o[:, :], o[:, :], ostd[:, :], MUL))
                    link(ts(o[:, :], o[:, :], gpc[:, 0:1], gpc[:, 1:2], MUL, ADD))

                def norm_out(i):
                    linker(post, i)(tt(o[:, :], o[:, :], bon[:, :], ADD))
                    v_.wait_ge(s_l["z"], i * 16)
                    post["dve"].did(tt(o[:, :], o[:, :], z[:, :], MUL), "y")

                def post_steps(lv, part, i):
                    for at, step in {(1, 1): norm_mean, (2, 1): norm_var, (3, 0): lambda i: norm_rstd(i, 0),
                                     (3, 1): lambda i: norm_rstd(i, 1), (4, 0): norm_scale}.items():
                        if at == (lv, part):
                            step(i)

                def body(i, has_post, has_prep):
                    begin(main["dve"], post["dve"], prep["dve"])
                    j = i + 1
                    md = main["dve"]
                    link = linker(main, i)

                    def wide_mask(m, n):
                        return m.rearrange("p (o n) -> p o n", o=1).to_broadcast([P, n, m.shape[1]])

                    def take_scores(n, g, us):
                        wait(main["pe"], (n, g), i)
                        cnt = us.stop - us.start
                        mask = T_(("mk_f", "mk_b")[us.start // NC]).rearrange("p (q n) -> p q n", q=2)
                        for h in range(2):
                            hh = HALVES[h]
                            src = ps[hh, BANK[n, g], 0:cnt * P].rearrange("p (c q t) -> p c q t", c=cnt, q=2)
                            m = mask[hh, :, hh].rearrange("p (o q) t -> p o q t", o=1).to_broadcast([C, cnt, 2, C])
                            md.did(tt({"Mb": QA, "Mk": AK}[n][hh, us, :, hh], src, m, MUL), (n, g))

                    def product(n, g):
                        wait(main["pe"], (n, g), i)
                        c0, cnt = G4[g]
                        return slice(c0, c0 + cnt), ps[:, BANK[n, g], 0:cnt * P].rearrange("p (c n) -> p c n", c=cnt)

                    def choose(lv, g):
                        cs = slice(G4[g][0], G4[g][0] + G4[g][1])
                        md.did(tt(M1[:, cs, :], F[:, cs, :], wide_mask(chosen[:, lv, :], G4[g][1]), MUL), ("M1", lv, g))

                    for g in SIDE_ORDER:
                        take_scores("Mb", g, SIDES[g])
                        take_scores("Mk", g, SIDES[g])
                    v_.wait_ge(md.sem, md.here(i))
                    groups = [slice(c0, c0 + n) for c0, n in G4]
                    for g, cs in enumerate(groups):
                        md.did(tt(C_[:, cs, :], Q[:, cs, :], F[:, cs, :], ADD), ("C", g))
                    for g, cs in enumerate(groups):
                        v_.wait_ge(md.sem, md.now(("C", g), i))
                        md.did(tt(F[:, cs, :], C_[:, cs, :], wide_mask(between[:, 0, :], cs.stop - cs.start), MUL), ("F", g))
                    for g, cs in enumerate(groups):
                        v_.wait_ge(md.sem, md.now(("F", g), i))
                        md.did(tt(F[:, cs, :], F[:, cs, :], wide_mask(ident, cs.stop - cs.start), ADD), "F0")
                    v_.wait_ge(md.sem, md.here(i))
                    wait(main["pe"], ("CT", 2), i)
                    for g in range(3):
                        choose(1, g)
                    if has_prep:
                        columns(j)
                    for lv in range(1, LEVELS):
                        for g in range(3):
                            cs, src = product(("T", lv), g)
                            md.did(tt(M2T[:, cs, :], src, wide_mask(chosen[:, lv, :], src.shape[1]), MUL), (("T", lv), g))
                            cs, src = product(("Y", lv), g)
                            md.did(tt(Y[:, cs, :], src, wide_mask(between[:, lv, :], src.shape[1]), MUL), (("Y", lv), g))
                        if has_post:
                            post_steps(lv, 0, i)
                        for g in range(3):
                            cs, src = product(("Z", lv), g)
                            md.did(tt(F[:, cs, :], F[:, cs, :], src, ADD), (("Z", lv), g))
                            if lv < LEVELS - 1 and g:
                                v_.wait_ge(md.sem, md.now((("Z", lv), g - 1), i))
                                choose(lv + 1, g - 1)
                        v_.wait_ge(md.sem, md.here(i))
                        if lv < LEVELS - 1:
                            choose(lv + 1, 2)
                        if has_post:
                            post_steps(lv, 1, i)
                    for d in range(2):
                        for g, (c0, cnt) in enumerate(G4):
                            us = slice(d * NC + c0, d * NC + c0 + cnt)
                            md.did(tt(Q[:, us, :], F[:, c0:c0 + cnt, :], wide_mask(T_(("mk_f", "mk_b")[d])[:, P:2 * P], cnt), MUL),
                                   ("Q", us.stop // 4 - 1))
                    if has_post:
                        norm_out(i)
                    else:
                        skip(v_, post["dve"], POST_STEPS)
                    post["dve"].did(tt(bon[:, :], kr[:, :], r[:, :], MUL), "bonus_in")
                    if has_prep:
                        sums(j, 0)
                        sums(j, 1)
                    wait(post["pe"], "bonus", i)
                    linker(post, i)(tt(bon[:, :], wide[:, 0:T], v[:, :], MUL), "bonus")
                    later = key_steps(j) if has_prep else iter(())
                    wait(main["act"], ("TX", 4), i)
                    for n, chains in enumerate(STEPS):
                        slot = {(s, d): q for q, (s, d, m, cs) in enumerate(chains)}
                        for s, d, m, cs in chains:
                            u = unit(d, cs[m])
                            if (m == 0 and s == "p") or (s == "s" and m == CS - 1):
                                continue
                            if m == 0:
                                wait(prep["act"], "S0", i)
                            state = S0[:, d, :] if m == 0 else S_at[:, u, :]
                            md.did(ts(Sd[:, slot[s, d], :], state, pcd[:, u:u + 1], None, MUL))
                        for s, d, m, cs in chains:
                            u = unit(d, cs[m])
                            if not has_u(s, m):
                                continue
                            wait(main["pe"], [("U", s2, d2, m2) for s2, d2, m2, _ in chains if has_u(s2, m2)][-1], i)
                            md.did(tt(TX[:, u, :], place(ps, UB[s, d]), TX[:, u, :], ADD), ("U", s, d, m))
                        for s, d, m, cs in chains:
                            u = unit(d, cs[m])
                            if s == "s" and m == CS - 1:
                                continue
                            wait(main["pe"], [("S", s2, d2, m2) for s2, d2, m2, _ in chains
                                              if has_s(s2, m2) and SB[s2, d2][0] == SB[s, d][0]][-1], i)
                            nxt = S_at[:, unit(d, cs[m + 1]), :] if m + 1 < len(cs) else Sfin[:, d, :]
                            if m == 0 and s == "p":
                                link(ts(nxt, place(ps, SB[s, d]), pcd[:, u:u + 1], None, MUL), ("S", s, d, m))
                            else:
                                link(stt(nxt, place(ps, SB[s, d]), pcd[:, u:u + 1], Sd[:, slot[s, d], :], MUL, ADD), ("S", s, d, m))
                        for _ in range(2 if n < CS // 2 else 3):
                            next(later, None)
                    for _ in later:
                        pass
                    if has_prep:
                        ends(j)
                    v_.wait_ge(s_fy, i + 1)
                    for g, (c0, n) in enumerate(G4):
                        wait(main["pe"], ("O", g), i)
                        for h in range(2):
                            dst = o[HALVES[h], c0 * C:(c0 + n) * C].rearrange("p (c t) -> p c t", t=C)
                            src = ps[HALVES[h], g, 0:n * P].rearrange("p (c t) -> p c t", c=n)[:, :, HALVES[h]]
                            md.did(vec.tensor_copy(dst, src), "O")

                POST_STEPS = 9
                columns(0)
                sums(0, 0)
                sums(0, 1)
                for _ in key_steps(0):
                    pass
                ends(0)
                rounds(v_, body)
                begin(post["dve"])
                norm_mean(KE)
                norm_var(KE)
                norm_rstd(KE, 0)
                norm_rstd(KE, 1)
                norm_scale(KE)
                norm_out(KE)


def rwkv(nc, A, G, M):
    with ExitStack() as st:
        for n in ("wlo", "alo"):
            G[n] = st.enter_context(nc.sbuf_tensor(n, [P, T], F32))
        with nc.sbuf_tensor("x1", [P, NT, D], F32) as x:
            out_proj(nc, A, G, M, 0, A["hy_w_out"], x)
            with nc.sbuf_tensor("hT1", [P, KD, T], F32) as hT:
                load_norm(nc, A, G, M, 1, hT, x)
                rwkv_in(nc, A, G, M, hT)
        rwkv_scan(nc, A, G, M)


def program(nc, A, M):
    with ExitStack() as st:
        G = {}
        G["ps"] = st.enter_context(nc.psum_tensor("ps", [P, 8, 512], F32))
        for n, s in (("tab", [P, TAB_N]), ("col", [P, 4, P]), ("fcol", [HID, 4]),
                     ("scl", [P, 2, KD, 2]), ("shf", [P, 2, KD, 2])):
            G[n] = st.enter_context(nc.sbuf_tensor(n, s, F32))
        modulation(nc, A, G, M)
        with ExitStack() as s1:
            G["hid"] = s1.enter_context(nc.sbuf_tensor("hid", [HID, T], F32))
            filter_hidden(nc, A, G, M)
            with nc.sbuf_tensor("hT0", [P, KD, T], F32) as hT:
                with nc.sbuf_tensor("x0", [P, NT, D], F32) as x:
                    load_norm(nc, A, G, M, 0, hT, x)
                hyena_in(nc, A, G, M, hT)
            hyena_conv(nc, A, G, M)
        rwkv(nc, A, G, M)
        with nc.sbuf_tensor("x2", [P, NT, D], F32) as x:
            out_proj(nc, A, G, M, 1, A["rw_w_o"], x)


def constants():
    f = np.float32
    tab = np.zeros((P, TAB_N), np.float64)
    put = lambda n, a: tab.__setitem__((slice(0, a.shape[0]), slice(*TAB[n])), a)
    r = np.arange(P)
    row, c = r[:, None], r[None, :]
    same = row // 64 == c // 64
    put("ident", np.eye(P))
    put("heads", same.astype(f))
    for d, less in (("f", row < c), ("b", row > c)):
        put(f"mk_{d}", np.concatenate([same & less, same & (less | (row == c))], 1).astype(f))
    levels = range(LEVELS)
    put("between", np.concatenate([((row >> (l + 1)) == (c >> (l + 1))) & ((row >> l) != (c >> l)) for l in levels], 1).astype(f))
    put("chosen", np.concatenate([((row >> l) == (c >> l)) & np.where((row >> l) % 2 == 1, row <= c, row >= c) for l in levels], 1).astype(f))
    put("chunk", np.tile((np.arange(T) % C != 0).astype(f), (P, 1)))

    def order(L):
        return np.concatenate([np.arange(0, L, 2), np.arange(1, L, 2)]) if L == LS else np.arange(L)

    feats, decay = [], []
    lo, hi = np.log(1e-2) / 1.5, np.log(1e-2) / 0.3
    deltas = np.abs(np.linspace(lo, hi, E))
    for L in (LS, LP):
        pos = order(L).astype(np.float64)[:, None]
        t = pos / (L - 1)
        ang = (2 * np.pi / L) * pos * np.linspace(1e-4, 15, 16)[None, :]
        feats.append(np.concatenate([t, np.cos(ang), -np.sin(ang)], 1).T)
        decay.append(np.exp(-t * deltas))
    dft = np.zeros((P, DFT_N), np.float64)
    k = np.arange(LS // 2)
    i = np.arange(LS // 2)
    fwd, inv = [], []
    for fn in (np.cos, np.sin):
        for par in range(2):
            m = fn(np.pi * (2 * k[None, :] + 1) * (2 * i[:, None] + par) / (2 * LS))
            fwd.append(m.reshape(2, P, 256).transpose(1, 0, 2).reshape(P, 512))
            inv.append((m.T / LS).reshape(2, P, 256).transpose(1, 0, 2).reshape(P, 512))
    dft[:, slice(*DFT["fwd"])] = np.concatenate(fwd, 1)
    dft[:, slice(*DFT["inv"])] = np.concatenate(inv, 1)
    k = np.arange(LP)
    mp = [fn(np.pi * (2 * k[None, :] + 1) * k[:, None] / (2 * LP)) for fn in (np.cos, np.sin)]
    dft[:, slice(*DFT["fwdp"])] = np.concatenate(mp, 1)
    dft[:, slice(*DFT["invp"])] = np.concatenate([m.T / LP for m in mp], 1)
    return {"tab": tab.astype(f), "dft": dft.astype(f), "feats": np.concatenate(feats, 1).astype(f), "decay": np.concatenate(decay, 0).astype(f)}


SCRATCH = {"vx_d": [2, T, E], "g_d": [E, T], "y_d": [E, T], "x1_d": [T, D], "gate_d": [2, 2, D], "rkvz_d": [4, E, T]}
OUTS = {"y_prompt": [1, LP, D], "y_sample": [1, LS, D], "new_state_fwd": [1, 1, 32, 64, 64], "new_state_bwd": [1, 1, 32, 64, 64]}


def build(nc, shapes, marks, debug=()):
    A = {n: nc.dram_tensor(f"in_{n}", list(s), F32, kind="ExternalInput").ap() for n, s in shapes.items()}
    for n, s in SCRATCH.items():
        A[n] = nc.dram_tensor(f"scratch_{n}", s, F32, kind="ExternalOutput" if n in debug else "Internal").ap()
    for n, s in OUTS.items():
        A[n] = nc.dram_tensor(f"out_{n}", s, F32, kind="ExternalOutput").ap()
    program(nc, A, marks)


def kernel(**inputs):
    import concourse.bacc as bacc
    from concourse.bass_utils import run_bass_kernel_spmd

    arrays = {n: np.ascontiguousarray(a) for n, a in inputs.items()}
    arrays.update(constants())
    shapes = {n: a.shape for n, a in arrays.items()}
    marks = {}
    build(bacc.Bacc("TRN2", target_bir_lowering=False, num_devices=1), shapes, marks)
    marks["counted"] = True
    nc = bacc.Bacc("TRN2", target_bir_lowering=False, num_devices=1)
    build(nc, shapes, marks)
    r = run_bass_kernel_spmd(nc, [{f"in_{n}": a for n, a in arrays.items()}], core_ids=[0]).results[0]
    return tuple(r[f"out_{n}"] for n in OUTS)
```
